# Optimizing a Trainium2 kernel written in Bass

```python
import numpy as np
import jax, jax.numpy as jnp
from jax import lax

D_MODEL = 1024
BATCH = 1
SEQ = 512
DEPTH = 1

PLE_DIM = 256
NSA_HEADS = 8
NSA_GROUPS = 2
NSA_HPG = NSA_HEADS // NSA_GROUPS
HEAD_DIM = 64
CMP_LEN = 32
CMP_STRIDE = 16
CMP_HIDDEN = 256
SEL_LEN = 64
SEL_TOP = 16
WINDOW = 512
Q_BLOCK = 128
FORCE_SCORE = 1e4
CONV_CH = 512
CONV_WIDTH = 31
D_FF = 2816
FFN_CONV_WIDTH = 3
EPS = 1e-6
NEG = -1e30

NSA_Q = NSA_HEADS * HEAD_DIM
NSA_KV = 3 * 2 * NSA_GROUPS * HEAD_DIM
NSA_GATE = 3 * NSA_HEADS
CONV_IN = 2 * CONV_CH
MERGE = 2 * D_MODEL
N_IN = NSA_Q + NSA_KV + NSA_GATE + CONV_IN + MERGE
IN_SPLITS = (NSA_Q, NSA_Q + NSA_KV, NSA_Q + NSA_KV + NSA_GATE, NSA_Q + NSA_KV + NSA_GATE + CONV_IN)


def rmsnorm(x, g):
    xf = x.astype(jnp.float32)
    y = xf * lax.rsqrt(jnp.mean(xf * xf, axis=-1, keepdims=True) + EPS)
    return (y * g.astype(jnp.float32)).astype(x.dtype)

def layernorm(x, g, b):
    xf = x.astype(jnp.float32)
    mu = jnp.mean(xf, axis=-1, keepdims=True)
    xc = xf - mu
    y = xc * lax.rsqrt(jnp.mean(xc * xc, axis=-1, keepdims=True) + EPS)
    return (y * g.astype(jnp.float32) + b.astype(jnp.float32)).astype(x.dtype)

def causal_dwconv(x, w, b):
    k = w.shape[0]
    c = x.shape[-1]
    y = lax.conv_general_dilated(x, w[:, None, :].astype(x.dtype), window_strides=(1,),
                                 padding=((k - 1, 0),), dimension_numbers=('NWC', 'WIO', 'NWC'),
                                 feature_group_count=c)
    return y + b

def masked_softmax(logits, mask):
    logits = jnp.where(mask, logits.astype(jnp.float32), NEG)
    return jnp.where(mask, jax.nn.softmax(logits, axis=-1), 0.0)

def compress(kv, pos, w1, w2):
    s = kv.shape[2]
    n_cmp = (s - CMP_LEN) // CMP_STRIDE + 1
    idx = np.arange(n_cmp)[:, None] * CMP_STRIDE + np.arange(CMP_LEN)[None, :]
    blocks = kv[:, :, idx] + pos
    flat = blocks.reshape(blocks.shape[0], blocks.shape[1], n_cmp, CMP_LEN * HEAD_DIM)
    return jax.nn.gelu(flat @ w1) @ w2

def cmp_to_sel_matrix(n_cmp, n_sel):
    c0 = np.arange(n_cmp) * CMP_STRIDE
    j0 = np.arange(n_sel) * SEL_LEN
    lo = np.maximum(c0[:, None], j0[None, :])
    hi = np.minimum(c0[:, None] + CMP_LEN, j0[None, :] + SEL_LEN)
    return (np.maximum(hi - lo, 0) / CMP_LEN).astype(np.float32)

def nsa_attention(q, kc, vc, ks, vs, kw, vw):
    b, g, hg, s, dh = q.shape
    scale = dh ** -0.5
    n_cmp = kc.shape[2]
    n_sel = s // SEL_LEN
    top = min(SEL_TOP, n_sel)
    cmp_end = jnp.arange(n_cmp) * CMP_STRIDE + CMP_LEN - 1
    sel_map = jnp.asarray(cmp_to_sel_matrix(n_cmp, n_sel))
    ks_blk = ks.reshape(b, g, n_sel, SEL_LEN, dh)
    vs_blk = vs.reshape(b, g, n_sel, SEL_LEN, dh)
    kw_pad = jnp.pad(kw, ((0, 0), (0, 0), (WINDOW, 0), (0, 0)))
    vw_pad = jnp.pad(vw, ((0, 0), (0, 0), (WINDOW, 0), (0, 0)))
    bi = jnp.arange(b)[:, None, None, None]
    gi = jnp.arange(g)[None, :, None, None]
    jsel = jnp.arange(n_sel)

    def query_block(qb_idx):
        t0 = qb_idx * Q_BLOCK
        qb = lax.dynamic_slice_in_dim(q, t0, Q_BLOCK, axis=3) * scale
        t = t0 + jnp.arange(Q_BLOCK)
        lc = jnp.einsum('bghqd,bgcd->bghqc', qb, kc)
        pc = masked_softmax(lc, cmp_end[None, :] <= t[:, None])
        o_c = jnp.einsum('bghqc,bgcd->bghqd', pc.astype(vc.dtype), vc)
        imp = jnp.einsum('bghqc,cj->bgqj', pc, sel_map)
        cur = (t // SEL_LEN)[:, None]
        forced = (jsel[None, :] == 0) | (jsel[None, :] == cur) | (jsel[None, :] == cur - 1)
        valid = jsel[None, :] <= cur
        imp = jnp.where(valid, jnp.where(forced, FORCE_SCORE, imp), NEG)
        _, sel_idx = lax.top_k(imp, top)
        kg = ks_blk[bi, gi, sel_idx]
        vg = vs_blk[bi, gi, sel_idx]
        ls = jnp.einsum('bghqd,bgqnkd->bghqnk', qb, kg).reshape(b, g, hg, Q_BLOCK, top * SEL_LEN)
        kpos = sel_idx[..., None] * SEL_LEN + jnp.arange(SEL_LEN)
        ms = (kpos <= t[None, None, :, None, None]).reshape(b, g, 1, Q_BLOCK, top * SEL_LEN)
        ps = masked_softmax(ls, ms).reshape(b, g, hg, Q_BLOCK, top, SEL_LEN)
        o_s = jnp.einsum('bghqnk,bgqnkd->bghqd', ps.astype(vg.dtype), vg)
        kwb = lax.dynamic_slice_in_dim(kw_pad, t0, WINDOW + Q_BLOCK, axis=2)
        vwb = lax.dynamic_slice_in_dim(vw_pad, t0, WINDOW + Q_BLOCK, axis=2)
        spos = t0 - WINDOW + jnp.arange(WINDOW + Q_BLOCK)
        dist = t[:, None] - spos[None, :]
        mw = (dist >= 0) & (dist < WINDOW) & (spos[None, :] >= 0)
        lw = jnp.einsum('bghqd,bgkd->bghqk', qb, kwb)
        pw = masked_softmax(lw, mw)
        o_w = jnp.einsum('bghqk,bgkd->bghqd', pw.astype(vwb.dtype), vwb)
        return (o_c, o_s, o_w)

    o_c, o_s, o_w = lax.map(query_block, jnp.arange(s // Q_BLOCK))

    def unblock(o):
        return jnp.transpose(o, (1, 2, 3, 0, 4, 5)).reshape(b, g, hg, s, dh)

    return (unblock(o_c), unblock(o_s), unblock(o_w))

def first_inputs(seed: int = 0) -> dict:
    key = jax.random.key(seed)
    ks = jax.random.split(key, 32)
    f32 = jnp.float32

    def nrm(k, shape, fan_in):
        return jax.random.normal(k, shape, f32) * (fan_in ** -0.5)

    def gain(k, shape):
        return 1.0 + 0.05 * jax.random.normal(k, shape, f32)

    def small(k, shape):
        return 0.02 * jax.random.normal(k, shape, f32)

    L = DEPTH
    return {
        "x": jax.random.normal(ks[0], (BATCH, SEQ, D_MODEL), f32),
        "p": jax.random.normal(ks[1], (DEPTH, BATCH, SEQ, PLE_DIM), f32),
        "g_mix": gain(ks[2], (L, D_MODEL)),
        "w_in": nrm(ks[3], (L, D_MODEL, N_IN), D_MODEL),
        "cmp_pos_k": small(ks[4], (L, CMP_LEN, HEAD_DIM)),
        "cmp_pos_v": small(ks[5], (L, CMP_LEN, HEAD_DIM)),
        "w_cmp_k1": nrm(ks[6], (L, CMP_LEN * HEAD_DIM, CMP_HIDDEN), CMP_LEN * HEAD_DIM),
        "w_cmp_k2": nrm(ks[7], (L, CMP_HIDDEN, HEAD_DIM), CMP_HIDDEN),
        "w_cmp_v1": nrm(ks[8], (L, CMP_LEN * HEAD_DIM, CMP_HIDDEN), CMP_LEN * HEAD_DIM),
        "w_cmp_v2": nrm(ks[9], (L, CMP_HIDDEN, HEAD_DIM), CMP_HIDDEN),
        "w_o_nsa": nrm(ks[10], (L, NSA_Q, D_MODEL), NSA_Q),
        "conv_w": nrm(ks[11], (L, CONV_WIDTH, CONV_CH), CONV_WIDTH),
        "conv_b": small(ks[12], (L, CONV_CH)),
        "conv_ln_g": gain(ks[13], (L, CONV_CH)),
        "conv_ln_b": small(ks[14], (L, CONV_CH)),
        "w_conv_out": nrm(ks[15], (L, CONV_CH, D_MODEL), CONV_CH),
        "b_conv_out": small(ks[16], (L, D_MODEL)),
        "w_out": nrm(ks[17], (L, D_MODEL, D_MODEL), D_MODEL),
        "g_ffn": gain(ks[18], (L, D_MODEL)),
        "w_up": nrm(ks[19], (L, D_MODEL, 2 * D_FF), D_MODEL),
        "ffn_conv_w": nrm(ks[20], (L, FFN_CONV_WIDTH, 2 * D_FF), FFN_CONV_WIDTH),
        "ffn_conv_b": small(ks[21], (L, 2 * D_FF)),
        "w_down": nrm(ks[22], (L, D_FF, D_MODEL), D_FF),
        "g_ple": gain(ks[23], (L, D_MODEL)),
        "w_ple_gate": nrm(ks[24], (L, D_MODEL, D_MODEL), D_MODEL),
        "w_ple": nrm(ks[25], (L, PLE_DIM, D_MODEL), PLE_DIM),
        "g_final": gain(ks[26], (D_MODEL,)),
    }

def first_block(x, p, g_mix, w_in, cmp_pos_k, cmp_pos_v, w_cmp_k1, w_cmp_k2, w_cmp_v1, w_cmp_v2,
              w_o_nsa, conv_w, conv_b, conv_ln_g, conv_ln_b, w_conv_out, b_conv_out, w_out,
              g_ffn, w_up, ffn_conv_w, ffn_conv_b, w_down, g_ple, w_ple_gate, w_ple, g_final):
    b, s, _ = x.shape
    h = x
    for i in range(DEPTH):
        u = rmsnorm(h, g_mix[i])
        z = u @ w_in[i]
        zq, zkv, zg, zc, zm = jnp.split(z, IN_SPLITS, axis=-1)

        q = jnp.transpose(zq.reshape(b, s, NSA_GROUPS, NSA_HPG, HEAD_DIM), (0, 2, 3, 1, 4))
        kv = jnp.transpose(zkv.reshape(b, s, 6, NSA_GROUPS, HEAD_DIM), (2, 0, 3, 1, 4))
        kc = compress(kv[0], cmp_pos_k[i], w_cmp_k1[i], w_cmp_k2[i])
        vc = compress(kv[1], cmp_pos_v[i], w_cmp_v1[i], w_cmp_v2[i])
        o_c, o_s, o_w = nsa_attention(q, kc, vc, kv[2], kv[3], kv[4], kv[5])
        gates = jnp.transpose(jax.nn.sigmoid(zg.reshape(b, s, 3, NSA_GROUPS, NSA_HPG)),
                              (2, 0, 3, 4, 1))[..., None]
        o = gates[0] * o_c + gates[1] * o_s + gates[2] * o_w
        o = jnp.transpose(o, (0, 3, 1, 2, 4)).reshape(b, s, NSA_Q)
        y_a = o @ w_o_nsa[i]

        c_val, c_gate = jnp.split(zc, 2, axis=-1)
        c = c_val * jax.nn.sigmoid(c_gate)
        c = causal_dwconv(c, conv_w[i], conv_b[i])
        c = jax.nn.silu(layernorm(c, conv_ln_g[i], conv_ln_b[i]))
        y_b = c @ w_conv_out[i] + b_conv_out[i]

        ga, gb = jnp.split(jax.nn.sigmoid(zm), 2, axis=-1)
        h = h + (ga * y_a + gb * y_b) @ w_out[i]

        v = rmsnorm(h, g_ffn[i]) @ w_up[i]
        v = causal_dwconv(v, ffn_conv_w[i], ffn_conv_b[i])
        v_gate, v_val = jnp.split(v, 2, axis=-1)
        h = h + (jax.nn.gelu(v_gate) * v_val) @ w_down[i]

        gate = jax.nn.sigmoid(rmsnorm(h, g_ple[i]) @ w_ple_gate[i])
        h = h + gate * (p[i] @ w_ple[i])
    return rmsnorm(h, g_final)


DEPTH_2 = 2

N_MIXERS = 2
N_HEADS = 16
HEAD_DIM_2 = D_MODEL // N_HEADS
CONV_WIDTH_2 = 3
D_FF_2 = 4 * D_MODEL
N_ATTN = (DEPTH_2 + 1) // 2
N_CONV = DEPTH_2 // 2
RMS_EPS = 1e-6
NEG_INF = -1e30


def rmsnorm_2(x, g):
    xf = x.astype(jnp.float32)
    y = xf * lax.rsqrt(jnp.mean(xf * xf, axis=-1, keepdims=True) + RMS_EPS)
    return (y * g.astype(jnp.float32)).astype(x.dtype)

def fox_attention(h, w_in, b_f, w_out):
    B, S, D = h.shape
    proj = h @ w_in
    q = proj[..., :D].reshape(B, S, N_HEADS, HEAD_DIM_2).transpose(0, 2, 1, 3)
    k = proj[..., D:2 * D].reshape(B, S, N_HEADS, HEAD_DIM_2).transpose(0, 2, 1, 3)
    v = proj[..., 2 * D:3 * D].reshape(B, S, N_HEADS, HEAD_DIM_2).transpose(0, 2, 1, 3)
    q = q * jnp.asarray(HEAD_DIM_2 ** -0.5, q.dtype)
    f_logit = (proj[..., 3 * D:] + b_f).astype(jnp.float32)
    log_f = jax.nn.log_sigmoid(f_logit)
    c = lax.cumsum(log_f, axis=1).transpose(0, 2, 1)
    k_pos = jnp.arange(S)

    def q_block(i):
        start = i * Q_BLOCK
        qb = lax.dynamic_slice_in_dim(q, start, Q_BLOCK, axis=2)
        cb = lax.dynamic_slice_in_dim(c, start, Q_BLOCK, axis=2)
        s = jnp.einsum('bhqd,bhkd->bhqk', qb, k, preferred_element_type=jnp.float32)
        s = s + cb[..., :, None] - c[..., None, :]
        q_pos = start + jnp.arange(Q_BLOCK)
        s = jnp.where(k_pos[None, :] <= q_pos[:, None], s, NEG_INF)
        pr = jax.nn.softmax(s, axis=-1)
        return jnp.einsum('bhqk,bhkd->bhqd', pr.astype(v.dtype), v)

    o = lax.map(q_block, jnp.arange(S // Q_BLOCK))
    o = o.transpose(1, 0, 3, 2, 4).reshape(B, S, D)
    return o @ w_out

def short_conv(h, w_in, conv_w, w_out):
    D = h.shape[-1]
    proj = h @ w_in
    b_gate = proj[..., :D]
    c_gate = proj[..., D:2 * D]
    u = proj[..., 2 * D:]
    z = c_gate * u
    zc = lax.conv_general_dilated(
        z, conv_w[:, None, :].astype(z.dtype), window_strides=(1,),
        padding=[(CONV_WIDTH_2 - 1, 0)],
        dimension_numbers=('NWC', 'WIO', 'NWC'),
        feature_group_count=D)
    return (b_gate * zc) @ w_out

def sq_relu_mlp(h, w_up, w_down):
    return jnp.square(jax.nn.relu(h @ w_up)) @ w_down

def second_inputs(seed: int = 0) -> dict:
    key = jax.random.key(seed)
    ks = jax.random.split(key, 14)
    f32 = jnp.float32
    nrm = lambda k, shape, scale: jax.random.normal(k, shape, f32) * scale
    x = jax.random.normal(ks[0], (BATCH, SEQ, D_MODEL), f32)
    p = jax.random.normal(ks[1], (DEPTH_2, BATCH, SEQ, PLE_DIM), f32)
    norm_g = 1.0 + nrm(ks[2], (DEPTH_2, 6, D_MODEL), 0.05)
    w_attn_in = nrm(ks[3], (N_ATTN, D_MODEL, 3 * D_MODEL + N_HEADS), D_MODEL ** -0.5)
    b_forget = 2.0 + nrm(ks[4], (N_ATTN, N_HEADS), 0.5)
    w_attn_out = nrm(ks[5], (N_ATTN, D_MODEL, D_MODEL), D_MODEL ** -0.5)
    w_conv_in = nrm(ks[6], (N_CONV, D_MODEL, 3 * D_MODEL), D_MODEL ** -0.5)
    conv_w = nrm(ks[7], (N_CONV, CONV_WIDTH_2, D_MODEL), CONV_WIDTH_2 ** -0.5)
    w_conv_out = nrm(ks[8], (N_CONV, D_MODEL, D_MODEL), D_MODEL ** -0.5)
    w_mlp_up = nrm(ks[9], (DEPTH_2, D_MODEL, D_FF_2), D_MODEL ** -0.5)
    w_mlp_down = nrm(ks[10], (DEPTH_2, D_FF_2, D_MODEL), D_FF_2 ** -0.5)
    w_ple_proj = nrm(ks[11], (DEPTH_2, PLE_DIM, D_MODEL), PLE_DIM ** -0.5)
    w_ple_gate = nrm(ks[12], (DEPTH_2, D_MODEL, D_MODEL), D_MODEL ** -0.5)
    return {"x": x, "p": p, "norm_g": norm_g, "w_attn_in": w_attn_in,
            "b_forget": b_forget, "w_attn_out": w_attn_out, "w_conv_in": w_conv_in,
            "conv_w": conv_w, "w_conv_out": w_conv_out, "w_mlp_up": w_mlp_up,
            "w_mlp_down": w_mlp_down, "w_ple_proj": w_ple_proj, "w_ple_gate": w_ple_gate}

def second_block(x, p, norm_g, w_attn_in, b_forget, w_attn_out, w_conv_in, conv_w,
              w_conv_out, w_mlp_up, w_mlp_down, w_ple_proj, w_ple_gate):
    for i in range(DEPTH_2):
        g = norm_g[i]
        hn = rmsnorm_2(x, g[0])
        j = i // N_MIXERS
        if i % N_MIXERS == 0:
            m = fox_attention(hn, w_attn_in[j], b_forget[j], w_attn_out[j])
        else:
            m = short_conv(hn, w_conv_in[j], conv_w[j], w_conv_out[j])
        x = x + rmsnorm_2(m, g[1])
        f = sq_relu_mlp(rmsnorm_2(x, g[2]), w_mlp_up[i], w_mlp_down[i])
        x = x + rmsnorm_2(f, g[3])
        gate = jax.nn.sigmoid(rmsnorm_2(x, g[4]) @ w_ple_gate[i])
        e = (p[i] @ w_ple_proj[i]) * gate
        x = x + rmsnorm_2(e, g[5])
    return x


def setup_inputs(seed=0):
    out = dict(first_inputs(seed))
    for name, value in second_inputs(seed + 1).items():
        if name != "x":
            out[name + "_2"] = value
    return out


def reference(
    x, p, g_mix, w_in, cmp_pos_k, cmp_pos_v, w_cmp_k1, w_cmp_k2, w_cmp_v1, w_cmp_v2, w_o_nsa,
    conv_w, conv_b, conv_ln_g, conv_ln_b, w_conv_out, b_conv_out, w_out, g_ffn, w_up,
    ffn_conv_w, ffn_conv_b, w_down, g_ple, w_ple_gate, w_ple, g_final, p_2, norm_g_2,
    w_attn_in_2, b_forget_2, w_attn_out_2, w_conv_in_2, conv_w_2, w_conv_out_2, w_mlp_up_2,
    w_mlp_down_2, w_ple_proj_2, w_ple_gate_2,
):
    x = first_block(
        x, p, g_mix, w_in, cmp_pos_k, cmp_pos_v, w_cmp_k1, w_cmp_k2, w_cmp_v1, w_cmp_v2,
        w_o_nsa, conv_w, conv_b, conv_ln_g, conv_ln_b, w_conv_out, b_conv_out, w_out, g_ffn,
        w_up, ffn_conv_w, ffn_conv_b, w_down, g_ple, w_ple_gate, w_ple, g_final,
    )
    return second_block(
        x, p_2, norm_g_2, w_attn_in_2, b_forget_2, w_attn_out_2, w_conv_in_2, conv_w_2,
        w_conv_out_2, w_mlp_up_2, w_mlp_down_2, w_ple_proj_2, w_ple_gate_2,
    )


_drawn_inputs = setup_inputs


def setup_inputs(seed=0):
    import zlib

    import numpy as np

    out = dict(_drawn_inputs(seed))
    spreads = {}
    factors = {'cmp_pos_k': 64.0,
     'cmp_pos_v': 8.0,
     'conv_b': 2.876,
     'conv_ln_b': 5.488,
     'b_conv_out': 3.117,
     'ffn_conv_b': 2.696,
     'g_ple': 5.619}
    for name, (base, spread) in spreads.items():
        noise = np.random.default_rng([zlib.crc32(name.encode()), seed]).standard_normal(out[name].shape)
        drawn = base * np.exp(spread * noise) if base else spread * noise
        out[name] = __import__('jax').numpy.asarray(drawn.astype(out[name].dtype))
    for name, factor in factors.items():
        out[name] = (out[name] * factor).astype(out[name].dtype)
    return out
```

```python
from contextlib import ExitStack

import numpy as np

import concourse.bass as bass
from concourse import mybir

P = 128
S = 512
D = 1024
DC = D // P
HD = 64
NEG = -1e30
EPS = 1e-6
RAW = 4
UW = 1024
CONV_TAPS = 31
PAD = CONV_TAPS - 1
CT = 4
NC1 = 31
NCP = 32
FF1_PARTS = (8, 8, 6)
FF2_PARTS = (8, 8, 8, 8)
QB = S // P
P_OFF = (0, 128, 384, 768)
CREDIT = 2
F32 = mybir.dt.float32
F32R = mybir.dt.float32r
ALU = mybir.AluOpType
ACT = mybir.ActivationFunctionType
AX = mybir.AxisListType
ds = bass.ds


def layout_units():
    u, at = 0, {}

    def stage(name, n):
        nonlocal u
        at[name] = u
        u += n

    stage("glu", 8)
    stage("cmp_in", 4)
    stage("cmp_hidden", 8)
    stage("cmp_out", 1)
    stage("keys", 2)
    stage("values", 2)
    stage("gates", 1)
    stage("q0", 1)
    stage("pairs", 19)
    stage("mix", 8)
    stage("w_out", 8)
    for kind, p in ffn_order(len(FF1_PARTS)):
        stage(f"ffn_{kind}{p}", 2 * FF1_PARTS[p] if kind == "up" else 8)
    stage("ple0", 10)
    stage("forget", 1)
    stage("fox", 24)
    stage("fox_out", 8)
    for kind, p in ffn_order(len(FF2_PARTS)):
        stage(f"mlp1_{kind}{p}", 8)
    stage("ple1", 10)
    stage("conv3", 24)
    stage("conv3_out", 8)
    for kind, p in ffn_order(len(FF2_PARTS)):
        stage(f"mlp2_{kind}{p}", 8)
    stage("ple2", 10)
    at["end"] = u
    return at


def pair_units(p):
    u0 = layout_units()["pairs"] + 5 * p
    return (u0, u0 + 1, u0 + 3, u0 + 4, u0 + 2) if p < 3 else (u0, u0 + 1, u0 + 2, u0 + 3, None)


def ffn_order(parts):
    order = [("up", 0)]
    for p in range(1, parts):
        order += [("up", p), ("down", p - 1)]
    return order + [("down", parts - 1)]


VEC = {}
_n = 0
for _name, _w in (("g_mix", 8), ("g_ffn", 8), ("g_ple", 8), ("g_final", 8), ("norm2", 96), ("conv_w", CT * CONV_TAPS),
                  ("conv_b", CT), ("ln_g", CT), ("ln_b", CT), ("b_conv_out", 8), ("ffn_w", 3 * 44), ("ffn_b", 44),
                  ("conv3_w", 24), ("b_forget", 1), ("pos_k", 16), ("pos_v", 16)):
    VEC[_name] = _n
    _n += _w
NVEC = _n


def build(nc, x_in, p_in, weights, vectors, out):
    U = layout_units()
    with ExitStack() as ctx:
        def sb(name, shape, dt=F32, scope=ctx):
            return scope.enter_context(nc.sbuf_tensor(name, shape, dt))

        def sem(name):
            return ctx.enter_context(nc.semaphore(name))

        w_raw = sb("w_raw", [P, RAW, UW])
        w_hi = sb("w_hi", [P, 2, UW], F32R)
        w_lo = sb("w_lo", [P, 2, UW], F32R)
        X = sb("resid", [P, DC, S])
        xg_hi = sb("xg_hi", [P, DC, S], F32R)
        xg_lo = sb("xg_lo", [P, DC, S], F32R)
        R = sb("inv_rms", [P, 1, S])
        sq = sb("sq", [P, 2, S])
        sq_sum = sb("sq_sum", [P, 1, S])
        T = sb("tile_a", [P, 2, S])
        T2 = sb("tile_b", [P, 2, S])
        vec = sb("vec", [P, NVEC])
        ident = sb("ident", [P, P])
        ident_r = sb("ident_r", [P, P], F32R)
        causal_r = sb("causal_r", [P, P], F32R)
        cmp_mask_r = sb("cmp_mask_r", [P, QB, NCP], F32R)
        valid = sb("valid", [P, QB, 1])
        ones = sb("ones", [P, P])
        ones_r = sb("ones_r", [P, P], F32R)
        mean_col = sb("mean_col", [P, 1])
        mean_ch = sb("mean_ch", [P, P])
        eps_col = sb("eps_col", [P, 1])
        one_col = sb("one_col", [P, 1])
        rms_c = sb("rms_c", [P, 2, QB])
        r_diag = sb("r_diag", [P, QB, P])
        token = sb("token", [P, 14])
        head_sel = sb("head_sel", [P, 16])

        m1 = ExitStack()
        conv_acc = sb("conv_acc", [P, CT, S], scope=m1)
        with ExitStack() as early:
            sb("before_glu", [P, S], scope=early)
            glu = sb("glu", [P, CT, PAD + S], scope=early)
        o_hi = sb("o_hi", [P, 4, S], F32R, m1)
        sb("end_of_glu", [P, S + CT * (PAD + S) - 4 * S], scope=m1)
        o_lo = sb("o_lo", [P, 4, S], F32R, m1)
        with ExitStack() as early:
            cmask = sb("cmask", [P, QB, NCP], scope=early)
            causal = sb("causal", [P, P], scope=early)
            kv_dup = sb("kv_dup", [P, 4, S], scope=early)
            blk = sb("blk", [P, 2, 16, 2 * NC1], scope=early)
            blk_hi = sb("blk_hi", [P, 2, 16, 2 * NC1], F32R, early)
            blk_lo = sb("blk_lo", [P, 2, 16, 2 * NC1], F32R, early)
            hid = sb("hid", [P, 2, 2, 2 * NC1], scope=early)
            hid_hi = sb("hid_hi", [P, 2, 2, 2 * NC1], F32R, early)
            hid_lo = sb("hid_lo", [P, 2, 2, 2 * NC1], F32R, early)
        merge = sb("merge", [P, 16, S], scope=m1)
        with ExitStack() as att:
            kk_hi = sb("kk_hi", [P, 2, S], F32R, att)
            kk_lo = sb("kk_lo", [P, 2, S], F32R, att)
            vv_hi = sb("vv_hi", [P, 2, QB, P], F32R, att)
            vv_lo = sb("vv_lo", [P, 2, QB, P], F32R, att)
            kc_f = sb("kc_f", [P, NCP], scope=att)
            kc_hi = sb("kc_hi", [P, NCP], F32R, att)
            kc_lo = sb("kc_lo", [P, NCP], F32R, att)
            vc_f = sb("vc_f", [NCP, P], scope=att)
            vc_hi = sb("vc_hi", [NCP, P], F32R, att)
            vc_lo = sb("vc_lo", [NCP, P], F32R, att)
            gates = sb("gates", [P, QB, 32], scope=att)
            q_hi = sb("q_hi", [P, 2, S], F32R, att)
            q_lo = sb("q_lo", [P, 2, S], F32R, att)
            prob_c = sb("prob_c", [P, 2, QB, NCP], scope=att)
            c_stat = sb("c_stat", [P, 4, QB], scope=att)
            prob = sb("prob", [P, 2, 1280], scope=att)
            stat = sb("stat", [P, 3, 2, QB], scope=att)
            pt_hi = sb("pt_hi", [P, 2, S], F32R, att)
            pt_lo = sb("pt_lo", [P, 2, S], F32R, att)
        y_hi = sb("y_hi", [P, DC, S], F32R, m1)
        y_lo = sb("y_lo", [P, DC, S], F32R, m1)
        m1.close()

        later = ctx
        M = sb("mixed", [P, DC, S], scope=later)
        with ExitStack() as ff:
            h_hi = sb("h_hi", [P, 2, 8, S], F32R, ff)
            h_lo = sb("h_lo", [P, 2, 8, S], F32R, ff)
            u4 = sb("u4", [P, 4, S], scope=ff)
            p_raw = sb("p_raw", [P, 2, S], scope=ff)
            p_hi = sb("p_hi", [P, 2, S], F32R, ff)
            p_lo = sb("p_lo", [P, 2, S], F32R, ff)
        with ExitStack() as pl:
            E = sb("ple_e", [P, DC, S], scope=pl)
        with ExitStack() as fx:
            fq_hi = sb("fq_hi", [P, 2, S], F32R, fx)
            fq_lo = sb("fq_lo", [P, 2, S], F32R, fx)
            fk_hi = sb("fk_hi", [P, 2, S], F32R, fx)
            fk_lo = sb("fk_lo", [P, 2, S], F32R, fx)
            fv = sb("fv", [P, 1, S], scope=fx)
            fv_hi = sb("fv_hi", [P, 2, QB, P], F32R, fx)
            fv_lo = sb("fv_lo", [P, 2, QB, P], F32R, fx)
            fprob = sb("fprob", [P, 2, 1280], scope=fx)
            fstat = sb("fstat", [P, 3, 2, QB], scope=fx)
            fpt_hi = sb("fpt_hi", [P, 2, S], F32R, fx)
            fpt_lo = sb("fpt_lo", [P, 2, S], F32R, fx)
            with ExitStack() as early:
                logf = sb("logf", [P, 4, S], scope=early)
            fo_hi = sb("fo_hi", [P, DC, S], F32R, fx)
            fo_lo = sb("fo_lo", [P, DC, S], F32R, fx)
            c_rows = sb("c_rows", [P, S], scope=fx)
            c_hi = sb("c_hi", [P, S], F32R, fx)
            c_head = sb("c_head", [P, 2, S], F32R, fx)
        with ExitStack() as c3:
            cy_hi = sb("cy_hi", [P, DC, S], F32R, c3)
            cy_lo = sb("cy_lo", [P, DC, S], F32R, c3)
            c3t = sb("c3t", [P, 5, S], scope=c3)

        ps = ctx.enter_context(nc.psum_tensor("ps", [P, 8, S], F32))

        w_loaded = [sem(f"w_loaded{s}") for s in range(RAW)]
        slot_ready = sem("slot_ready")
        w_hi_ready = sem("w_hi_ready")
        w_ready = sem("w_ready")
        unit_done = sem("unit_done")
        bank_free = sem("bank_free")
        x_loaded, vec_loaded, p_loaded, out_stored = (sem(n) for n in ("x_loaded", "vec_loaded", "p_loaded", "out_stored"))
        c_pool, c_dve, c_act = sem("const_pool"), sem("const_dve"), sem("const_act")
        squared, summed = sem("squared"), sem("summed")
        ssq_done, rms_done, inv_done, diag_done, bcast_done, r_done = (
            sem(f"norm_{n}") for n in ("ssq", "rms", "inverse", "diag", "broadcast", "r"))
        prep_hi, prep_lo = sem("prep_hi"), sem("prep_lo")
        post_t, post_x = sem("post_t"), sem("post_x")
        final_x = sem("final_x")

        def stage_sems(stage, *names):
            return {n: sem(f"{stage}_{n}") for n in names}

        s_glu = stage_sems("glu", "sig", "gated")
        s_cmp = stage_sems("cmp", "dup", "blk", "hi", "lo", "gelu", "ghi", "glo", "out", "khi", "klo")
        s_kv = stage_sems("kv", "hi", "lo", "turned")
        s_gate = stage_sems("gate", "sig", "turned", "ready")
        s_mrg = stage_sems("merge", "sig", "conv")
        s_ln = stage_sems("ln", "sum", "mean", "cent", "sq", "acc", "var", "sd", "inv", "diag", "bc", "r", "n", "act", "hi", "lo")
        s_mix = stage_sems("mix", "a", "y", "hi", "lo")
        att_names = ("scores", "peak", "exps", "inv", "probs", "turned", "hi", "lo", "pv", "ohi", "olo")
        A1 = stage_sems("nsa", *att_names, "qhi", "qlo", "c", "cs")
        A2 = stage_sems("fox", *att_names, "qkhi", "qklo", "vs", "vturned", "vhi", "crow")
        s_fg = stage_sems("forget", "dve", "act")
        s_ffn = stage_sems("ffn", "tap", "conv", "t2", "gelu", "h", "hhi", "hlo")
        s_mlp = stage_sems("mlp", "s", "hi", "lo")
        s_ple = stage_sems("ple", "phi", "plo", "epe", "e", "sig", "g", "x")
        s_c3 = stage_sems("c3", "zz", "z2", "tap", "y", "hi", "lo")

        def vcol(name, i, n=1):
            return vec[:, ds(i + VEC[name], n)]

        def norm2_col(layer, which, i):
            return vec[:, ds(i + (VEC["norm2"] + (layer * 6 + which) * DC), 1)]

        block = ctx.enter_context(nc.Block())

        @block.sync
        def _(sp):
            def load(u, slot):
                sp.dma_start(w_raw[:, slot:slot + 1, :].rearrange("p a n -> p (a n)"),
                             weights[ds(u, 1)].rearrange("a p n -> (a p) n")).then_inc(w_loaded[slot], 16)

            sp.dma_start(X[:, 0:1, :], x_in[:, 0:1, :]).then_inc(x_loaded, 16)
            sp.dma_start(vec[:], vectors).then_inc(vec_loaded, 16)
            load(0, 0)
            sp.dma_start(X[:, 1:DC, :], x_in[:, 1:DC, :]).then_inc(x_loaded, 16)
            for s in range(1, RAW):
                load(s, s)
            groups = U["end"] // RAW
            with sp.Fori(0, groups - 1) as i:
                for s in range(RAW):
                    sp.wait_ge(w_ready, i * RAW + (s + 1))
                    load(i * RAW + (RAW + s), s)
            for u in range(groups * RAW, U["end"]):
                sp.wait_ge(w_ready, u - RAW + 1)
                load(u, u % RAW)
            for m in range(DC):
                sp.wait_ge(post_x, 5 * DC + m + 1)
                sp.dma_start(out[:, m:m + 1, :], X[:, m:m + 1, :]).then_inc(out_stored, 16)
            sp.wait_ge(out_stored, 16 * DC)

        @block.gpsimd
        def _(pool):
            pool.memset(ident[:], 0.0).then_inc(c_pool, 1)
            pool.memset(causal[:], 0.0).then_inc(c_pool, 1)
            pool.memset(cmask[:], 0.0).then_inc(c_pool, 1)
            pool.memset(valid[:], 1.0).then_inc(c_pool, 1)
            pool.memset(head_sel[:], 0.0).then_inc(c_pool, 1)
            pool.wait_ge(c_pool, 5)
            pool.affine_select(out=ident[:], in_=ident[:], compare_op=ALU.not_equal, fill=1.0, base=0,
                               pattern=[[-1, P]], channel_multiplier=1).then_inc(c_pool, 1)
            pool.affine_select(out=causal[:], in_=causal[:], compare_op=ALU.is_ge, fill=NEG, base=0,
                               pattern=[[-1, P]], channel_multiplier=1).then_inc(c_pool, 1)
            pool.affine_select(out=cmask[:], in_=cmask[:], compare_op=ALU.is_ge, fill=NEG, base=-31,
                               pattern=[[P, QB], [-16, NCP]], channel_multiplier=1).then_inc(c_pool, 1)
            pool.affine_select(out=valid[:], in_=valid[:], compare_op=ALU.is_ge, fill=0.0, base=-31,
                               pattern=[[P, QB], [0, 1]], channel_multiplier=1).then_inc(c_pool, 1)
            for n, first in enumerate((0, 32)):
                rows = head_sel[first:first + 32, :]
                pool.wait_ge(c_pool, 9 + n)
                pool.affine_select(out=rows, in_=rows, compare_op=ALU.not_equal, fill=1.0, base=0,
                                   pattern=[[-1, 16]], channel_multiplier=1).then_inc(c_pool, 1)

            pool.wait_ge(c_pool, 11)
            pool.wait_ge(c_dve, 1)

            def split(u, slot):
                raw = w_raw[:, slot, :]
                pool.tensor_tensor(w_hi[:, slot % 2, :].rearrange("p (a b) -> p a b", b=P), raw.rearrange("p (a b) -> p a b", b=P),
                                   ones[:].unsqueeze(1).to_broadcast([P, UW // P, P]), ALU.mult).then_inc(w_hi_ready, 1)
                pool.wait_ge(w_hi_ready, u + 1)
                pool.tensor_tensor(w_lo[:, slot % 2, :], w_raw[:, slot, :], w_hi[:, slot % 2, :].bitcast(F32),
                                   ALU.subtract).then_inc(w_ready, 1)

            for u in range(RAW):
                pool.wait_ge(w_loaded[u], 16)
                if u >= 2:
                    pool.wait_ge(unit_done, u - 1)
                split(u, u)
            groups = U["end"] // RAW
            with pool.Fori(1, groups) as i:
                for s in range(RAW):
                    pool.wait_ge(w_loaded[s], i * 16 + 16)
                    pool.wait_ge(unit_done, i * RAW + (s - 1))
                    split(i * RAW + s, s)
            for u in range(groups * RAW, U["end"]):
                pool.wait_ge(w_loaded[u % RAW], 16 * (u // RAW + 1))
                pool.wait_ge(unit_done, u - 1)
                split(u, u % RAW)

        @block.tensor
        def _(pe):
            def three(o, w, x, wl, xl, start, stop):
                pe.matmul(o, w, x, start=start, stop=False)
                pe.matmul(o, w, xl, start=False, stop=False)
                return pe.matmul(o, wl, x, start=False, stop=stop)

            def wblock(slot, k):
                return w_hi[:, slot, k * P:(k + 1) * P], w_lo[:, slot, k * P:(k + 1) * P]

            def unit(u, slot, xh, xl, n=DC, o=None, first=0, k_ready=None, wait_bank=True, inc=True):
                if first == 0:
                    pe.wait_ge(w_ready, u + 1)
                if wait_bank:
                    pe.wait_ge(bank_free, u + 1)
                o = ps[:, slot, :] if o is None else o
                for k in range(n):
                    if k_ready is not None:
                        pe.wait_ge(k_ready[0], k_ready[1] + k + 1)
                    wh, wl = wblock(slot, first + k)
                    mm = three(o, wh, xh[:, k, :], wl, xl[:, k, :], k == 0, k == n - 1)
                return mm.then_inc(unit_done, 1) if inc else mm

            def part(u, slot, k0, k1, xh=xg_hi, xl=xg_lo):
                if k0 == 0:
                    pe.wait_ge(w_ready, u + 1)
                    pe.wait_ge(bank_free, u + 1)
                for k in range(k0, k1):
                    wh, wl = wblock(slot, k)
                    mm = three(ps[:, slot, :], wh, xh[:, k, :], wl, xl[:, k, :], k == 0, k == DC - 1)
                if k1 == DC:
                    mm.then_inc(unit_done, 1)

            def units(u0, n, xh, xl, k=DC, k_ready=None):
                with pe.Fori(0, n // 2) as i:
                    for j in range(2):
                        unit(i * 2 + (u0 + j), (u0 + j) % 2, xh, xl, k, k_ready=k_ready if j == 0 else None)

            def norm_sums(n):
                pe.wait_ge(summed, 10 * n)
                for tb in range(QB):
                    mm = pe.matmul(ps[:, 7, tb:tb + 1], sq_sum[:, 0, tb * P:(tb + 1) * P], mean_col[:], start=True, stop=True)
                mm.then_inc(ssq_done, 1)

            def norm_spread(n):
                pe.wait_ge(diag_done, n)
                pe.matmul(ps[:, 7, :], ones[:], r_diag[:].rearrange("p a b -> p (a b)"), start=True, stop=True).then_inc(bcast_done, 1)

            def norm(n):
                norm_sums(n)
                norm_spread(n)

            def first_two(u0, n, prep):
                unit(u0, u0 % 2, xg_hi, xg_lo, k_ready=(prep_lo, DC * prep))
                norm_sums(n)
                unit(u0 + 1, (u0 + 1) % 2, xg_hi, xg_lo)
                norm_spread(n)

            def rest(u0, n):
                with pe.Fori(1, n // 2) as i:
                    for j in range(2):
                        unit(i * 2 + (u0 + j), (u0 + j) % 2, xg_hi, xg_lo)

            pe.wait_ge(c_pool, 11)
            pe.wait_ge(c_dve, 4)
            pe.wait_ge(c_act, 4)
            first_two(U["glu"], 1, 0)
            rest(U["glu"], 8)
            units(U["cmp_in"], 4, xg_hi, xg_lo)
            for kv in range(2):
                pe.wait_ge(s_cmp["lo"], kv + 1)
                for i in range(4):
                    uu = U["cmp_hidden"] + 4 * kv + i
                    pe.wait_ge(w_ready, uu + 1)
                    for c in range(4):
                        for half in range(2):
                            wh, wl = wblock(uu % 2, 2 * c + half)
                            mm = three(ps[:, 2 + 2 * kv + half, 0:2 * NC1], wh, blk_hi[:, kv, 4 * i + c, :],
                                       wl, blk_lo[:, kv, 4 * i + c, :], i == 0 and c == 0, i == 3 and c == 3)
                    mm.then_inc(unit_done, 1)
            uu = U["cmp_out"]
            sl = uu % 2
            pe.wait_ge(w_ready, uu + 1)
            pe.wait_ge(s_cmp["glo"], 2)
            for half in range(2):
                wh, wl = wblock(sl, half)
                three(ps[:, 6, 0:2 * NC1], wh, hid_hi[:, 0, half, :], wl, hid_lo[:, 0, half, :], half == 0, half == 1)
            for g in range(2):
                for half in range(2):
                    cols = slice(256 + half * HD, 256 + (half + 1) * HD)
                    own = slice(g * NC1, (g + 1) * NC1)
                    o = ps[0:NC1, 7, g * HD:(g + 1) * HD]
                    mm = three(o, hid_hi[:, 1, half, own], w_hi[:, sl, cols], hid_lo[:, 1, half, own], w_lo[:, sl, cols],
                               half == 0, half == 1)
            mm.then_inc(unit_done, 1)
            for j in range(2):
                uu = U["keys"] + j
                unit(uu, uu % 2, xg_hi, xg_lo)
            for j in range(2):
                uu = U["values"] + j
                unit(uu, uu % 2, xg_hi, xg_lo)
            uu = U["gates"]
            unit(uu, uu % 2, xg_hi, xg_lo)
            for j in range(2):
                pe.wait_ge(bank_free, U["values"] + j + 1 + CREDIT)
                for tb in range(QB):
                    mm = pe.transpose(ps[:, 2 + j, tb * P:(tb + 1) * P], T2[:, j, tb * P:(tb + 1) * P], ident[:])
                mm.then_inc(s_kv["turned"], 1)
            pe.wait_ge(s_gate["sig"], 1)
            for tb in range(QB):
                mm = pe.transpose(ps[:, 4, tb * 32:(tb + 1) * 32], sq[0:32, 0, tb * P:(tb + 1) * P], ident[0:32, 0:32])
            mm.then_inc(s_gate["turned"], 1)
            def attention(A, q, k, v, pt, probs, h, r0, idx, branch_bank):
                qh, ql = q
                kh, kl = k
                vh, vl = v

                def scores(qi, c_row=None):
                    e = idx + qi
                    pe.wait_ge(A["exps"], e + 1)
                    b = 2 + (h["par"] + qi) % 2
                    n = (qi + 1) * P
                    rows = slice(r0, r0 + HD)
                    o = ps[:, b, 0:n]
                    qs = slice(qi * P, n)
                    pe.matmul(o, qh[rows, qs], kh[rows, 0:n], start=True, stop=False)
                    pe.matmul(o, qh[rows, qs], kl[rows, 0:n], start=False, stop=False)
                    pe.matmul(o, ql[rows, qs], kh[rows, 0:n], start=False, stop=False)
                    if c_row is not None:
                        pe.matmul(o, ones_r[:], c_row[:, 0:n], start=False, stop=False)
                    pe.matmul(ps[:, b, qi * P:n], ident_r[:], causal_r[:], start=False, stop=True).then_inc(A["scores"], 1)

                def turn(kb):
                    e = idx + kb
                    pe.wait_ge(A["lo"], e + 1)
                    if kb == 0:
                        pe.wait_ge(A["probs"], h["sidx"] + (QB + CREDIT))
                    b = 4 + (h["par"] + kb) % 2
                    for qi in range(kb, QB):
                        off = P_OFF[qi] + kb * P
                        mm = pe.transpose(ps[:, b, qi * P:(qi + 1) * P], probs[:, off:off + P], ident[:])
                    mm.then_inc(A["turned"], 1)

                def pv(kb, start, stop):
                    e = idx + kb
                    pe.wait_ge(A["lo"], e + 1 + CREDIT)
                    b = (h["par"] + kb) % 2
                    o = ps[:, branch_bank, kb * P:S]
                    ph, plo = pt[0][:, b, kb * P:S], pt[1][:, b, kb * P:S]
                    pe.matmul(o, vh[:, kb, :], ph, start=start and kb == 0, stop=False)
                    pe.matmul(o, vh[:, kb, :], plo, start=False, stop=False)
                    pe.matmul(o, vl[:, kb, :], ph, start=False, stop=stop and kb == QB - 1).then_inc(A["pv"], 1)

                return scores, turn, pv

            pair_events = 18

            unit(U["q0"], U["q0"] % 2, xg_hi, xg_lo)
            pe.wait_ge(s_kv["lo"], 4)
            pe.wait_ge(s_cmp["klo"], 2)
            for p in range(4):
                qp = (q_hi[:, p % 2, :], q_lo[:, p % 2, :])
                pe.wait_ge(A1["qlo"], p + 1)

                def cmp_scores(hd):
                    e = p * pair_events + 9 * hd
                    pe.wait_ge(A1["exps"], e + 1)
                    b = 2 + e % 2
                    rows = slice(hd * HD, (hd + 1) * HD)
                    for qi in range(QB):
                        o, qs = ps[:, b, qi * NCP:(qi + 1) * NCP], slice(qi * P, (qi + 1) * P)
                        pe.matmul(o, qp[0][rows, qs], kc_hi[rows, :], start=True, stop=False)
                        pe.matmul(o, qp[0][rows, qs], kc_lo[rows, :], start=False, stop=False)
                        pe.matmul(o, qp[1][rows, qs], kc_hi[rows, :], start=False, stop=False)
                        mm = pe.matmul(o, ident_r[:], cmp_mask_r[:, qi, :], start=False, stop=True)
                    mm.then_inc(A1["scores"], 1)

                def cmp_turn(hd):
                    e = p * pair_events + 9 * hd
                    pe.wait_ge(A1["lo"], e + 1)
                    pe.wait_ge(A1["c"], 2 * p + hd + 1)
                    b = 4 + e % 2
                    for qi in range(QB):
                        mm = pe.transpose(ps[0:NCP, b, qi * P:(qi + 1) * P], prob_c[:, hd, qi, :], ident[:])
                    mm.then_inc(A1["turned"], 1)

                def cmp_pv(hd):
                    e = p * pair_events + 9 * hd
                    pe.wait_ge(A1["lo"], e + 1 + CREDIT)
                    pe.wait_ge(A1["olo"], 2 * p + hd + 1)
                    b = e % 2
                    o = ps[:, 6 + hd, :]
                    pe.matmul(o, vc_hi[:], pt_hi[0:NCP, b, :], start=True, stop=False)
                    pe.matmul(o, vc_hi[:], pt_lo[0:NCP, b, :], start=False, stop=False)
                    pe.matmul(o, vc_lo[:], pt_hi[0:NCP, b, :], start=False, stop=False).then_inc(A1["pv"], 1)

                F = []
                for hd in range(2):
                    for br in range(2):
                        idx = p * pair_events + 9 * hd + 1 + 4 * br
                        n = 4 * p + 2 * hd + br
                        F.append(attention(A1, qp, (kk_hi[:, br, :], kk_lo[:, br, :]), (vv_hi[:, br], vv_lo[:, br]),
                                           (pt_hi, pt_lo), prob[:, n % 2, :], {"par": idx, "sidx": 4 * n}, hd * HD, idx, 6 + hd))

                mine = pair_units(p)

                def fill(n, k0, k1):
                    if mine[n] is not None:
                        part(mine[n], mine[n] % 2, k0, k1)

                def two_steps(new, old, last, n):
                    ns, (_, ot, ov) = new[0], old
                    ns(0); ns(1); fill(n, 2, 5); ot(0); ot(1); ns(2); ov(0, False, last); ot(2); ns(3); fill(n, 5, 8)
                    ov(1, False, last); ot(3); ov(2, False, last); ov(3, False, last)

                cmp_scores(0)
                F[0][0](0); fill(0, 0, 2); cmp_turn(0); F[0][0](1); fill(0, 2, 6)
                cmp_pv(0); F[0][0](2); F[0][0](3); fill(0, 6, 8); fill(1, 0, 2)
                two_steps(F[1], F[0], False, 1)
                fill(4, 0, 2); cmp_scores(1)
                two_steps(F[2], F[1], True, 4)
                cmp_turn(1); fill(2, 0, 2); cmp_pv(1)
                two_steps(F[3], F[2], False, 2)
                _, ot, ov = F[3]
                ot(0); ot(1)
                if p < 3:
                    fill(3, 0, 4)
                ov(0, False, True); ot(2); ov(1, False, True); ot(3); ov(2, False, True)
                if p < 3:
                    fill(3, 4, 8)
                ov(3, False, True)

            pe.wait_ge(s_ln["sum"], 3)
            pe.matmul(ps[:, 4, :], mean_ch[:], T[:, 0, :], start=True, stop=True).then_inc(s_ln["mean"], 1)
            part(mine[3], mine[3] % 2, 0, 8)
            pe.wait_ge(s_ln["acc"], 4)
            for tb in range(QB):
                mm = pe.matmul(ps[:, 5, tb:tb + 1], T[:, 1, tb * P:(tb + 1) * P], mean_ch[:, 0:1], start=True, stop=True)
            mm.then_inc(s_ln["var"], 1)
            pe.wait_ge(s_ln["diag"], 1)
            pe.matmul(ps[:, 5, :], ones[:], r_diag[:].rearrange("p a b -> p (a b)"), start=True, stop=True).then_inc(s_ln["bc"], 1)
            pe.wait_ge(A1["olo"], CREDIT + 8)
            with pe.Fori(0, 4) as i:
                for j in range(2):
                    u0 = U["mix"] + j
                    uu = i * 2 + u0
                    unit(uu, u0 % 2, o_hi, o_lo, 4, inc=False)
                    if j == 0:
                        pe.wait_ge(s_ln["lo"], 4)
                    unit(uu, u0 % 2, xg_hi, xg_lo, 4, o=ps[:, 2 + u0 % 2, :], first=4, wait_bank=False)
            units(U["w_out"], 8, y_hi, y_lo, k_ready=(s_mix["lo"], 0))

            for n, (kind, p) in enumerate(ffn_order(len(FF1_PARTS))):
                u0 = U[f"ffn_{kind}{p}"]
                if kind == "up":
                    if p == 0:
                        first_two(u0, 2, 1)
                        rest(u0, 2 * FF1_PARTS[0])
                    else:
                        units(u0, 2 * FF1_PARTS[p], xg_hi, xg_lo)
                else:
                    base = sum(FF1_PARTS[:p])
                    units(u0, 8, h_hi[:, p % 2], h_lo[:, p % 2], FF1_PARTS[p], k_ready=(s_ffn["hlo"], base))

            def ple_gate(n, norm_n, prep):
                first_two(U[f"ple{n}"] + 2, norm_n, prep)
                rest(U[f"ple{n}"] + 2, DC)

            def ple_embed(n):
                u0 = U[f"ple{n}"]
                pe.wait_ge(s_ple["plo"], n + 1)
                for half in range(2):
                    uu = u0 + half
                    pe.wait_ge(w_ready, uu + 1)
                    for m in range(4):
                        t = 4 * half + m
                        if t >= 4:
                            pe.wait_ge(s_ple["e"], DC * n + t - 4 + 1)
                        for k in range(2):
                            wh, wl = wblock(uu % 2, 2 * m + k)
                            mm = three(ps[:, 2 + t % 4, :], wh, p_hi[:, k, :], wl, p_lo[:, k, :], k == 0, k == 1)
                        if m < 3:
                            mm.then_inc(s_ple["epe"], 1)
                    mm.then_inc(unit_done, 1)

            ple_embed(0)
            ple_gate(0, 3, 2)
            norm(4)

            uu = U["forget"]
            unit(uu, uu % 2, xg_hi, xg_lo, k_ready=(prep_lo, DC * 3))
            norm(5)

            def fox_unit(j, uu, slot):
                unit(uu, slot, xg_hi, xg_lo)

            def fox_turn(p, slot):
                pe.wait_ge(A2["vs"], p + 1)
                for tb in range(QB):
                    mm = pe.transpose(ps[:, slot, tb * P:(tb + 1) * P], fv[:, 0, tb * P:(tb + 1) * P], ident[:])
                mm.then_inc(A2["vturned"], 1)

            u0 = U["fox"]
            for j in range(3):
                fox_unit(j, u0 + j, (u0 + j) % 2)
            fox_turn(0, (u0 + 2) % 2)

            def fox_pair(p, par, more):
                nxt = [(u0 + 3 + 3 * par + j) % 2 for j in range(3)]
                pe.wait_ge(A2["qklo"], p * 2 + 2)
                pe.wait_ge(bank_free, p * 3 + (u0 + 3 + CREDIT))
                hs = []
                for hd in range(2):
                    hs.append(attention(A2, (fq_hi[:, par, :], fq_lo[:, par, :]), (fk_hi[:, par, :], fk_lo[:, par, :]),
                                        (fv_hi[:, par], fv_lo[:, par]), (fpt_hi, fpt_lo), fprob[:, hd, :],
                                        {"par": 0, "sidx": p * 8 + 4 * hd}, hd * HD, p * 8 + 4 * hd, 6 + hd))
                (sa, ta, va), (sb_, tb_, vb) = hs
                pe.wait_ge(A2["crow"], p * 2 + 1)
                ca, cb = c_head[:, 0, :], c_head[:, 1, :]

                def fill(j, k0, k1):
                    if more:
                        part(p * 3 + (u0 + 3 + j), nxt[j], k0, k1)

                sa(0, ca); sa(1, ca); fill(0, 0, 8)
                sa(2, ca); sa(3, ca); fill(1, 0, 4)
                pe.wait_ge(A2["crow"], p * 2 + 2)
                sb_(0, cb); sb_(1, cb); fill(1, 4, 8)
                pe.wait_ge(A2["olo"], p * 2 + 1)
                ta(0); ta(1); fill(2, 0, 2); sb_(2, cb); va(0, True, True); ta(2); sb_(3, cb); va(1, True, True); ta(3)
                va(2, True, True); fill(2, 2, 5); va(3, True, True)
                pe.wait_ge(A2["olo"], p * 2 + 2)
                tb_(0); tb_(1); fill(2, 5, 8); vb(0, True, True); tb_(2); vb(1, True, True); tb_(3); vb(2, True, True)
                if more:
                    fox_turn(p + 1, nxt[2])
                vb(3, True, True)

            with pe.Fori(0, 3) as i:
                for par in range(2):
                    fox_pair(i * 2 + par, par, True)
            fox_pair(6, 0, True)
            fox_pair(7, 1, False)
            pe.wait_ge(A2["olo"], CREDIT + 16)
            units(U["fox_out"], 8, fo_hi, fo_lo)
            norm(6)

            def mlp(n, norm_n, prep):
                for kind, p in ffn_order(len(FF2_PARTS)):
                    u0 = U[f"mlp{n}_{kind}{p}"]
                    if kind == "up" and p == 0:
                        first_two(u0, norm_n, prep)
                        rest(u0, 8)
                    elif kind == "up":
                        units(u0, 8, xg_hi, xg_lo)
                    else:
                        units(u0, 8, h_hi[:, p % 2], h_lo[:, p % 2], 8, k_ready=(s_mlp["lo"], 32 * (n - 1) + 8 * p))
                norm(norm_n + 1)

            mlp(1, 7, 4)
            ple_embed(1)
            ple_gate(1, 9, 5)
            norm(10)
            u0 = U["conv3"]
            first_two(u0, 11, 6)
            for j in range(2, 6):
                unit(u0 + j, (u0 + j) % 2, xg_hi, xg_lo)
            with pe.Fori(1, 4) as i:
                for j in range(6):
                    unit(i * 6 + (u0 + j), (u0 + j) % 2, xg_hi, xg_lo)
            units(U["conv3_out"], 8, cy_hi, cy_lo, k_ready=(s_c3["lo"], 0))
            norm(12)
            mlp(2, 13, 7)
            ple_embed(2)
            ple_gate(2, 15, 8)
            norm(16)

        @block.vector
        def _(dve):
            def scaled(u, slot, out, n_done=None):
                dve.wait_ge(unit_done, u + 1)
                dve.tensor_tensor(out, ps[:, slot:slot + 1, :], R[:], ALU.mult).then_inc(bank_free, 1)

            def units(u0, n, body, per=2, start=0):
                with dve.Fori(start, n // per) as i:
                    for j in range(per):
                        body(i * per + j, j, i * per + (u0 + j), (u0 + j) % 2)

            def low(out, x, hi, done):
                dve.tensor_tensor(out, x, hi.bitcast(F32), ALU.subtract).then_inc(done, 1)

            def norm_start(n):
                if n > 1:
                    dve.wait_ge(ssq_done, n - 1)
                dve.memset(sq_sum[:], 0.0).then_inc(summed, CREDIT)

            def add_square(n, m, j):
                dve.wait_ge(squared, m + (DC * (n - 1) + 1))
                dve.wait_ge(summed, m + (10 * (n - 1) + CREDIT))
                dve.tensor_tensor(sq_sum[:], sq_sum[:], sq[:, j:j + 1, :], ALU.add).then_inc(summed, 1)

            def norm_inverse(n):
                dve.wait_ge(rms_done, n)
                if n > 1:
                    dve.wait_ge(diag_done, n - 1)
                dve.reciprocal(rms_c[:, 1, :], rms_c[:, 0, :]).then_inc(inv_done, 1)
                dve.wait_ge(inv_done, n)
                if n > 1:
                    dve.wait_ge(bcast_done, n - 1)
                dve.tensor_tensor(r_diag[:], ident[:].unsqueeze(1).to_broadcast([P, QB, P]),
                                  rms_c[:, 1, :].unsqueeze(2).to_broadcast([P, QB, P]), ALU.mult).then_inc(diag_done, 1)

            def prep_low(prep, m, g):
                dve.wait_ge(prep_hi, m + (DC * prep + 1))
                dve.scalar_tensor_tensor(xg_lo[:, ds(m, 1), :], X[:, ds(m, 1), :], g, xg_hi[:, ds(m, 1), :].bitcast(F32),
                                         ALU.mult, ALU.subtract).then_inc(prep_lo, 1)

            dve.memset(ones[:], 1.0).then_inc(c_dve, 1)
            dve.memset(mean_col[:], 1.0 / D).then_inc(c_dve, 1)
            dve.memset(mean_ch[:], 1.0 / (CT * P)).then_inc(c_dve, 1)
            dve.memset(eps_col[:], EPS).then_inc(c_dve, 1)
            dve.memset(token[:, 0:1], 0.0).then_inc(bank_free, CREDIT)
            for n, key in enumerate(("exps", "lo", "olo", "probs")):
                for g, A in enumerate((A1, A2)):
                    dve.memset(token[:, 4 * g + n + 1:4 * g + n + 2], 0.0).then_inc(A[key], CREDIT)
            dve.memset(token[:, 9:10], 0.0).then_inc(s_mrg["sig"], CREDIT)
            norm_start(1)
            dve.memset(glu[:, :, 0:PAD], 0.0).then_inc(s_glu["gated"], 1)
            dve.wait_ge(vec_loaded, 16)
            dve.wait_ge(c_pool, 11)
            with dve.Fori(0, DC // 2) as i:
                for j in range(2):
                    m = i * 2 + j
                    add_square(1, m, j)
                    prep_low(0, m, vcol("g_mix", m))
            norm_inverse(1)
            dve.wait_ge(r_done, 1)
            u0 = U["glu"]
            with dve.Fori(0, CT) as i:
                dve.wait_ge(s_glu["gated"], i + 1)
                for j in range(2):
                    scaled(i * 2 + (u0 + j), j, T[:, j:j + 1, :])
                dve.wait_ge(s_glu["sig"], i + 1)
                dve.tensor_tensor(glu[:, ds(i, 1), PAD:PAD + S], T[:, 0:1, :], T2[:, 0:1, :], ALU.mult).then_inc(s_glu["gated"], 1)
            for j in range(4):
                uu = U["cmp_in"] + j
                dve.wait_ge(unit_done, uu + 1)
                dve.tensor_tensor(kv_dup[0:HD, j, :], ps[0:HD, uu % 2, :], R[0:HD, 0, :], ALU.mult).then_inc(s_cmp["dup"], 1)
                dve.tensor_tensor(kv_dup[HD:P, j, 0:S - 1], ps[HD:P, uu % 2, 1:S], R[HD:P, 0, 1:S], ALU.mult).then_inc(bank_free, 1)
            dve.memset(kc_f[:], 0.0).then_inc(s_cmp["out"], 1)
            dve.memset(vc_f[:], 0.0).then_inc(bank_free, 9)
            dve.wait_ge(s_cmp["dup"], 4)
            dve.wait_ge(bank_free, U["keys"] + CREDIT)
            for kv, pos in enumerate(("pos_k", "pos_v")):
                for g in range(2):
                    src = kv_dup[:, 2 * kv + g, :].rearrange("p (c s) -> p s c", s=16)
                    for half in range(2):
                        o = blk[:, kv, 8 * half:8 * half + 8, g * NC1:(g + 1) * NC1]
                        at = VEC[pos] + 8 * half
                        dve.tensor_tensor(o, src[:, 0:16:2, half:half + NC1],
                                          vec[:, at:at + 8].unsqueeze(2).to_broadcast([P, 8, NC1]), ALU.add).then_inc(s_cmp["blk"], 1)
            for kv in range(2):
                dve.wait_ge(s_cmp["hi"], kv + 1)
                low(blk_lo[:, kv], blk[:, kv], blk_hi[:, kv], s_cmp["lo"])
            for kv in range(2):
                dve.wait_ge(s_cmp["ghi"], kv + 1)
                low(hid_lo[:, kv], hid[:, kv], hid_hi[:, kv], s_cmp["glo"])
            dve.wait_ge(unit_done, U["cmp_out"] + 1)
            dve.wait_ge(s_cmp["out"], 1)
            dve.tensor_copy(kc_f[0:HD, 0:NC1], ps[0:HD, 6, 0:NC1]).then_inc(s_cmp["out"], 1)
            dve.tensor_copy(kc_f[HD:P, 0:NC1], ps[HD:P, 6, NC1:2 * NC1]).then_inc(s_cmp["out"], 1)
            dve.tensor_copy(vc_f[0:NC1, :], ps[0:NC1, 7, 0:P]).then_inc(s_cmp["out"], 1)
            dve.wait_ge(s_cmp["khi"], 2)
            dve.wait_ge(s_cmp["out"], 4)
            low(kc_lo[:], kc_f[:], kc_hi[:], s_cmp["klo"])
            low(vc_lo[:], vc_f[:], vc_hi[:], s_cmp["klo"])
            dve.wait_ge(s_glu["gated"], CT + 1)
            for j in range(2):
                uu = U["keys"] + j
                scaled(uu, uu % 2, T[:, j:j + 1, :])
                dve.wait_ge(s_kv["hi"], j + 1)
                low(kk_lo[:, j, :], T[:, j, :], kk_hi[:, j, :], s_kv["lo"])
            for j in range(2):
                uu = U["values"] + j
                scaled(uu, uu % 2, T2[:, j:j + 1, :])
            uu = U["gates"]
            dve.wait_ge(s_kv["lo"], 2)
            scaled(uu, uu % 2, T[:, 0:1, :])
            for j in range(2):
                dve.wait_ge(s_kv["hi"], 3 + j)
                low(vv_lo[:, j], ps[:, 2 + j, :].rearrange("p (a b) -> p a b", b=P), vv_hi[:, j], s_kv["lo"])
            dve.wait_ge(s_gate["turned"], 1)
            dve.tensor_copy(gates[:], ps[:, 4, 0:QB * 32].rearrange("p (a b) -> p a b", b=32)).then_inc(s_gate["ready"], 1)

            dve.wait_ge(s_kv["lo"], 4)
            dve.wait_ge(s_glu["gated"], CT + 1)

            def taps(ct, k0, k1):
                for k in range(k0, k1):
                    acc, src, w = conv_acc[:, ct, :], glu[:, ct, k:k + S], vcol("conv_w", ct * CONV_TAPS + k)
                    if k == 0:
                        ins = dve.tensor_scalar(acc, src, w, vcol("conv_b", ct), ALU.mult, ALU.add)
                    else:
                        dve.wait_ge(s_mrg["conv"], ct * CONV_TAPS + k)
                        ins = dve.scalar_tensor_tensor(acc, src, w, acc, ALU.mult, ALU.add)
                    ins.then_inc(s_mrg["conv"], 1)

            def merge_gate(p, i):
                uu, m = pair_units(p)[i], 4 * p + i
                scaled(uu, uu % 2, merge[:, m:m + 1, :])

            def peak(A, e, par, st, qi, b):
                dve.wait_ge(A["scores"], e + 1)
                dve.tensor_reduce(st[:, 0, par, qi:qi + 1], ps[:, b, 0:(qi + 1) * P], AX.X, ALU.max, negate=True).then_inc(A["peak"], 1)

            def normalise(A, e, n, par, st, pr, qi, gate=None):
                dve.wait_ge(A["exps"], e + 1 + CREDIT)
                dve.wait_ge(A["probs"], n * QB + (qi + CREDIT))
                dve.reciprocal(st[:, 2, par, qi:qi + 1], st[:, 1, par, qi:qi + 1]).then_inc(A["inv"], 1)
                dve.wait_ge(A["inv"], n * QB + (qi + 1))
                row = pr[:, P_OFF[qi]:P_OFF[qi] + (qi + 1) * P]
                dve.tensor_scalar(row, row, st[:, 2, par, qi:qi + 1], gate, ALU.mult,
                                  ALU.bypass if gate is None else ALU.mult).then_inc(A["probs"], 1)

            def split_turned(A, e, b, pt, kb):
                dve.wait_ge(A["hi"], e + 1)
                low(pt[1][:, b, kb * P:S], ps[:, 4 + b, kb * P:S], pt[0][:, b, kb * P:S], A["lo"])

            def low_q(A, out, x, hi, done):
                dve.scalar_tensor_tensor(out, x, HD ** -0.5, hi.bitcast(F32), ALU.mult, ALU.subtract).then_inc(done, 1)

            def nsa_q(p):
                uu = pair_units(p - 1)[4] if p else U["q0"]
                if p >= 2:
                    dve.wait_ge(A1["qlo"], p - 1)
                scaled(uu, uu % 2, T[:, p % 2:p % 2 + 1, :])
                dve.wait_ge(A1["qhi"], p + 1)
                low_q(A1, q_lo[:, p % 2, :], T[:, p % 2, :], q_hi[:, p % 2, :], A1["qlo"])

            dve.wait_ge(s_gate["ready"], 1)
            nsa_q(0)
            for p in range(4):
                e0 = 18 * p

                def cmp_peak(hd):
                    e = e0 + 9 * hd
                    sc = ps[:, 2 + e % 2, 0:QB * NCP].rearrange("p (a b) -> p a b", b=NCP)
                    dve.wait_ge(A1["scores"], e + 1)
                    if e:
                        dve.wait_ge(A1["c"], 2 * p + hd)
                    dve.tensor_reduce(c_stat[:, 0, :], sc, AX.X, ALU.max).then_inc(A1["cs"], 1)
                    dve.wait_ge(A1["cs"], 5 * (2 * p + hd) + 1)
                    dve.tensor_tensor(prob_c[:, hd], sc, c_stat[:, 0, :].unsqueeze(2).to_broadcast([P, QB, NCP]),
                                      ALU.subtract).then_inc(A1["peak"], 1)

                def cmp_normalise(hd):
                    e = e0 + 9 * hd
                    n = 5 * (2 * p + hd)
                    dve.wait_ge(A1["exps"], e + 1 + CREDIT)
                    dve.tensor_reduce(c_stat[:, 1, :], prob_c[:, hd], AX.X, ALU.add).then_inc(A1["cs"], 1)
                    dve.wait_ge(A1["cs"], n + 2)
                    dve.reciprocal(c_stat[:, 2, :], c_stat[:, 1, :]).then_inc(A1["cs"], 1)
                    dve.wait_ge(A1["cs"], n + 3)
                    dve.tensor_tensor(c_stat[:, 2, :], c_stat[:, 2, :], gates[:, :, 4 * hd + p], ALU.mult).then_inc(A1["cs"], 1)
                    dve.wait_ge(A1["cs"], n + 4)
                    dve.tensor_tensor(c_stat[:, 3, :], c_stat[:, 2, :], valid[:, :, 0], ALU.mult).then_inc(A1["cs"], 1)
                    dve.wait_ge(A1["cs"], n + 5)
                    dve.tensor_tensor(prob_c[:, hd], prob_c[:, hd], c_stat[:, 3, :].unsqueeze(2).to_broadcast([P, QB, NCP]),
                                      ALU.mult).then_inc(A1["c"], 1)

                def cmp_split(hd):
                    e = e0 + 9 * hd
                    dve.wait_ge(A1["hi"], e + 1)
                    low(pt_lo[0:NCP, e % 2, :], ps[0:NCP, 4 + e % 2, :], pt_hi[0:NCP, e % 2, :], A1["lo"])

                def where(f):
                    return e0 + 9 * (f // 2) + 1 + 4 * (f % 2), 4 * p + f, 8 * (1 + f % 2) + 4 * (f // 2) + p

                def mx(f, qi):
                    e, n, _ = where(f)
                    peak(A1, e + qi, n % 2, stat, qi, 2 + (e + qi) % 2)

                def nrm(f, qi):
                    e, n, col = where(f)
                    normalise(A1, e + qi, n, n % 2, stat, prob[:, n % 2, :], qi, gates[:, qi, col:col + 1])

                def lo(f, kb):
                    e = where(f)[0] + kb
                    split_turned(A1, e, e % 2, (pt_hi, pt_lo), kb)

                def out_low(hd):
                    rows = slice(hd * HD, (hd + 1) * HD)
                    dve.wait_ge(A1["ohi"], 2 * p + hd + 1)
                    low(o_lo[rows, p, :], ps[rows, 6 + hd, :], o_hi[rows, p, :], A1["olo"])

                def two_steps(new, old, n, k):
                    mx(new, 0); mx(new, 1); taps(p, k, k + 2); lo(old, 0); nrm(new, 0); mx(new, 2); lo(old, 1); nrm(new, 1)
                    lo(old, 2); taps(p, k + 2, k + 4); mx(new, 3); nrm(new, 2); nrm(new, 3)
                    if n < 4:
                        merge_gate(p, n)
                    elif p < 3:
                        nsa_q(p + 1)
                    lo(old, 3); taps(p, k + 4, k + 6)

                cmp_peak(0); mx(0, 0); cmp_normalise(0); cmp_split(0); mx(0, 1); nrm(0, 0); nrm(0, 1); taps(p, 0, 5)
                mx(0, 2); mx(0, 3); nrm(0, 2); nrm(0, 3); merge_gate(p, 0); taps(p, 5, 7)
                two_steps(1, 0, 1, 7)
                cmp_peak(1)
                two_steps(2, 1, 4, 13)
                cmp_normalise(1); out_low(0); cmp_split(1)
                two_steps(3, 2, 2, 19)
                lo(3, 0); taps(p, 25, 27); lo(3, 1); taps(p, 27, 29); lo(3, 2); taps(p, 29, CONV_TAPS); lo(3, 3)
                if p < 3:
                    merge_gate(p, 3)
                out_low(1)

            acc4 = [conv_acc[:, ct, :] for ct in range(CT)]
            dve.wait_ge(s_mrg["conv"], CT * CONV_TAPS)
            dve.wait_ge(A1["qlo"], 4)
            dve.tensor_tensor(T[:, 0, :], acc4[0], acc4[1], ALU.add).then_inc(s_ln["sum"], 1)
            for ct in (2, 3):
                dve.wait_ge(s_ln["sum"], ct - 1)
                dve.tensor_tensor(T[:, 0, :], T[:, 0, :], acc4[ct], ALU.add).then_inc(s_ln["sum"], 1)
            dve.wait_ge(s_ln["mean"], 1)
            for ct in range(CT):
                dve.tensor_tensor(acc4[ct], acc4[ct], ps[:, 4, :], ALU.subtract).then_inc(s_ln["cent"], 1)
            merge_gate(3, 3)
            for ct in range(CT):
                dve.wait_ge(s_ln["sq"], ct + 1)
                if ct == 0:
                    dve.tensor_copy(T[:, 1, :], sq[:, 0, :]).then_inc(s_ln["acc"], 1)
                else:
                    dve.wait_ge(s_ln["acc"], ct)
                    dve.tensor_tensor(T[:, 1, :], T[:, 1, :], sq[:, ct % 2, :], ALU.add).then_inc(s_ln["acc"], 1)
            dve.wait_ge(s_ln["sd"], 1)
            dve.reciprocal(rms_c[:, 1, :], rms_c[:, 0, :]).then_inc(s_ln["inv"], 1)
            dve.wait_ge(s_ln["inv"], 1)
            dve.tensor_tensor(r_diag[:], ident[:].unsqueeze(1).to_broadcast([P, QB, P]),
                              rms_c[:, 1, :].unsqueeze(2).to_broadcast([P, QB, P]), ALU.mult).then_inc(s_ln["diag"], 1)
            dve.wait_ge(s_ln["r"], 1)
            dve.wait_ge(s_ln["cent"], 4)
            for ct in range(CT):
                if ct >= 2:
                    dve.wait_ge(s_ln["act"], ct - 1)
                dve.tensor_tensor(T2[:, ct % 2, :], acc4[ct], R[:, 0, :], ALU.mult).then_inc(s_ln["n"], 1)
                if ct >= 1:
                    dve.wait_ge(s_ln["hi"], ct)
                    low(xg_lo[:, ct - 1, :], acc4[ct - 1], xg_hi[:, ct - 1, :], s_ln["lo"])
            dve.wait_ge(s_ln["hi"], CT)
            low(xg_lo[:, CT - 1, :], acc4[CT - 1], xg_hi[:, CT - 1, :], s_ln["lo"])

            def mix(m, j, u, slot):
                dve.wait_ge(unit_done, u + 1)
                dve.wait_ge(s_mrg["sig"], CREDIT + 4)
                dve.tensor_tensor(T[:, j:j + 1, :], ps[:, slot:slot + 1, :], merge[:, ds(m, 1), :], ALU.mult).then_inc(s_mix["a"], 1)
                dve.scalar_tensor_tensor(T2[:, j:j + 1, :], ps[:, slot + 2:slot + 3, :], vcol("b_conv_out", m), merge[:, ds(m + DC, 1), :],
                                         ALU.add, ALU.mult).then_inc(bank_free, 1)
                dve.wait_ge(s_mix["a"], m + 1)
                dve.wait_ge(bank_free, u + (1 + CREDIT))
                dve.tensor_tensor(T[:, j:j + 1, :], T[:, j:j + 1, :], T2[:, j:j + 1, :], ALU.add).then_inc(s_mix["y"], 1)
                dve.wait_ge(s_mix["hi"], m + 1)
                low(y_lo[:, ds(m, 1), :], T[:, j:j + 1, :], y_hi[:, ds(m, 1), :], s_mix["lo"])
                dve.wait_ge(s_mix["lo"], m + 1)

            units(U["mix"], DC, mix)

            def add_to(dst, m, u, slot):
                dve.wait_ge(unit_done, u + 1)
                dve.wait_ge(bank_free, u + CREDIT)
                dve.tensor_tensor(dst[:, ds(m, 1), :], dst[:, ds(m, 1), :], ps[:, slot:slot + 1, :], ALU.add).then_inc(bank_free, 1)

            def into_norm(dst, n, prep=None, gain=None):
                def body(m, j, u, slot):
                    add_to(dst, m, u, slot)
                    add_square(n, m, j)
                    if prep is not None:
                        prep_low(prep, m, vcol(gain, m))
                return body

            norm_start(2)
            units(U["w_out"], DC, into_norm(X, 2, 1, "g_ffn"))
            norm_inverse(2)
            dve.wait_ge(r_done, 2)

            for kind, p in ffn_order(len(FF1_PARTS)):
                u0 = U[f"ffn_{kind}{p}"]
                base = sum(FF1_PARTS[:p])
                if kind == "up":
                    with dve.Fori(0, FF1_PARTS[p]) as m:
                        for j in range(2):
                            uu = m * 2 + (u0 + j)
                            scaled(uu, (u0 + j) % 2, T[:, j:j + 1, :])
                            tile = m + (base + 22 * j)
                            done = m * 2 + (2 * base + j)
                            y, t = u4[:, j:j + 1, :], T[:, j:j + 1, :]
                            dve.wait_ge(s_ffn["t2"], done + 1)
                            dve.wait_ge(bank_free, uu + (1 + CREDIT))
                            dve.scalar_tensor_tensor(y[:, :, 1:S], t[:, :, 0:S - 1], vcol("ffn_w", tile + 44), y[:, :, 1:S],
                                                     ALU.mult, ALU.add).then_inc(s_ffn["tap"], 1)
                            dve.wait_ge(s_ffn["tap"], done + 1)
                            dve.scalar_tensor_tensor(y[:, :, 2:S], t[:, :, 0:S - 2], vcol("ffn_w", tile), y[:, :, 2:S],
                                                     ALU.mult, ALU.add).then_inc(s_ffn["conv"], 1)
                        dve.wait_ge(s_ffn["gelu"], m + (base + 1))
                        dve.wait_ge(s_ffn["conv"], m * 2 + (2 * base + 2))
                        dve.tensor_tensor(u4[:, 3:4, :], u4[:, 2:3, :], u4[:, 1:2, :], ALU.mult).then_inc(s_ffn["h"], 1)
                        dve.wait_ge(s_ffn["hhi"], m + (base + 1))
                        low(h_lo[:, p % 2, ds(m, 1), :], u4[:, 3:4, :], h_hi[:, p % 2, ds(m, 1), :], s_ffn["hlo"])
                        dve.wait_ge(s_ffn["hlo"], m + (base + 1))
                elif p < len(FF1_PARTS) - 1:
                    units(u0, DC, lambda m, j, u, slot: add_to(X, m, u, slot))
                else:
                    norm_start(3)
                    units(u0, DC, into_norm(X, 3, 2, "g_ple"))

            def p_low(n):
                dve.wait_ge(s_ple["phi"], n + 1)
                low(p_lo[:], p_raw[:], p_hi[:], s_ple["plo"])

            def ple_gate(n, norm_n, dst, last):
                dve.wait_ge(s_ple["e"], DC * (n + 1))
                dve.memset(token[:, 10 + n:11 + n], 0.0).then_inc(bank_free, 2)
                norm_inverse(norm_n)
                norm_start(norm_n + 1)
                dve.wait_ge(r_done, norm_n)

                def body(m, j, u, slot):
                    scaled(u, slot, T[:, j:j + 1, :])
                    dve.wait_ge(s_ple["sig"], m + (DC * n + 1))
                    if dst is X:
                        dve.tensor_tensor(T[:, j:j + 1, :], E[:, ds(m, 1), :], T2[:, j:j + 1, :], ALU.mult).then_inc(s_ple["g"], 1)
                        dve.wait_ge(s_ple["g"], m + 1)
                        dve.tensor_tensor(X[:, ds(m, 1), :], X[:, ds(m, 1), :], T[:, j:j + 1, :], ALU.add).then_inc(s_ple["x"], 1)
                    else:
                        dve.tensor_tensor(M[:, ds(m, 1), :], E[:, ds(m, 1), :], T2[:, j:j + 1, :], ALU.mult).then_inc(s_ple["x"], 1)
                    add_square(norm_n + 1, m, j)

                units(U[f"ple{n}"] + 2, DC, body)

            p_low(0)
            ple_gate(0, 3, X, False)
            norm_inverse(4)
            norm_start(5)
            dve.wait_ge(r_done, 4)
            with dve.Fori(0, DC // 2) as i:
                for j in range(2):
                    m = i * 2 + j
                    dve.scalar_tensor_tensor(X[:, ds(m, 1), :], X[:, ds(m, 1), :], vcol("g_final", m), R[:],
                                             ALU.mult, ALU.mult).then_inc(final_x, 1)
                    add_square(5, m, j)
                    prep_low(3, m, norm2_col(0, 0, m))
            norm_inverse(5)
            dve.wait_ge(r_done, 5)

            uu = U["forget"]
            dve.wait_ge(unit_done, uu + 1)
            f0, f1, f2, f3 = (logf[:, n, :] for n in range(4))
            dve.tensor_tensor(f0, ps[:, uu % 2, :], R[:, 0, :], ALU.mult).then_inc(bank_free, 1)
            dve.memset(f3, 1.0).then_inc(s_fg["dve"], 1)
            dve.wait_ge(bank_free, uu + 1 + CREDIT)
            dve.tensor_scalar(f1, f0, vec[:, VEC["b_forget"]:VEC["b_forget"] + 1], 0.0, ALU.add, ALU.min).then_inc(s_fg["dve"], 1)
            dve.wait_ge(s_fg["act"], 3)
            dve.wait_ge(s_fg["dve"], 2)
            dve.tensor_tensor(f0, f2, f1, ALU.subtract).then_inc(s_fg["dve"], 1)
            dve.wait_ge(s_fg["dve"], 3)
            dve.tensor_tensor_scan(c_rows[:], f3, f0, 0.0, ALU.mult, ALU.add).then_inc(s_fg["dve"], 1)
            dve.wait_ge(s_fg["act"], 4)
            dve.wait_ge(s_fg["dve"], 4)
            low(c_rows[32:64, :], c_rows[32:64, :], c_hi[32:64, :], s_fg["dve"])
            dve.wait_ge(s_fg["dve"], 5)

            u0 = U["fox"]

            def fox_qk(which, p, par, u):
                slot = (u0 + 3 * par + which) % 2
                scaled(u, slot, T[:, which:which + 1, :])
                dve.wait_ge(A2["qkhi"], p * 2 + (which + 1))
                if which == 0:
                    low_q(A2, fq_lo[:, par, :], T[:, 0, :], fq_hi[:, par, :], A2["qklo"])
                else:
                    low(fk_lo[:, par, :], T[:, 1, :], fk_hi[:, par, :], A2["qklo"])

            def fox_v(p, par, u):
                slot = (u0 + 3 * par + 2) % 2
                dve.wait_ge(unit_done, u + 1)
                dve.tensor_tensor(fv[:], ps[:, slot:slot + 1, :], R[:], ALU.mult).then_inc(A2["vs"], 1)

            def fox_v_low(p, par):
                slot = (u0 + 3 * par + 2) % 2
                dve.wait_ge(A2["vhi"], p + 1)
                low(fv_lo[:, par], ps[:, slot, :].rearrange("p (a b) -> p a b", b=P), fv_hi[:, par], bank_free)

            def head_rows(h, hd):
                dve.tensor_scalar(c_head[:, hd:hd + 1, :], c_rows[:].unsqueeze(1), head_sel[:, ds(h, 1)], None,
                                  ALU.mult).then_inc(A2["crow"], 1)

            head_rows(0, 0); head_rows(1, 1)
            fox_qk(0, 0, 0, u0)
            fox_qk(1, 0, 0, u0 + 1)
            fox_v(0, 0, u0 + 2)
            fox_v_low(0, 0)

            def fox_pair(p, par, more):
                nxt, npar = p + 1, 1 - par
                e0, n0 = p * 8, p * 2

                def mx(hd, qi):
                    peak(A2, e0 + (4 * hd + qi), hd, fstat, qi, 2 + qi % 2)

                def nrm(hd, qi):
                    normalise(A2, e0 + (4 * hd + qi), n0 + hd, hd, fstat, fprob[:, hd, :], qi)

                def lo(hd, kb):
                    split_turned(A2, e0 + (4 * hd + kb), kb % 2, (fpt_hi, fpt_lo), kb)

                def out_low(hd):
                    rows = slice(hd * HD, (hd + 1) * HD)
                    dve.wait_ge(A2["ohi"], n0 + (hd + 1))
                    low(fo_lo[rows, ds(p, 1), :], ps[rows, 6 + hd:7 + hd, :], fo_hi[rows, ds(p, 1), :], A2["olo"])

                mx(0, 0); mx(0, 1); nrm(0, 0); nrm(0, 1)
                if more:
                    fox_qk(0, nxt, npar, p * 3 + (u0 + 3))
                mx(0, 2); mx(0, 3); nrm(0, 2); nrm(0, 3); mx(1, 0); mx(1, 1)
                if more:
                    fox_qk(1, nxt, npar, p * 3 + (u0 + 4))
                lo(0, 0); nrm(1, 0); lo(0, 1); nrm(1, 1); mx(1, 2); lo(0, 2); nrm(1, 2); mx(1, 3); lo(0, 3); nrm(1, 3)
                out_low(0); lo(1, 0); lo(1, 1)
                if more:
                    fox_v(nxt, npar, p * 3 + (u0 + 5))
                lo(1, 2)
                if more:
                    head_rows(n0 + 2, 0); head_rows(n0 + 3, 1); fox_v_low(nxt, npar)
                lo(1, 3); out_low(1)

            with dve.Fori(0, 3) as i:
                for par in range(2):
                    fox_pair(i * 2 + par, par, True)
            fox_pair(6, 0, True)
            fox_pair(7, 1, False)

            def branch_out(u0, n):
                norm_start(n)

                def body(m, j, u, slot):
                    dve.wait_ge(unit_done, u + 1)
                    dve.tensor_copy(M[:, ds(m, 1), :], ps[:, slot:slot + 1, :]).then_inc(bank_free, 1)
                    add_square(n, m, j)
                units(u0, DC, body)

            def post(k, n, layer, which, prep=None):
                norm_inverse(n)
                if prep is not None:
                    norm_start(n + 1)
                dve.wait_ge(r_done, n)
                with dve.Fori(0, DC // 2) as i:
                    for j in range(2):
                        m = i * 2 + j
                        dve.scalar_tensor_tensor(T[:, j:j + 1, :], M[:, ds(m, 1), :], norm2_col(layer, which, m), R[:],
                                                 ALU.mult, ALU.mult).then_inc(post_t, 1)
                        dve.wait_ge(post_t, m + (DC * k + 1))
                        dve.tensor_tensor(X[:, ds(m, 1), :], X[:, ds(m, 1), :], T[:, j:j + 1, :], ALU.add).then_inc(post_x, 1)
                        if prep is not None:
                            add_square(n + 1, m, j)
                            prep_low(prep[0], m, norm2_col(prep[1], prep[2], m))
                if prep is not None:
                    norm_inverse(n + 1) if prep[0] not in (5, 8) else None
                    dve.wait_ge(r_done, n + 1) if prep[0] not in (5, 8) else None

            def mlp(k):
                for kind, p in ffn_order(len(FF2_PARTS)):
                    u0 = U[f"mlp{k + 1}_{kind}{p}"]
                    if kind == "up":
                        def body(m, j, u, slot, base=32 * k + 8 * p, p=p):
                            t, s = T[:, j:j + 1, :], T2[:, j:j + 1, :]
                            scaled(u, slot, t)
                            dve.wait_ge(bank_free, u + (1 + CREDIT))
                            dve.scalar_tensor_tensor(s, t, 0.0, t, ALU.max, ALU.mult).then_inc(s_mlp["s"], 1)
                            dve.wait_ge(s_mlp["hi"], m + (base + 1))
                            low(h_lo[:, p % 2, ds(m, 1), :], s, h_hi[:, p % 2, ds(m, 1), :], s_mlp["lo"])
                            dve.wait_ge(s_mlp["lo"], m + (base + 1))
                        units(u0, DC, body)
                    elif p == 0:
                        def body(m, j, u, slot):
                            dve.wait_ge(unit_done, u + 1)
                            dve.tensor_copy(M[:, ds(m, 1), :], ps[:, slot:slot + 1, :]).then_inc(bank_free, 1)
                        units(u0, DC, body)
                    elif p < len(FF2_PARTS) - 1:
                        units(u0, DC, lambda m, j, u, slot: add_to(M, m, u, slot))
                    else:
                        norm_start(8 + 6 * k)
                        units(u0, DC, into_norm(M, 8 + 6 * k))

            branch_out(U["fox_out"], 6)
            post(0, 6, 0, 1, (4, 0, 2))
            mlp(0)
            p_low(1)
            post(1, 8, 0, 3, (5, 0, 4))
            ple_gate(1, 9, M, False)
            post(2, 10, 0, 5, (6, 1, 0))
            u0 = U["conv3"]
            with dve.Fori(0, DC // 2) as i:
                for jm in range(2):
                    m = i * 2 + jm
                    for j in range(3):
                        n = 3 * jm + j
                        scaled(i * 6 + (u0 + n), (u0 + n) % 2, c3t[:, j:j + 1, :])
                    dve.wait_ge(bank_free, i * 6 + (u0 + 3 * jm + 3 + CREDIT))
                    z, y = c3t[:, 3:4, :], c3t[:, 4:5, :]
                    dve.tensor_tensor(z, c3t[:, 1:2, :], c3t[:, 2:3, :], ALU.mult).then_inc(s_c3["zz"], 1)
                    dve.wait_ge(s_c3["z2"], m + 1)
                    dve.scalar_tensor_tensor(y[:, :, 1:S], z[:, :, 0:S - 1], vcol("conv3_w", m + DC), y[:, :, 1:S],
                                             ALU.mult, ALU.add).then_inc(s_c3["tap"], 1)
                    dve.wait_ge(s_c3["tap"], m * 2 + 1)
                    dve.scalar_tensor_tensor(y[:, :, 2:S], z[:, :, 0:S - 2], vcol("conv3_w", m), y[:, :, 2:S],
                                             ALU.mult, ALU.add).then_inc(s_c3["tap"], 1)
                    dve.wait_ge(s_c3["tap"], m * 2 + 2)
                    dve.tensor_tensor(c3t[:, 1:2, :], c3t[:, 0:1, :], y, ALU.mult).then_inc(s_c3["y"], 1)
                    dve.wait_ge(s_c3["hi"], m + 1)
                    low(cy_lo[:, ds(m, 1), :], c3t[:, 1:2, :], cy_hi[:, ds(m, 1), :], s_c3["lo"])
                    dve.wait_ge(s_c3["lo"], m + 1)
            branch_out(U["conv3_out"], 12)
            post(3, 12, 1, 1, (7, 1, 2))
            mlp(1)
            p_low(2)
            post(4, 14, 1, 3, (8, 1, 4))
            ple_gate(2, 15, M, True)
            post(5, 16, 1, 5)

        @block.scalar
        def _(act):
            def copy_hi(out, x, done, scale=1.0):
                act.activation(out, x, ACT.Copy, scale=scale).then_inc(done, 1)

            def units(u0, n, body, per=2):
                with act.Fori(0, n // per) as i:
                    for j in range(per):
                        body(i * per + j, j, i * per + (u0 + j), (u0 + j) % 2)

            def taken(u):
                act.wait_ge(bank_free, u + (1 + CREDIT))

            def square(n, src, m, j):
                act.wait_ge(summed, m + (10 * (n - 1) + 1))
                act.activation(sq[:, j:j + 1, :], src[:, ds(m, 1), :], ACT.Square).then_inc(squared, 1)

            def prep_high(m, g):
                act.activation(xg_hi[:, ds(m, 1), :], X[:, ds(m, 1), :], ACT.Copy, scale=g).then_inc(prep_hi, 1)

            def norm_root(n):
                act.wait_ge(ssq_done, n)
                act.activation(rms_c[:, 0, :], ps[:, 7, 0:QB], ACT.Sqrt, bias=eps_col[:]).then_inc(rms_done, 1)

            def norm_copy(n):
                act.wait_ge(bcast_done, n)
                act.activation(R[:, 0, :], ps[:, 7, :], ACT.Copy).then_inc(r_done, 1)

            def norm(n):
                norm_root(n)
                norm_copy(n)

            act.wait_ge(vec_loaded, 16)
            act.wait_ge(x_loaded, 32)
            act.wait_ge(c_dve, 4)
            for j in range(2):
                square(1, X, j, j)
                prep_high(j, vcol("g_mix", j))
            with act.Fori(1, DC // 2) as i:
                for j in range(2):
                    square(1, X, i * 2 + j, j)
                    prep_high(i * 2 + j, vcol("g_mix", i * 2 + j))
            act.wait_ge(c_pool, 11)
            act.activation(ident_r[:], ident[:], ACT.Copy).then_inc(c_act, 1)
            act.activation(causal_r[:], causal[:], ACT.Copy).then_inc(c_act, 1)
            act.activation(cmp_mask_r[:], cmask[:], ACT.Copy).then_inc(c_act, 1)
            act.activation(ones_r[:], ones[:], ACT.Copy).then_inc(c_act, 1)
            norm(1)
            u0 = U["glu"]
            with act.Fori(0, CT) as i:
                taken(i * 2 + (u0 + 1))
                act.activation(T2[:, 0:1, :], T[:, 1:2, :], ACT.Sigmoid).then_inc(s_glu["sig"], 1)
            for kv in range(2):
                act.wait_ge(s_cmp["blk"], 4 * (kv + 1))
                copy_hi(blk_hi[:, kv], blk[:, kv], s_cmp["hi"])
            for kv in range(2):
                act.wait_ge(unit_done, U["cmp_hidden"] + 4 * (kv + 1))
                for half in range(2):
                    act.activation(hid[:, kv, half, :], ps[:, 2 + 2 * kv + half, 0:2 * NC1], ACT.Gelu_apprx_tanh).then_inc(s_cmp["gelu"], 1)
                act.wait_ge(s_cmp["gelu"], 2 * (kv + 1))
                copy_hi(hid_hi[:, kv], hid[:, kv], s_cmp["ghi"])
            act.wait_ge(s_cmp["out"], 4)
            copy_hi(kc_hi[:], kc_f[:], s_cmp["khi"])
            copy_hi(vc_hi[:], vc_f[:], s_cmp["khi"])
            for j in range(2):
                taken(U["keys"] + j)
                copy_hi(kk_hi[:, j, :], T[:, j, :], s_kv["hi"])
            taken(U["gates"])
            act.activation(sq[:, 0, :], T[:, 0, :], ACT.Sigmoid).then_inc(s_gate["sig"], 1)
            for j in range(2):
                act.wait_ge(s_kv["turned"], j + 1)
                copy_hi(vv_hi[:, j], ps[:, 2 + j, :].rearrange("p (a b) -> p a b", b=P), s_kv["hi"])

            def exps(A, e, par, st, pr, qi, b):
                act.wait_ge(A["peak"], e + 1)
                act.activation(pr[:, P_OFF[qi]:P_OFF[qi] + (qi + 1) * P], ps[:, b, 0:(qi + 1) * P], ACT.Exp,
                               bias=st[:, 0, par, qi:qi + 1], accum_out=st[:, 1, par, qi:qi + 1]).then_inc(A["exps"], 1)

            def turned_hi(A, e, b, pt, kb):
                act.wait_ge(A["turned"], e + 1)
                copy_hi(pt[:, b, kb * P:S], ps[:, 4 + b, kb * P:S], A["hi"])

            def nsa_q(p):
                taken(pair_units(p - 1)[4] if p else U["q0"])
                copy_hi(q_hi[:, p % 2, :], T[:, p % 2, :], A1["qhi"], HD ** -0.5)

            nsa_q(0)
            for p in range(4):
                e0 = 18 * p

                def cmp_exps(hd):
                    e = e0 + 9 * hd
                    act.wait_ge(A1["peak"], e + 1)
                    act.activation(prob_c[:, hd], prob_c[:, hd], ACT.Exp).then_inc(A1["exps"], 1)

                def cmp_hi(hd):
                    e = e0 + 9 * hd
                    act.wait_ge(A1["turned"], e + 1)
                    copy_hi(pt_hi[0:NCP, e % 2, :], ps[0:NCP, 4 + e % 2, :], A1["hi"])

                def where(f):
                    return e0 + 9 * (f // 2) + 1 + 4 * (f % 2), 4 * p + f

                def ex(f, qi):
                    e, n = where(f)
                    exps(A1, e + qi, n % 2, stat, prob[:, n % 2, :], qi, 2 + (e + qi) % 2)

                def hi(f, kb):
                    e = where(f)[0] + kb
                    turned_hi(A1, e, e % 2, pt_hi, kb)

                def out_hi(hd):
                    rows = slice(hd * HD, (hd + 1) * HD)
                    act.wait_ge(A1["pv"], e0 + 9 * (hd + 1))
                    copy_hi(o_hi[rows, p, :], ps[rows, 6 + hd, :], A1["ohi"])

                def two_steps(new, old, q=False):
                    ex(new, 0); ex(new, 1); hi(old, 0); hi(old, 1); ex(new, 2); hi(old, 2); ex(new, 3)
                    if q:
                        nsa_q(p + 1)
                    hi(old, 3)

                cmp_exps(0); ex(0, 0); cmp_hi(0); ex(0, 1); ex(0, 2); ex(0, 3)
                two_steps(1, 0)
                cmp_exps(1)
                two_steps(2, 1, p < 3)
                out_hi(0); cmp_hi(1)
                two_steps(3, 2)
                for kb in range(QB):
                    hi(3, kb)
                out_hi(1)

            def merge_sigmoid(m):
                tiles = merge[:, m:m + 4, :]
                act.activation(tiles, tiles, ACT.Sigmoid).then_inc(s_mrg["sig"], 1)

            taken(pair_units(3)[2])
            merge_sigmoid(0)
            merge_sigmoid(DC)
            for ct in range(CT):
                act.wait_ge(s_ln["cent"], ct + 1)
                if ct >= 2:
                    act.wait_ge(s_ln["acc"], ct - 1)
                act.activation(sq[:, ct % 2, :], conv_acc[:, ct, :], ACT.Square).then_inc(s_ln["sq"], 1)
            act.wait_ge(s_ln["var"], 1)
            act.activation(rms_c[:, 0, :], ps[:, 5, 0:QB], ACT.Sqrt, bias=eps_col[:]).then_inc(s_ln["sd"], 1)
            act.wait_ge(s_ln["bc"], 1)
            act.activation(R[:, 0, :], ps[:, 5, :], ACT.Copy).then_inc(s_ln["r"], 1)
            for ct in range(CT):
                act.wait_ge(s_ln["n"], ct + 1)
                act.activation(conv_acc[:, ct, :], T2[:, ct % 2, :], ACT.Silu, bias=vcol("ln_b", ct), scale=vcol("ln_g", ct)).then_inc(s_ln["act"], 1)
                act.wait_ge(s_ln["act"], ct + 1)
                copy_hi(xg_hi[:, ct, :], conv_acc[:, ct, :], s_ln["hi"])

            merge_sigmoid(4)
            taken(pair_units(3)[3])
            merge_sigmoid(DC + 4)

            def mix(m, j, u, slot):
                act.wait_ge(s_mix["y"], m + 1)
                copy_hi(y_hi[:, ds(m, 1), :], T[:, j:j + 1, :], s_mix["hi"])

            units(U["mix"], DC, mix)

            def into_norm(src, n, gain=None):
                def body(m, j, u, slot):
                    taken(u)
                    square(n, src, m, j)
                    if gain is not None:
                        prep_high(m, vcol(gain, m))
                return body

            units(U["w_out"], DC, into_norm(X, 2, "g_ffn"))
            norm(2)
            act.dma_start(p_raw[:], p_in[0]).then_inc(p_loaded, 16)

            for kind, p in ffn_order(len(FF1_PARTS)):
                u0 = U[f"ffn_{kind}{p}"]
                base = sum(FF1_PARTS[:p])
                if kind == "up":
                    with act.Fori(0, FF1_PARTS[p]) as m:
                        for j in range(2):
                            taken(m * 2 + (u0 + j))
                            tile = m + (base + 22 * j)
                            act.activation(u4[:, j:j + 1, :], T[:, j:j + 1, :], ACT.Identity, bias=vcol("ffn_b", tile),
                                           scale=vcol("ffn_w", tile + 88)).then_inc(s_ffn["t2"], 1)
                        act.wait_ge(s_ffn["conv"], m * 2 + (2 * base + 1))
                        act.activation(u4[:, 2:3, :], u4[:, 0:1, :], ACT.Gelu_apprx_tanh).then_inc(s_ffn["gelu"], 1)
                        act.wait_ge(s_ffn["h"], m + (base + 1))
                        copy_hi(h_hi[:, p % 2, ds(m, 1), :], u4[:, 3:4, :], s_ffn["hhi"])
                elif p == len(FF1_PARTS) - 1:
                    units(u0, DC, into_norm(X, 3, "g_ple"))

            def p_high(n):
                act.wait_ge(p_loaded, 16 * (n + 1))
                copy_hi(p_hi[:], p_raw[:], s_ple["phi"])

            def p_next(n):
                act.wait_ge(s_ple["plo"], n)
                act.dma_start(p_raw[:], p_in[n]).then_inc(p_loaded, 16)

            def embed_tile(n, t):
                if t % 4 < 3:
                    act.wait_ge(s_ple["epe"], 6 * n + 3 * (t // 4) + t % 4 + 1)
                else:
                    act.wait_ge(unit_done, U[f"ple{n}"] + t // 4 + 1)
                act.activation(E[:, t, :], ps[:, 2 + t % 4, :], ACT.Copy).then_inc(s_ple["e"], 1)

            def ple_gate(n, norm_n, src, x_base):
                norm(norm_n)

                def body(m, j, u, slot):
                    taken(u)
                    act.activation(T2[:, j:j + 1, :], T[:, j:j + 1, :], ACT.Sigmoid).then_inc(s_ple["sig"], 1)
                    act.wait_ge(s_ple["x"], m + (DC * n + 1))
                    square(norm_n + 1, src, m, j)

                units(U[f"ple{n}"] + 2, DC, body)

            p_high(0)
            for t in range(DC):
                embed_tile(0, t)
            ple_gate(0, 3, X, 0)
            norm(4)
            with act.Fori(0, DC // 2) as i:
                for j in range(2):
                    m = i * 2 + j
                    act.wait_ge(final_x, m + 1)
                    square(5, X, m, j)
                    prep_high(m, norm2_col(0, 0, m))
            norm(5)

            taken(U["forget"])
            f0, f1, f2, f3 = (logf[:, n, :] for n in range(4))
            act.activation(f2, f0, ACT.Abs, bias=vec[:, VEC["b_forget"]:VEC["b_forget"] + 1]).then_inc(s_fg["act"], 1)
            act.wait_ge(s_fg["act"], 1)
            act.activation(f2, f2, ACT.Exp, scale=-1.0).then_inc(s_fg["act"], 1)
            act.wait_ge(s_fg["act"], 2)
            act.activation(f2, f2, ACT.Ln, bias=ones[:, 0:1]).then_inc(s_fg["act"], 1)
            act.wait_ge(s_fg["dve"], 4)
            act.activation(c_hi[:], c_rows[:], ACT.Copy).then_inc(s_fg["act"], 1)

            u0 = U["fox"]

            def fox_qk(which, p, par, u):
                taken(u)
                if which == 0:
                    copy_hi(fq_hi[:, par, :], T[:, 0, :], A2["qkhi"], HD ** -0.5)
                else:
                    copy_hi(fk_hi[:, par, :], T[:, 1, :], A2["qkhi"])

            def fox_v_high(p, par):
                slot = (u0 + 3 * par + 2) % 2
                act.wait_ge(A2["vturned"], p + 1)
                copy_hi(fv_hi[:, par], ps[:, slot, :].rearrange("p (a b) -> p a b", b=P), A2["vhi"])

            fox_qk(0, 0, 0, u0)
            fox_qk(1, 0, 0, u0 + 1)
            fox_v_high(0, 0)

            def fox_pair(p, par, more):
                nxt, npar = p + 1, 1 - par
                e0 = p * 8

                def ex(hd, qi):
                    exps(A2, e0 + (4 * hd + qi), hd, fstat, fprob[:, hd, :], qi, 2 + qi % 2)

                def hi(hd, kb):
                    turned_hi(A2, e0 + (4 * hd + kb), kb % 2, fpt_hi, kb)

                def out_hi(hd):
                    rows = slice(hd * HD, (hd + 1) * HD)
                    act.wait_ge(A2["pv"], e0 + 4 * (hd + 1))
                    copy_hi(fo_hi[rows, ds(p, 1), :], ps[rows, 6 + hd:7 + hd, :], A2["ohi"])

                ex(0, 0); ex(0, 1)
                if more:
                    fox_qk(0, nxt, npar, p * 3 + (u0 + 3))
                ex(0, 2); ex(0, 3); ex(1, 0); ex(1, 1)
                if more:
                    fox_qk(1, nxt, npar, p * 3 + (u0 + 4))
                hi(0, 0); hi(0, 1); ex(1, 2); hi(0, 2); ex(1, 3); hi(0, 3); out_hi(0)
                hi(1, 0); hi(1, 1); hi(1, 2)
                if more:
                    fox_v_high(nxt, npar)
                hi(1, 3); out_hi(1)

            with act.Fori(0, 3) as i:
                for par in range(2):
                    fox_pair(i * 2 + par, par, True)
            fox_pair(6, 0, True)
            fox_pair(7, 1, False)

            def post(k, n, prep=None, embed=None):
                norm(n)
                if embed is not None:
                    for m in range(DC):
                        act.wait_ge(post_x, DC * k + m + 1)
                        square(n + 1, X, m, m % 2)
                        prep_high(m, norm2_col(prep[1], prep[2], m))
                        embed_tile(embed, m)
                elif prep is not None:
                    with act.Fori(0, DC // 2) as i:
                        for j in range(2):
                            m = i * 2 + j
                            act.wait_ge(post_x, m + (DC * k + 1))
                            square(n + 1, X, m, j)
                            prep_high(m, norm2_col(prep[1], prep[2], m))
                    norm(n + 1)

            def mlp(k):
                for kind, p in ffn_order(len(FF2_PARTS)):
                    u0 = U[f"mlp{k + 1}_{kind}{p}"]
                    if kind == "up":
                        def body(m, j, u, slot, base=32 * k + 8 * p, p=p):
                            act.wait_ge(s_mlp["s"], m + (base + 1))
                            copy_hi(h_hi[:, p % 2, ds(m, 1), :], T2[:, j:j + 1, :], s_mlp["hi"])
                        units(u0, DC, body)
                    elif p == len(FF2_PARTS) - 1:
                        units(u0, DC, into_norm(M, 8 + 6 * k))

            units(U["fox_out"], DC, into_norm(M, 6))
            p_next(1)
            post(0, 6, (4, 0, 2))
            mlp(0)
            p_high(1)
            post(1, 8, (5, 0, 4), embed=1)
            p_next(2)
            ple_gate(1, 9, M, 1)
            post(2, 10, (6, 1, 0))
            with act.Fori(0, DC // 2) as i:
                for j in range(2):
                    m = i * 2 + j
                    act.wait_ge(s_c3["zz"], m + 1)
                    act.activation(c3t[:, 4:5, :], c3t[:, 3:4, :], ACT.Copy, scale=vcol("conv3_w", m + 2 * DC)).then_inc(s_c3["z2"], 1)
                    act.wait_ge(s_c3["y"], m + 1)
                    copy_hi(cy_hi[:, ds(m, 1), :], c3t[:, 1:2, :], s_c3["hi"])
            units(U["conv3_out"], DC, into_norm(M, 12))
            post(3, 12, (7, 1, 2))
            mlp(1)
            p_high(2)
            post(4, 14, (8, 1, 4), embed=2)
            ple_gate(2, 15, M, 2)
            post(5, 16)


def _pack(w, rows=None, cols=None):
    w = w if cols is None else w[:, cols]
    k, n = w.shape
    return w.reshape(k // P, P, n // P, P).transpose(2, 1, 0, 3).reshape(n // P, P, k)


def _full(t):
    return np.concatenate([t, np.zeros((*t.shape[:-1], UW - t.shape[-1]), t.dtype)], -1) if t.shape[-1] < UW else t


def _weights(a):
    U = layout_units()
    f = np.float32
    w_in = a["w_in"][0]
    nq, kv0 = 512, 512
    gates0, conv0 = kv0 + 768, kv0 + 768 + 24
    merge0 = conv0 + 1024
    out = []

    def add(stage, t):
        assert len(out) == U[stage], stage
        out.extend(_full(t))

    def inter(*ts):
        return np.stack(ts, 1).reshape(-1, *ts[0].shape[1:])

    add("glu", inter(_pack(w_in[:, conv0:conv0 + 512]), _pack(w_in[:, conv0 + 512:conv0 + 1024])))
    dup = [w_in[:, kv0 + i * P + g * HD:kv0 + i * P + (g + 1) * HD] for i in range(2) for g in range(2)]
    add("cmp_in", np.concatenate([_pack(np.concatenate([d, d], 1)) for d in dup]))
    hidden = [a[n][0].reshape(4, 4, P, 256).transpose(0, 2, 1, 3).reshape(4, P, UW) for n in ("w_cmp_k1", "w_cmp_v1")]
    add("cmp_hidden", np.concatenate(hidden))
    k2, v2 = a["w_cmp_k2"][0], a["w_cmp_v2"][0]
    add("cmp_out", np.concatenate([_pack(np.concatenate([k2, k2], 1)), v2.reshape(2, P, HD).transpose(1, 0, 2).reshape(1, P, P)], -1))
    kv = lambda i: w_in[:, kv0 + i * P:kv0 + (i + 1) * P]
    add("keys", np.concatenate([_pack(kv(2)), _pack(kv(4))]))
    add("values", np.concatenate([_pack(kv(3)), _pack(kv(5))]))
    gate = np.zeros((D, P), f)
    gate[:, :24] = w_in[:, gates0:gates0 + 24]
    add("gates", _pack(gate))
    heads = np.concatenate([np.arange(g * 256 + p * HD, g * 256 + (p + 1) * HD) for p in range(4) for g in range(2)])
    q, merge = _pack(w_in[:, heads]), _pack(w_in[:, merge0:])
    add("q0", q[:1])
    add("pairs", np.concatenate([np.stack([merge[4 * p], merge[4 * p + 1], *q[p + 1:p + 2], merge[4 * p + 2], merge[4 * p + 3]])
                                 for p in range(4)]))
    add("mix", np.concatenate([_pack(a["w_o_nsa"][0][heads]), _pack(a["w_conv_out"][0])], -1))
    add("w_out", _pack(a["w_out"][0]))
    up, down = a["w_up"][0], a["w_down"][0]
    for kind, p in ffn_order(len(FF1_PARTS)):
        r = slice(P * sum(FF1_PARTS[:p]), P * sum(FF1_PARTS[:p + 1]))
        add(f"ffn_{kind}{p}", inter(_pack(up[:, :22 * P][:, r]), _pack(up[:, 22 * P:][:, r])) if kind == "up" else _pack(down[r]))

    def embed(w):
        return _pack(w).reshape(2, 4, P, 256).transpose(0, 2, 1, 3).reshape(2, P, UW)

    add("ple0", np.concatenate([embed(a["w_ple"][0]), _pack(a["w_ple_gate"][0])]))
    w = a["w_attn_in_2"][0]
    gate = np.zeros((D, P), f)
    gate[:, 0:16] = gate[:, 32:48] = w[:, 3 * D:]
    add("forget", _pack(gate))
    add("fox", inter(_pack(w[:, :D]), _pack(w[:, D:2 * D]), _pack(w[:, 2 * D:3 * D])))
    add("fox_out", _pack(a["w_attn_out_2"][0]))
    for n in (1, 2):
        if n == 2:
            w = a["w_conv_in_2"][0]
            add("conv3", inter(_pack(w[:, :D]), _pack(w[:, D:2 * D]), _pack(w[:, 2 * D:])))
            add("conv3_out", _pack(a["w_conv_out_2"][0]))
        for kind, p in ffn_order(len(FF2_PARTS)):
            r = slice(p * D, (p + 1) * D)
            add(f"mlp{n}_{kind}{p}", _pack(a["w_mlp_up_2"][n - 1][:, r]) if kind == "up" else _pack(a["w_mlp_down_2"][n - 1][r]))
        add(f"ple{n}", np.concatenate([embed(a["w_ple_proj_2"][n - 1]), _pack(a["w_ple_gate_2"][n - 1])]))
    assert len(out) == U["end"]
    return np.ascontiguousarray(np.stack(out))


def _vectors(a):
    v = np.zeros((P, NVEC), np.float32)

    def put(name, cols):
        v[:cols.shape[0], VEC[name]:VEC[name] + cols.shape[1]] = cols

    def tiles(x):
        return x.reshape(-1, P).T

    for name, key in (("g_mix", "g_mix"), ("g_ffn", "g_ffn"), ("g_ple", "g_ple"), ("g_final", "g_final"), ("norm2", "norm_g_2"),
                      ("conv_b", "conv_b"), ("ln_g", "conv_ln_g"), ("ln_b", "conv_ln_b"), ("b_conv_out", "b_conv_out"),
                      ("ffn_w", "ffn_conv_w"), ("ffn_b", "ffn_conv_b"), ("conv3_w", "conv_w_2")):
        put(name, tiles(a[key]))
    put("conv_w", a["conv_w"][0].reshape(CONV_TAPS, CT, P).transpose(2, 1, 0).reshape(P, -1))
    b = np.zeros((P, 1), np.float32)
    b[0:16, 0] = b[32:48, 0] = a["b_forget_2"][0]
    put("b_forget", b)
    put("pos_k", a["cmp_pos_k"][0].reshape(16, P).T)
    put("pos_v", a["cmp_pos_v"][0].reshape(16, P).T)
    return v


def kernel(**inputs):
    import concourse.bacc as bacc
    from concourse.bass_utils import run_bass_kernel_spmd

    a = {k: np.asarray(v) for k, v in inputs.items()}

    def feature_tiles(x):
        return np.ascontiguousarray(x.T.reshape(-1, P, S).transpose(1, 0, 2))

    arrays = {
        "in_x": feature_tiles(a["x"][0]),
        "in_p": np.stack([feature_tiles(t) for t in (a["p"][0, 0], a["p_2"][0, 0], a["p_2"][1, 0])]),
        "in_weights": _weights(a),
        "in_vectors": _vectors(a),
    }
    nc = bacc.Bacc("TRN2", target_bir_lowering=False, num_devices=1)
    args = [nc.dram_tensor(n, v.shape, F32, kind="ExternalInput").ap() for n, v in arrays.items()]
    out = nc.dram_tensor("out_x", (P, DC, S), F32, kind="ExternalOutput").ap()
    build(nc, *args, out)
    r = run_bass_kernel_spmd(nc, [arrays], core_ids=[0])
    got = r.results[0]["out_x"]
    return np.ascontiguousarray(got.transpose(2, 1, 0).reshape(1, S, D))
```

```python
from contextlib import ExitStack

import numpy as np

import concourse.bass as bass
from concourse import mybir

P = 128
S = 512
D = 1024
DC = D // P
HD = 64
NEG = -1e30
EPS = 1e-6
RAW = 2
UW = 1024
CONV_TAPS = 31
PAD = CONV_TAPS - 1
CT = 4
NC1 = 31
NCP = 32
FF1_PARTS = (8, 8, 6)
FF2_PARTS = (8, 8, 8, 8)
QB = S // P
P_OFF = (0, 128, 384, 768)
CREDIT = 2
F32 = mybir.dt.float32
F32R = mybir.dt.float32r
ALU = mybir.AluOpType
ACT = mybir.ActivationFunctionType
AX = mybir.AxisListType
ds = bass.ds


def layout_units():
    u, at = 0, {}

    def stage(name, n):
        nonlocal u
        at[name] = u
        u += n

    stage("glu", 8)
    stage("cmp_in", 4)
    stage("cmp_hidden", 8)
    stage("keys", 2)
    stage("cmp_out", 1)
    stage("values", 2)
    stage("gates", 1)
    stage("q0", 1)
    stage("pairs", 19)
    stage("mix", 8)
    stage("w_out", 8)
    for kind, p in ffn_order(len(FF1_PARTS)):
        stage(f"ffn_{kind}{p}", 2 * FF1_PARTS[p] if kind == "up" else 8)
    stage("ple0", 10)
    stage("forget", 1)
    stage("fox", 24)
    stage("fox_out", 8)
    for kind, p in ffn_order(len(FF2_PARTS)):
        stage(f"mlp1_{kind}{p}", 8)
    stage("ple1", 10)
    stage("conv3", 24)
    stage("conv3_out", 8)
    for kind, p in ffn_order(len(FF2_PARTS)):
        stage(f"mlp2_{kind}{p}", 8)
    stage("ple2", 10)
    at["end"] = u
    return at


def pair_units(p):
    u0 = layout_units()["pairs"] + 5 * p
    return (u0, u0 + 1, u0 + 3, u0 + 4, u0 + 2) if p < 3 else (u0, u0 + 1, u0 + 2, u0 + 3, None)


def ffn_order(parts):
    order = [("up", 0)]
    for p in range(1, parts):
        order += [("up", p), ("down", p - 1)]
    return order + [("down", parts - 1)]


VEC = {}
_n = 0
for _name, _w in (("g_mix", 8), ("g_ffn", 8), ("g_ple", 8), ("g_final", 8), ("norm2", 96), ("conv_w", CT * CONV_TAPS),
                  ("conv_b", CT), ("ln_g", CT), ("ln_b", CT), ("b_conv_out", 8), ("ffn_w", 3 * 44), ("ffn_b", 44),
                  ("conv3_w", 24), ("b_forget", 1), ("pos_k", 16), ("pos_v", 16)):
    VEC[_name] = _n
    _n += _w
NVEC = _n


def build(nc, x_in, p_in, weights, vectors, out):
    U = layout_units()
    with ExitStack() as ctx:
        def sb(name, shape, dt=F32, scope=ctx):
            return scope.enter_context(nc.sbuf_tensor(name, shape, dt))

        def sem(name):
            return ctx.enter_context(nc.semaphore(name))

        w_raw = sb("w_raw", [P, RAW, UW])
        w_hi = sb("w_hi", [P, 2, UW], F32R)
        w_lo = sb("w_lo", [P, 2, UW], F32R)
        X = sb("resid", [P, DC, S])
        xg_hi = sb("xg_hi", [P, DC, S], F32R)
        xg_lo = sb("xg_lo", [P, DC, S], F32R)
        R = sb("inv_rms", [P, 1, S])
        sq = sb("sq", [P, 2, S])
        sq_sum = sb("sq_sum", [P, 1, S])
        T = sb("tile_a", [P, 2, S])
        T2 = sb("tile_b", [P, 2, S])
        vec = sb("vec", [P, NVEC])
        ident = sb("ident", [P, P])
        ident_r = sb("ident_r", [P, P], F32R)
        causal_r = sb("causal_r", [P, P], F32R)
        cmp_mask_r = sb("cmp_mask_r", [P, QB, NCP], F32R)
        valid = sb("valid", [P, QB, 1])
        ones = sb("ones", [P, P])
        ones_r = sb("ones_r", [P, P], F32R)
        mean_col = sb("mean_col", [P, 1])
        mean_ch = sb("mean_ch", [P, P])
        eps_col = sb("eps_col", [P, 1])
        one_col = sb("one_col", [P, 1])
        rms_c = sb("rms_c", [P, 2, QB])
        r_diag = sb("r_diag", [P, QB, P])
        token = sb("token", [P, 14])
        head_sel = sb("head_sel", [P, 16])

        m1 = ExitStack()
        conv_acc = sb("conv_acc", [P, CT, S], scope=m1)
        with ExitStack() as early:
            sb("before_glu", [P, S], scope=early)
            glu = sb("glu", [P, CT, PAD + S], scope=early)
        o_hi = sb("o_hi", [P, 4, S], F32R, m1)
        sb("end_of_glu", [P, S + CT * (PAD + S) - 4 * S], scope=m1)
        o_lo = sb("o_lo", [P, 4, S], F32R, m1)
        with ExitStack() as early:
            cmask = sb("cmask", [P, QB, NCP], scope=early)
            causal = sb("causal", [P, P], scope=early)
            hid = sb("hid", [2 * NC1, 2, 2 * P], scope=early)
            hid_hi = sb("hid_hi", [P, 2, 2, 2 * NC1], F32R, early)
            hid_lo = sb("hid_lo", [P, 2, 2, 2 * NC1], F32R, early)
            kv_dup = sb("kv_dup", [P, 4, S], scope=early)
            blk = sb("blk", [P, 2, 16, 2 * NC1], scope=early)
            blk_hi = sb("blk_hi", [P, 2, 16, 2 * NC1], F32R, early)
            blk_lo = sb("blk_lo", [P, 2, 16, 2 * NC1], F32R, early)
        merge = sb("merge", [P, 16, S], scope=m1)
        with ExitStack() as att:
            kk_hi = sb("kk_hi", [P, 2, S], F32R, att)
            kk_lo = sb("kk_lo", [P, 2, S], F32R, att)
            vv_hi = sb("vv_hi", [P, 2, QB, P], F32R, att)
            vv_lo = sb("vv_lo", [P, 2, QB, P], F32R, att)
            kc_f = sb("kc_f", [P, NCP], scope=att)
            kc_hi = sb("kc_hi", [P, NCP], F32R, att)
            kc_lo = sb("kc_lo", [P, NCP], F32R, att)
            vc_f = sb("vc_f", [NCP, P], scope=att)
            vc_hi = sb("vc_hi", [NCP, P], F32R, att)
            vc_lo = sb("vc_lo", [NCP, P], F32R, att)
            gates = sb("gates", [P, QB, 32], scope=att)
            q_hi = sb("q_hi", [P, 2, S], F32R, att)
            q_lo = sb("q_lo", [P, 2, S], F32R, att)
            prob_c = sb("prob_c", [P, 2, QB, NCP], scope=att)
            c_stat = sb("c_stat", [P, 4, QB], scope=att)
            prob = sb("prob", [P, 2, 1280], scope=att)
            stat = sb("stat", [P, 3, 2, QB], scope=att)
            pt_hi = sb("pt_hi", [P, 2, S], F32R, att)
            pt_lo = sb("pt_lo", [P, 2, S], F32R, att)
        y_hi = sb("y_hi", [P, DC, S], F32R, m1)
        y_lo = sb("y_lo", [P, DC, S], F32R, m1)
        m1.close()

        M = sb("mixed", [P, DC, S])
        with ExitStack() as ff:
            h_hi = sb("h_hi", [P, 2, 8, S], F32R, ff)
            h_lo = sb("h_lo", [P, 2, 8, S], F32R, ff)
            u4 = sb("u4", [P, 4, S], scope=ff)
            p_raw = sb("p_raw", [P, 2, S], scope=ff)
            p_hi = sb("p_hi", [P, 2, S], F32R, ff)
            p_lo = sb("p_lo", [P, 2, S], F32R, ff)
        with ExitStack() as pl:
            E = sb("ple_e", [P, DC, S], scope=pl)
        with ExitStack() as fx:
            fq_hi = sb("fq_hi", [P, 2, S], F32R, fx)
            fq_lo = sb("fq_lo", [P, 2, S], F32R, fx)
            fk_hi = sb("fk_hi", [P, 2, S], F32R, fx)
            fk_lo = sb("fk_lo", [P, 2, S], F32R, fx)
            fv = sb("fv", [P, 1, S], scope=fx)
            fv_hi = sb("fv_hi", [P, 2, QB, P], F32R, fx)
            fv_lo = sb("fv_lo", [P, 2, QB, P], F32R, fx)
            fprob = sb("fprob", [P, 2, 1280], scope=fx)
            fstat = sb("fstat", [P, 3, 2, QB], scope=fx)
            fpt_hi = sb("fpt_hi", [P, 2, S], F32R, fx)
            fpt_lo = sb("fpt_lo", [P, 2, S], F32R, fx)
            with ExitStack() as early:
                logf = sb("logf", [P, 4, S], scope=early)
            fo_hi = sb("fo_hi", [P, DC, S], F32R, fx)
            fo_lo = sb("fo_lo", [P, DC, S], F32R, fx)
            c_rows = sb("c_rows", [P, S], scope=fx)
            c_hi = sb("c_hi", [P, S], F32R, fx)
            c_head = sb("c_head", [P, 2, S], F32R, fx)
        with ExitStack() as c3:
            cy_hi = sb("cy_hi", [P, DC, S], F32R, c3)
            cy_lo = sb("cy_lo", [P, DC, S], F32R, c3)
            c3t = sb("c3t", [P, 5, S], scope=c3)

        ps = ctx.enter_context(nc.psum_tensor("ps", [P, 8, S], F32))

        w_loaded = [sem(f"w_loaded{s}") for s in range(RAW)]
        w_hi_ready = sem("w_hi_ready")
        w_ready = sem("w_ready")
        unit_done = sem("unit_done")
        bank_free = sem("bank_free")
        vec_loaded, p_loaded, out_stored = (sem(n) for n in ("vec_loaded", "p_loaded", "out_stored"))
        x_loaded = [sem(f"x_loaded{c}") for c in range(DC // 2)]
        c_pool, c_dve, c_act = sem("const_pool"), sem("const_dve"), sem("const_act")
        squared, summed = sem("squared"), sem("summed")
        ssq_done, rms_done, inv_done, diag_done, bcast_done, r_done = (
            sem(f"norm_{n}") for n in ("ssq", "rms", "inverse", "diag", "broadcast", "r"))
        prep_hi, prep_lo = sem("prep_hi"), sem("prep_lo")
        post_t, post_x = sem("post_t"), sem("post_x")
        final_x = sem("final_x")

        def stage_sems(stage, *names):
            return {n: sem(f"{stage}_{n}") for n in names}

        s_glu = stage_sems("glu", "sig", "gated")
        s_cmp = stage_sems("cmp", "dup", "blk", "hi", "lo", "gelu", "turned", "ghi", "glo", "out", "khi", "klo")
        s_kv = stage_sems("kv", "hi", "lo", "turned")
        s_gate = stage_sems("gate", "sig", "turned", "ready")
        s_mrg = stage_sems("merge", "sig", "conv")
        s_ln = stage_sems("ln", "sum", "mean", "cent", "sq", "acc", "var", "sd", "inv", "diag", "bc", "r", "n", "act", "hi", "lo")
        s_mix = stage_sems("mix", "a", "y", "hi", "lo")
        att_names = ("scores", "peak", "exps", "inv", "probs", "turned", "hi", "lo", "pv", "ohi", "olo")
        A1 = stage_sems("nsa", *att_names, "qhi", "qlo", "c", "cs")
        A2 = stage_sems("fox", *att_names, "qkhi", "qklo", "vs", "vturned", "vhi", "crow")
        s_fg = stage_sems("forget", "dve", "act")
        s_ffn = stage_sems("ffn", "tap", "conv", "t2", "gelu", "h", "hhi", "hlo")
        s_mlp = stage_sems("mlp", "s", "hi", "lo")
        s_ple = stage_sems("ple", "phi", "plo", "epe", "e", "sig", "g", "x")
        s_c3 = stage_sems("c3", "zz", "z2", "tap", "y", "hi", "lo")

        def vcol(name, i, n=1):
            return vec[:, ds(i + VEC[name], n)]

        def norm2_col(layer, which, i):
            return vec[:, ds(i + (VEC["norm2"] + (layer * 6 + which) * DC), 1)]

        block = ctx.enter_context(nc.Block())

        @block.sync
        def _(sp):
            def load(u, slot):
                sp.dma_start(w_raw[:, slot:slot + 1, :].rearrange("p a n -> p (a n)"),
                             weights[ds(u, 1)].rearrange("a p n -> (a p) n")).then_inc(w_loaded[slot], 16)

            def load_x(c):
                sp.dma_start(X[:, 2 * c:2 * c + 2, :], x_in[:, 2 * c:2 * c + 2, :]).then_inc(x_loaded[c], 16)

            load_x(0)
            sp.dma_start(vec[:], vectors).then_inc(vec_loaded, 16)
            load(0, 0)
            load_x(1)
            load_x(2)
            load_x(3)
            load(1, 1)
            with sp.Fori(1, U["end"] // RAW) as i:
                for s in range(RAW):
                    sp.wait_ge(w_ready, i * RAW + (s + 1 - RAW))
                    load(i * RAW + s, s)
            for u in range(U["end"] // RAW * RAW, U["end"]):
                sp.wait_ge(w_ready, u - RAW + 1)
                load(u, u % RAW)
            for m in range(DC):
                sp.wait_ge(post_x, 5 * DC + m + 1)
                sp.dma_start(out[:, m:m + 1, :], X[:, m:m + 1, :]).then_inc(out_stored, 16)
            sp.wait_ge(out_stored, 16 * DC)

        @block.gpsimd
        def _(pool):
            pool.memset(ident[:], 0.0).then_inc(c_pool, 1)
            pool.memset(causal[:], 0.0).then_inc(c_pool, 1)
            pool.memset(cmask[:], 0.0).then_inc(c_pool, 1)
            pool.memset(valid[:], 1.0).then_inc(c_pool, 1)
            pool.memset(head_sel[:], 0.0).then_inc(c_pool, 1)
            pool.wait_ge(c_pool, 5)
            pool.affine_select(out=ident[:], in_=ident[:], compare_op=ALU.not_equal, fill=1.0, base=0,
                               pattern=[[-1, P]], channel_multiplier=1).then_inc(c_pool, 1)
            pool.affine_select(out=causal[:], in_=causal[:], compare_op=ALU.is_ge, fill=NEG, base=0,
                               pattern=[[-1, P]], channel_multiplier=1).then_inc(c_pool, 1)
            pool.affine_select(out=cmask[:], in_=cmask[:], compare_op=ALU.is_ge, fill=NEG, base=-31,
                               pattern=[[P, QB], [-16, NCP]], channel_multiplier=1).then_inc(c_pool, 1)
            pool.affine_select(out=valid[:], in_=valid[:], compare_op=ALU.is_ge, fill=0.0, base=-31,
                               pattern=[[P, QB], [0, 1]], channel_multiplier=1).then_inc(c_pool, 1)
            for n, first in enumerate((0, 32)):
                rows = head_sel[first:first + 32, :]
                pool.wait_ge(c_pool, 9 + n)
                pool.affine_select(out=rows, in_=rows, compare_op=ALU.not_equal, fill=1.0, base=0,
                                   pattern=[[-1, 16]], channel_multiplier=1).then_inc(c_pool, 1)

            pool.wait_ge(c_pool, 11)

            def low(u, slot):
                pool.wait_ge(w_hi_ready, u + 1)
                pool.tensor_tensor(w_lo[:, slot, :], w_raw[:, slot, :], w_hi[:, slot, :].bitcast(F32),
                                   ALU.subtract).then_inc(w_ready, 1)

            def lows(u0, u1):
                pairs = (u1 - u0) // 2
                with pool.Fori(0, pairs) as i:
                    for s in range(2):
                        low(i * 2 + (u0 + s), (u0 + s) % 2)
                if (u1 - u0) % 2:
                    low(u1 - 1, (u1 - 1) % 2)

            def add_squares(n, m0, m1):
                for m in range(m0, m1):
                    pool.wait_ge(squared, m + (DC * (n - 1) + 1))
                    pool.wait_ge(summed, m + (10 * (n - 1) + CREDIT))
                    pool.tensor_tensor(sq_sum[:], sq_sum[:], sq[:, m % 2:m % 2 + 1, :], ALU.add).then_inc(summed, 1)

            u = 0

            for n, stage, before in ((5, "forget", 0), (7, "mlp1_up0", 0), (9, "ple1", 2), (11, "conv3", 0), (13, "mlp2_up0", 0), (15, "ple2", 2)):
                lows(u, U[stage] + 2)
                u = U[stage] + 2
                add_squares(n, 0, 4)
                if before:
                    low(u, u % 2)
                    u += 1
                add_squares(n, 4, DC)
            lows(u, U["end"])

        @block.tensor
        def _(pe):
            def three(o, w, x, wl, xl, start, stop):
                pe.matmul(o, w, x, start=start, stop=False)
                pe.matmul(o, w, xl, start=False, stop=False)
                return pe.matmul(o, wl, x, start=False, stop=stop)

            def wblock(slot, k):
                return w_hi[:, slot, k * P:(k + 1) * P], w_lo[:, slot, k * P:(k + 1) * P]

            def unit(u, slot, xh, xl, n=DC, o=None, first=0, k_ready=None, wait_bank=True, inc=True):
                if first == 0:
                    pe.wait_ge(w_ready, u + 1)
                if wait_bank:
                    pe.wait_ge(bank_free, u + 1)
                o = ps[:, slot, :] if o is None else o
                for k in range(n):
                    if k_ready is not None:
                        pe.wait_ge(k_ready[0], k_ready[1] + k + 1)
                    wh, wl = wblock(slot, first + k)
                    mm = three(o, wh, xh[:, k, :], wl, xl[:, k, :], k == 0, k == n - 1)
                return mm.then_inc(unit_done, 1) if inc else mm

            def part(u, slot, k0, k1, xh=xg_hi, xl=xg_lo):
                if k0 == 0:
                    pe.wait_ge(w_ready, u + 1)
                    pe.wait_ge(bank_free, u + 1)
                for k in range(k0, k1):
                    wh, wl = wblock(slot, k)
                    mm = three(ps[:, slot, :], wh, xh[:, k, :], wl, xl[:, k, :], k == 0, k == DC - 1)
                if k1 == DC:
                    mm.then_inc(unit_done, 1)

            def units(u0, n, xh, xl, k=DC, k_ready=None):
                with pe.Fori(0, n // 2) as i:
                    for j in range(2):
                        unit(i * 2 + (u0 + j), (u0 + j) % 2, xh, xl, k, k_ready=k_ready if j == 0 else None)

            def norm_sums(n):
                pe.wait_ge(summed, 10 * n)
                for tb in range(QB):
                    mm = pe.matmul(ps[:, 7, tb:tb + 1], sq_sum[:, 0, tb * P:(tb + 1) * P], mean_col[:], start=True, stop=True)
                mm.then_inc(ssq_done, 1)

            def norm_spread(n):
                pe.wait_ge(diag_done, n)
                pe.matmul(ps[:, 7, :], ones[:], r_diag[:].rearrange("p a b -> p (a b)"), start=True, stop=True).then_inc(bcast_done, 1)

            def norm(n):
                norm_sums(n)
                norm_spread(n)

            def first_two(u0, n, prep):
                unit(u0, u0 % 2, xg_hi, xg_lo, k_ready=(prep_lo, DC * prep))
                u = u0 + 1
                part(u, u % 2, 0, 2)
                norm_sums(n)
                part(u, u % 2, 2, 6)
                norm_spread(n)
                part(u, u % 2, 6, 8)

            def rest(u0, n):
                with pe.Fori(1, n // 2) as i:
                    for j in range(2):
                        unit(i * 2 + (u0 + j), (u0 + j) % 2, xg_hi, xg_lo)

            pe.wait_ge(c_pool, 11)
            pe.wait_ge(c_dve, 4)
            first_two(U["glu"], 1, 0)
            rest(U["glu"], 8)
            units(U["cmp_in"], 4, xg_hi, xg_lo)
            def hidden_turn(kv):
                pe.wait_ge(s_cmp["gelu"], kv + 1)
                for half in range(2):
                    mm = pe.transpose(ps[:, 6 + kv, half * 64:half * 64 + 2 * NC1], hid[:, kv, half * P:(half + 1) * P],
                                      ident[0:2 * NC1, 0:2 * NC1])
                mm.then_inc(s_cmp["turned"], 1)

            for kv in range(2):
                pe.wait_ge(s_cmp["lo"], kv + 1)
                for i in range(4):
                    uu = U["cmp_hidden"] + 4 * kv + i
                    pe.wait_ge(w_ready, uu + 1)
                    for c in range(4):
                        o = ps[0:2 * NC1, 2 + kv, 0:2 * P]
                        xh, xl = blk_hi[:, kv, 4 * i + c, :], blk_lo[:, kv, 4 * i + c, :]
                        wh, wl = (w[:, uu % 2, c * 2 * P:(c + 1) * 2 * P] for w in (w_hi, w_lo))
                        mm = three(o, xh, wh, xl, wl, i == 0 and c == 0, i == 3 and c == 3)
                    mm.then_inc(unit_done, 1)
                    if kv == 1 and i == 1:
                        hidden_turn(0)
            unit(U["keys"], U["keys"] % 2, xg_hi, xg_lo)
            hidden_turn(1)
            unit(U["keys"] + 1, (U["keys"] + 1) % 2, xg_hi, xg_lo)
            uu = U["cmp_out"]
            sl = uu % 2
            pe.wait_ge(w_ready, uu + 1)
            pe.wait_ge(s_cmp["glo"], 2)
            for half in range(2):
                wh, wl = wblock(sl, half)
                three(ps[:, 4, 0:2 * NC1], wh, hid_hi[:, 0, half, :], wl, hid_lo[:, 0, half, :], half == 0, half == 1)
            for g in range(2):
                for half in range(2):
                    cols = slice(256 + half * HD, 256 + (half + 1) * HD)
                    own = slice(g * NC1, (g + 1) * NC1)
                    o = ps[0:NC1, 5, g * HD:(g + 1) * HD]
                    mm = three(o, hid_hi[:, 1, half, own], w_hi[:, sl, cols], hid_lo[:, 1, half, own], w_lo[:, sl, cols],
                               half == 0, half == 1)
            mm.then_inc(unit_done, 1)
            for j in range(2):
                uu = U["values"] + j
                unit(uu, uu % 2, xg_hi, xg_lo)
            uu = U["gates"]
            unit(uu, uu % 2, xg_hi, xg_lo)
            unit(U["q0"], U["q0"] % 2, xg_hi, xg_lo)
            for j in range(2):
                pe.wait_ge(bank_free, U["values"] + j + 1 + CREDIT)
                for tb in range(QB):
                    mm = pe.transpose(ps[:, 6 + j, tb * P:(tb + 1) * P], T2[:, j, tb * P:(tb + 1) * P], ident[:])
                mm.then_inc(s_kv["turned"], 1)
            pe.wait_ge(s_gate["sig"], 1)
            for tb in range(QB):
                mm = pe.transpose(ps[:, 4, tb * 32:(tb + 1) * 32], sq[0:32, 0, tb * P:(tb + 1) * P], ident[0:32, 0:32])
            mm.then_inc(s_gate["turned"], 1)
            def attention(A, q, k, v, pt, probs, h, r0, idx, branch_bank):
                qh, ql = q
                kh, kl = k
                vh, vl = v

                def scores(qi, c_row=None):
                    e = idx + qi
                    pe.wait_ge(A["exps"], e + 1)
                    b = 2 + (h["par"] + qi) % 2
                    n = (qi + 1) * P
                    rows = slice(r0, r0 + HD)
                    o = ps[:, b, 0:n]
                    qs = slice(qi * P, n)
                    pe.matmul(o, qh[rows, qs], kh[rows, 0:n], start=True, stop=False)
                    pe.matmul(o, qh[rows, qs], kl[rows, 0:n], start=False, stop=False)
                    pe.matmul(o, ql[rows, qs], kh[rows, 0:n], start=False, stop=False)
                    if c_row is not None:
                        pe.matmul(o, ones_r[:], c_row[:, 0:n], start=False, stop=False)
                    pe.matmul(ps[:, b, qi * P:n], ident_r[:], causal_r[:], start=False, stop=True).then_inc(A["scores"], 1)

                def turn(kb):
                    e = idx + kb
                    pe.wait_ge(A["lo"], e + 1)
                    if kb == 0:
                        pe.wait_ge(A["probs"], h["sidx"] + (QB + CREDIT))
                    b = 4 + (h["par"] + kb) % 2
                    for qi in range(kb, QB):
                        off = P_OFF[qi] + kb * P
                        mm = pe.transpose(ps[:, b, qi * P:(qi + 1) * P], probs[:, off:off + P], ident[:])
                    mm.then_inc(A["turned"], 1)

                def pv(kb, start, stop):
                    e = idx + kb
                    pe.wait_ge(A["lo"], e + 1 + CREDIT)
                    b = (h["par"] + kb) % 2
                    o = ps[:, branch_bank, kb * P:S]
                    ph, plo = pt[0][:, b, kb * P:S], pt[1][:, b, kb * P:S]
                    pe.matmul(o, vh[:, kb, :], ph, start=start and kb == 0, stop=False)
                    pe.matmul(o, vh[:, kb, :], plo, start=False, stop=False)
                    pe.matmul(o, vl[:, kb, :], ph, start=False, stop=stop and kb == QB - 1).then_inc(A["pv"], 1)

                return scores, turn, pv

            pair_events = 18

            pe.wait_ge(c_act, 4)
            pe.wait_ge(s_kv["lo"], 2)
            pe.wait_ge(s_cmp["klo"], 2)
            for p in range(4):
                qp = (q_hi[:, p % 2, :], q_lo[:, p % 2, :])
                pe.wait_ge(A1["qlo"], p + 1)

                def cmp_scores(hd):
                    e = p * pair_events + 9 * hd
                    pe.wait_ge(A1["exps"], e + 1)
                    b = 2 + e % 2
                    rows = slice(hd * HD, (hd + 1) * HD)
                    for qi in range(QB):
                        o, qs = ps[:, b, qi * NCP:(qi + 1) * NCP], slice(qi * P, (qi + 1) * P)
                        pe.matmul(o, qp[0][rows, qs], kc_hi[rows, :], start=True, stop=False)
                        pe.matmul(o, qp[0][rows, qs], kc_lo[rows, :], start=False, stop=False)
                        pe.matmul(o, qp[1][rows, qs], kc_hi[rows, :], start=False, stop=False)
                        mm = pe.matmul(o, ident_r[:], cmp_mask_r[:, qi, :], start=False, stop=True)
                    mm.then_inc(A1["scores"], 1)

                def cmp_turn(hd):
                    e = p * pair_events + 9 * hd
                    pe.wait_ge(A1["lo"], e + 1)
                    pe.wait_ge(A1["c"], 2 * p + hd + 1)
                    b = 4 + e % 2
                    for qi in range(QB):
                        mm = pe.transpose(ps[0:NCP, b, qi * P:(qi + 1) * P], prob_c[:, hd, qi, :], ident[:])
                    mm.then_inc(A1["turned"], 1)

                def cmp_pv(hd):
                    e = p * pair_events + 9 * hd
                    pe.wait_ge(A1["lo"], e + 1 + CREDIT)
                    pe.wait_ge(A1["olo"], 2 * p + hd + 1)
                    b = e % 2
                    o = ps[:, 6 + hd, :]
                    pe.matmul(o, vc_hi[:], pt_hi[0:NCP, b, :], start=True, stop=False)
                    pe.matmul(o, vc_hi[:], pt_lo[0:NCP, b, :], start=False, stop=False)
                    pe.matmul(o, vc_lo[:], pt_hi[0:NCP, b, :], start=False, stop=False).then_inc(A1["pv"], 1)

                F = []
                for hd in range(2):
                    for br in range(2):
                        idx = p * pair_events + 9 * hd + 1 + 4 * br
                        n = 4 * p + 2 * hd + br
                        F.append(attention(A1, qp, (kk_hi[:, br, :], kk_lo[:, br, :]), (vv_hi[:, br], vv_lo[:, br]),
                                           (pt_hi, pt_lo), prob[:, n % 2, :], {"par": idx, "sidx": 4 * n}, hd * HD, idx, 6 + hd))

                mine = pair_units(p)

                def fill(n, k0, k1):
                    if mine[n] is not None:
                        part(mine[n], mine[n] % 2, k0, k1)

                def two_steps(new, old, last, n, k0=2):
                    ns, (_, ot, ov) = new[0], old
                    cut = [k0 + (8 - k0) * q // 4 for q in range(5)]
                    ns(0); ns(1); fill(n, cut[0], cut[1]); ot(0); ot(1); ns(2); fill(n, cut[1], cut[2])
                    ov(0, False, last); ot(2); ns(3); fill(n, cut[2], cut[3]); ov(1, False, last); ot(3)
                    fill(n, cut[3], cut[4]); ov(2, False, last); ov(3, False, last)

                cmp_scores(0)
                F[0][0](0); fill(0, 0, 2); cmp_turn(0); F[0][0](1); fill(0, 2, 6)
                if p == 0:
                    pe.wait_ge(s_kv["lo"], 4)
                cmp_pv(0); F[0][0](2); F[0][0](3); fill(0, 6, 8); fill(1, 0, 2)
                two_steps(F[1], F[0], False, 1)
                fill(4, 0, 2); cmp_scores(1)
                two_steps(F[2], F[1], True, 4)
                cmp_turn(1); fill(2, 0, 4); cmp_pv(1)
                two_steps(F[3], F[2], False, 2, 4)
                _, ot, ov = F[3]
                ot(0); ot(1)
                if p < 3:
                    fill(3, 0, 4)
                ov(0, False, True); ot(2); ov(1, False, True); ot(3); ov(2, False, True)
                if p < 3:
                    fill(3, 4, 8)
                ov(3, False, True)

            pe.wait_ge(s_ln["sum"], 3)
            pe.matmul(ps[:, 4, :], mean_ch[:], T[:, 0, :], start=True, stop=True).then_inc(s_ln["mean"], 1)
            part(mine[3], mine[3] % 2, 0, 8)
            pe.wait_ge(s_ln["acc"], 4)
            for tb in range(QB):
                mm = pe.matmul(ps[:, 5, tb:tb + 1], T[:, 1, tb * P:(tb + 1) * P], mean_ch[:, 0:1], start=True, stop=True)
            mm.then_inc(s_ln["var"], 1)
            pe.wait_ge(s_ln["diag"], 1)
            pe.matmul(ps[:, 5, :], ones[:], r_diag[:].rearrange("p a b -> p (a b)"), start=True, stop=True).then_inc(s_ln["bc"], 1)
            pe.wait_ge(A1["olo"], CREDIT + 8)
            def mix_nsa(u, slot):
                unit(u, slot, o_hi, o_lo, 4, inc=False)

            def mix_conv(u, slot):
                unit(u, slot, xg_hi, xg_lo, 4, o=ps[:, 2 + slot, :], first=4, wait_bank=False)

            for u in range(U["mix"], U["mix"] + 2):
                mix_nsa(u, u % 2)
            pe.wait_ge(s_ln["lo"], 4)
            for u in range(U["mix"], U["mix"] + 2):
                mix_conv(u, u % 2)
            with pe.Fori(1, 4) as i:
                for j in range(2):
                    mix_nsa(i * 2 + (U["mix"] + j), (U["mix"] + j) % 2)
                    mix_conv(i * 2 + (U["mix"] + j), (U["mix"] + j) % 2)
            units(U["w_out"], 8, y_hi, y_lo, k_ready=(s_mix["lo"], 0))

            for n, (kind, p) in enumerate(ffn_order(len(FF1_PARTS))):
                u0 = U[f"ffn_{kind}{p}"]
                if kind == "up":
                    if p == 0:
                        first_two(u0, 2, 1)
                        rest(u0, 2 * FF1_PARTS[0])
                    else:
                        units(u0, 2 * FF1_PARTS[p], xg_hi, xg_lo)
                else:
                    base = sum(FF1_PARTS[:p])
                    units(u0, 8, h_hi[:, p % 2], h_lo[:, p % 2], FF1_PARTS[p], k_ready=(s_ffn["hlo"], base))

            def ple_gate(n, norm_n, prep):
                first_two(U[f"ple{n}"] + 2, norm_n, prep)
                rest(U[f"ple{n}"] + 2, DC)

            def ple_embed(n):
                u0 = U[f"ple{n}"]
                pe.wait_ge(s_ple["plo"], n + 1)
                for half in range(2):
                    uu = u0 + half
                    pe.wait_ge(w_ready, uu + 1)
                    for m in range(4):
                        t = 4 * half + m
                        if t >= 4:
                            pe.wait_ge(s_ple["e"], DC * n + t - 4 + 1)
                        for k in range(2):
                            wh, wl = wblock(uu % 2, 2 * m + k)
                            mm = three(ps[:, 2 + t % 4, :], wh, p_hi[:, k, :], wl, p_lo[:, k, :], k == 0, k == 1)
                        if m < 3:
                            mm.then_inc(s_ple["epe"], 1)
                    mm.then_inc(unit_done, 1)

            ple_embed(0)
            ple_gate(0, 3, 2)
            norm(4)

            uu = U["forget"]
            unit(uu, uu % 2, xg_hi, xg_lo, k_ready=(prep_lo, DC * 3))
            norm(5)

            def fox_unit(j, uu, slot):
                unit(uu, slot, xg_hi, xg_lo)

            def fox_turn(p, slot):
                pe.wait_ge(A2["vs"], p + 1)
                for tb in range(QB):
                    mm = pe.transpose(ps[:, slot, tb * P:(tb + 1) * P], fv[:, 0, tb * P:(tb + 1) * P], ident[:])
                mm.then_inc(A2["vturned"], 1)

            u0 = U["fox"]
            for j in range(3):
                fox_unit(j, u0 + j, (u0 + j) % 2)
            fox_turn(0, (u0 + 2) % 2)

            def fox_pair(p, par, more):
                nxt = [(u0 + 3 + 3 * par + j) % 2 for j in range(3)]
                pe.wait_ge(A2["qklo"], p * 2 + 2)
                hs = []
                for hd in range(2):
                    hs.append(attention(A2, (fq_hi[:, par, :], fq_lo[:, par, :]), (fk_hi[:, par, :], fk_lo[:, par, :]),
                                        (fv_hi[:, par], fv_lo[:, par]), (fpt_hi, fpt_lo), fprob[:, hd, :],
                                        {"par": 0, "sidx": p * 8 + 4 * hd}, hd * HD, p * 8 + 4 * hd, 6 + hd))
                (sa, ta, va), (sb_, tb_, vb) = hs
                pe.wait_ge(A2["crow"], p * 2 + 1)
                ca, cb = c_head[:, 0, :], c_head[:, 1, :]

                def fill(j, k0, k1):
                    if more:
                        part(p * 3 + (u0 + 3 + j), nxt[j], k0, k1)

                sa(0, ca); sa(1, ca); fill(0, 0, 8)
                sa(2, ca); sa(3, ca); fill(1, 0, 4)
                pe.wait_ge(A2["crow"], p * 2 + 2)
                sb_(0, cb); sb_(1, cb); fill(1, 4, 8)
                pe.wait_ge(A2["olo"], p * 2 + 1)
                pe.wait_ge(bank_free, p * 3 + (u0 + 3 + CREDIT))
                ta(0); ta(1); fill(2, 0, 2); sb_(2, cb); va(0, True, True); ta(2); sb_(3, cb); va(1, True, True); ta(3)
                va(2, True, True); fill(2, 2, 5); va(3, True, True)
                pe.wait_ge(A2["olo"], p * 2 + 2)
                tb_(0); tb_(1); fill(2, 5, 8); vb(0, True, True); tb_(2); vb(1, True, True); tb_(3); vb(2, True, True)
                vb(3, True, True)
                if more:
                    fox_turn(p + 1, nxt[2])

            with pe.Fori(0, 3) as i:
                for par in range(2):
                    fox_pair(i * 2 + par, par, True)
            fox_pair(6, 0, True)
            fox_pair(7, 1, False)
            pe.wait_ge(A2["olo"], CREDIT + 16)
            units(U["fox_out"], 8, fo_hi, fo_lo)
            norm(6)

            def mlp(n, norm_n, prep):
                for kind, p in ffn_order(len(FF2_PARTS)):
                    u0 = U[f"mlp{n}_{kind}{p}"]
                    if kind == "up" and p == 0:
                        first_two(u0, norm_n, prep)
                        rest(u0, 8)
                    elif kind == "up":
                        units(u0, 8, xg_hi, xg_lo)
                    else:
                        units(u0, 8, h_hi[:, p % 2], h_lo[:, p % 2], 8, k_ready=(s_mlp["lo"], 32 * (n - 1) + 8 * p))
                norm(norm_n + 1)

            mlp(1, 7, 4)
            ple_embed(1)
            ple_gate(1, 9, 5)
            norm(10)
            u0 = U["conv3"]
            first_two(u0, 11, 6)
            for j in range(2, 6):
                unit(u0 + j, (u0 + j) % 2, xg_hi, xg_lo)
            with pe.Fori(1, 4) as i:
                for j in range(6):
                    unit(i * 6 + (u0 + j), (u0 + j) % 2, xg_hi, xg_lo)
            units(U["conv3_out"], 8, cy_hi, cy_lo, k_ready=(s_c3["lo"], 0))
            norm(12)
            mlp(2, 13, 7)
            ple_embed(2)
            ple_gate(2, 15, 8)
            norm(16)

        @block.vector
        def _(dve):
            def scaled(u, slot, out, n_done=None):
                dve.wait_ge(unit_done, u + 1)
                dve.tensor_tensor(out, ps[:, slot:slot + 1, :], R[:], ALU.mult).then_inc(bank_free, 1)

            def units(u0, n, body, per=2):
                with dve.Fori(0, n // per) as i:
                    for j in range(per):
                        body(i * per + j, j, i * per + (u0 + j), (u0 + j) % 2)

            def low(out, x, hi, done):
                dve.tensor_tensor(out, x, hi.bitcast(F32), ALU.subtract).then_inc(done, 1)

            def norm_start(n):
                if n > 1:
                    dve.wait_ge(ssq_done, n - 1)
                dve.memset(sq_sum[:], 0.0).then_inc(summed, CREDIT)

            def add_square(n, m, j):
                dve.wait_ge(squared, m + (DC * (n - 1) + 1))
                dve.wait_ge(summed, m + (10 * (n - 1) + CREDIT))
                dve.tensor_tensor(sq_sum[:], sq_sum[:], sq[:, j:j + 1, :], ALU.add).then_inc(summed, 1)

            def norm_inverse(n):
                dve.wait_ge(rms_done, n)
                if n > 1:
                    dve.wait_ge(diag_done, n - 1)
                dve.reciprocal(rms_c[:, 1, :], rms_c[:, 0, :]).then_inc(inv_done, 1)
                dve.wait_ge(inv_done, n)
                if n > 1:
                    dve.wait_ge(bcast_done, n - 1)
                dve.tensor_tensor(r_diag[:], ident[:].unsqueeze(1).to_broadcast([P, QB, P]),
                                  rms_c[:, 1, :].unsqueeze(2).to_broadcast([P, QB, P]), ALU.mult).then_inc(diag_done, 1)

            def prep_low(prep, m, g):
                dve.wait_ge(prep_hi, m + (DC * prep + 1))
                dve.scalar_tensor_tensor(xg_lo[:, ds(m, 1), :], X[:, ds(m, 1), :], g, xg_hi[:, ds(m, 1), :].bitcast(F32),
                                         ALU.mult, ALU.subtract).then_inc(prep_lo, 1)

            def spread_steps(tile, ahead, prep, gain):
                tile(0, 0)
                ahead(1, 1)
                with dve.Fori(0, DC // 2 - 1) as i:
                    for j in range(2):
                        m = i * 2 + (j + 1)
                        tile(m, 1 - j)
                        ahead(i * 2 + (j + 2), j)
                        prep_low(prep, i * 2 + j, gain(i * 2 + j))
                tile(DC - 1, 1)
                prep_low(prep, DC - 2, gain(DC - 2))
                prep_low(prep, DC - 1, gain(DC - 1))

            dve.memset(ones[:], 1.0).then_inc(c_dve, 1)
            dve.memset(mean_col[:], 1.0 / D).then_inc(c_dve, 1)
            dve.memset(mean_ch[:], 1.0 / (CT * P)).then_inc(c_dve, 1)
            dve.memset(eps_col[:], EPS).then_inc(c_dve, 1)
            dve.memset(token[:, 0:1], 0.0).then_inc(bank_free, CREDIT)
            for n, key in enumerate(("exps", "lo", "olo", "probs")):
                for g, A in enumerate((A1, A2)):
                    dve.memset(token[:, 4 * g + n + 1:4 * g + n + 2], 0.0).then_inc(A[key], CREDIT)
            dve.memset(token[:, 9:10], 0.0).then_inc(s_mrg["sig"], CREDIT)
            norm_start(1)
            dve.memset(glu[:, :, 0:PAD], 0.0).then_inc(s_glu["gated"], 1)
            dve.wait_ge(vec_loaded, 16)
            dve.wait_ge(c_pool, 11)
            with dve.Fori(0, DC // 2) as i:
                for j in range(2):
                    m = i * 2 + j
                    add_square(1, m, j)
                    prep_low(0, m, vcol("g_mix", m))
            norm_inverse(1)
            dve.wait_ge(r_done, 1)
            def taps(n0, n1):
                for n in range(n0, n1):
                    ct, k = divmod(n, CONV_TAPS)
                    acc, src, w = conv_acc[:, ct, :], glu[:, ct, k:k + S], vcol("conv_w", n)
                    if k == 0:
                        ins = dve.tensor_scalar(acc, src, w, vcol("conv_b", ct), ALU.mult, ALU.add)
                    else:
                        dve.wait_ge(s_mrg["conv"], n)
                        ins = dve.scalar_tensor_tensor(acc, src, w, acc, ALU.mult, ALU.add)
                    ins.then_inc(s_mrg["conv"], 1)

            u0 = U["glu"]
            for i in range(CT):
                dve.wait_ge(s_glu["gated"], i + 1)
                for j in range(2):
                    scaled(i * 2 + (u0 + j), j, T[:, j:j + 1, :])
                dve.wait_ge(s_glu["sig"], i + 1)
                dve.tensor_tensor(glu[:, i:i + 1, PAD:PAD + S], T[:, 0:1, :], T2[:, 0:1, :], ALU.mult).then_inc(s_glu["gated"], 1)
                if i:
                    taps(9 * (i - 1), 9 * i)
            dve.wait_ge(s_glu["gated"], CT + 1)
            for j in range(4):
                uu = U["cmp_in"] + j
                dve.wait_ge(unit_done, uu + 1)
                dve.tensor_tensor(kv_dup[0:HD, j, :], ps[0:HD, uu % 2, :], R[0:HD, 0, :], ALU.mult).then_inc(s_cmp["dup"], 1)
                dve.tensor_tensor(kv_dup[HD:P, j, 0:S - 1], ps[HD:P, uu % 2, 1:S], R[HD:P, 0, 1:S], ALU.mult).then_inc(bank_free, 1)
                if j < 3:
                    taps(27 + 4 * j, 31 + 4 * j)
            dve.memset(kc_f[:], 0.0).then_inc(s_cmp["out"], 1)
            dve.memset(vc_f[:], 0.0).then_inc(bank_free, 8)
            dve.wait_ge(s_cmp["dup"], 4)
            dve.wait_ge(bank_free, U["keys"] + CREDIT)
            for kv, pos in enumerate(("pos_k", "pos_v")):
                for g in range(2):
                    src = kv_dup[:, 2 * kv + g, :].rearrange("p (c s) -> p s c", s=16)
                    for half in range(2):
                        o = blk[:, kv, 8 * half:8 * half + 8, g * NC1:(g + 1) * NC1]
                        at = VEC[pos] + 8 * half
                        dve.tensor_tensor(o, src[:, 0:16:2, half:half + NC1],
                                          vec[:, at:at + 8].unsqueeze(2).to_broadcast([P, 8, NC1]), ALU.add).then_inc(s_cmp["blk"], 1)
            for kv in range(2):
                dve.wait_ge(s_cmp["hi"], kv + 1)
                low(blk_lo[:, kv], blk[:, kv], blk_hi[:, kv], s_cmp["lo"])

            def hidden_low(kv):
                dve.wait_ge(s_cmp["ghi"], kv + 1)
                low(hid_lo[:, kv], ps[:, 6 + kv, 0:P].rearrange("p (a b) -> p a b", b=64)[:, :, 0:2 * NC1], hid_hi[:, kv],
                    s_cmp["glo"])

            def keys(j):
                uu = U["keys"] + j
                scaled(uu, uu % 2, T[:, j:j + 1, :])
                dve.wait_ge(s_kv["hi"], j + 1)
                low(kk_lo[:, j, :], T[:, j, :], kk_hi[:, j, :], s_kv["lo"])

            taps(39, 62)
            hidden_low(0)
            taps(62, 78)
            keys(0)
            hidden_low(1)
            taps(78, 83)
            keys(1)
            dve.memset(token[:, 13:14], 0.0).then_inc(bank_free, 1)
            dve.wait_ge(unit_done, U["cmp_out"] + 1)
            dve.wait_ge(s_cmp["out"], 1)
            dve.tensor_copy(kc_f[0:HD, 0:NC1], ps[0:HD, 4, 0:NC1]).then_inc(s_cmp["out"], 1)
            dve.tensor_copy(kc_f[HD:P, 0:NC1], ps[HD:P, 4, NC1:2 * NC1]).then_inc(s_cmp["out"], 1)
            dve.tensor_copy(vc_f[0:NC1, :], ps[0:NC1, 5, 0:P]).then_inc(s_cmp["out"], 1)
            dve.wait_ge(s_cmp["khi"], 2)
            dve.wait_ge(s_cmp["out"], 4)
            low(kc_lo[:], kc_f[:], kc_hi[:], s_cmp["klo"])
            low(vc_lo[:], vc_f[:], vc_hi[:], s_cmp["klo"])
            taps(83, 87)
            for j in range(2):
                uu = U["values"] + j
                scaled(uu, uu % 2, T2[:, j:j + 1, :])
                taps(87 + 4 * j, 91 + 4 * j)
            uu = U["gates"]
            dve.wait_ge(s_kv["lo"], 2)
            scaled(uu, uu % 2, T[:, 0:1, :])
            def low_q(A, out, x, hi, done):
                dve.scalar_tensor_tensor(out, x, HD ** -0.5, hi.bitcast(F32), ALU.mult, ALU.subtract).then_inc(done, 1)

            def nsa_q(p):
                uu = pair_units(p - 1)[4] if p else U["q0"]
                if p >= 2:
                    dve.wait_ge(A1["qlo"], p - 1)
                scaled(uu, uu % 2, T[:, p % 2:p % 2 + 1, :])
                dve.wait_ge(A1["qhi"], p + 1)
                low_q(A1, q_lo[:, p % 2, :], T[:, p % 2, :], q_hi[:, p % 2, :], A1["qlo"])

            dve.wait_ge(s_gate["sig"], 1)
            nsa_q(0)
            for j in range(2):
                dve.wait_ge(s_kv["hi"], 3 + j)
                low(vv_lo[:, j], ps[:, 6 + j, :].rearrange("p (a b) -> p a b", b=P), vv_hi[:, j], s_kv["lo"])
            dve.wait_ge(s_gate["turned"], 1)
            dve.tensor_copy(gates[:], ps[:, 4, 0:QB * 32].rearrange("p (a b) -> p a b", b=32)).then_inc(s_gate["ready"], 1)

            dve.wait_ge(s_kv["lo"], 4)
            def merge_gate(p, i):
                uu, m = pair_units(p)[i], 4 * p + i
                scaled(uu, uu % 2, merge[:, m:m + 1, :])

            def peak(A, e, par, st, qi, b):
                dve.wait_ge(A["scores"], e + 1)
                dve.tensor_reduce(st[:, 0, par, qi:qi + 1], ps[:, b, 0:(qi + 1) * P], AX.X, ALU.max, negate=True).then_inc(A["peak"], 1)

            def normalise(A, e, n, par, st, pr, qi, gate=None):
                dve.wait_ge(A["exps"], e + 1 + CREDIT)
                dve.wait_ge(A["probs"], n * QB + (qi + CREDIT))
                dve.reciprocal(st[:, 2, par, qi:qi + 1], st[:, 1, par, qi:qi + 1]).then_inc(A["inv"], 1)
                dve.wait_ge(A["inv"], n * QB + (qi + 1))
                row = pr[:, P_OFF[qi]:P_OFF[qi] + (qi + 1) * P]
                dve.tensor_scalar(row, row, st[:, 2, par, qi:qi + 1], gate, ALU.mult,
                                  ALU.bypass if gate is None else ALU.mult).then_inc(A["probs"], 1)

            def split_turned(A, e, b, pt, kb):
                dve.wait_ge(A["hi"], e + 1)
                low(pt[1][:, b, kb * P:S], ps[:, 4 + b, kb * P:S], pt[0][:, b, kb * P:S], A["lo"])

            dve.wait_ge(s_gate["ready"], 1)
            for p in range(4):
                e0 = 18 * p

                def cmp_peak(hd):
                    e = e0 + 9 * hd
                    sc = ps[:, 2 + e % 2, 0:QB * NCP].rearrange("p (a b) -> p a b", b=NCP)
                    dve.wait_ge(A1["scores"], e + 1)
                    if e:
                        dve.wait_ge(A1["c"], 2 * p + hd)
                    dve.tensor_reduce(c_stat[:, 0, :], sc, AX.X, ALU.max).then_inc(A1["cs"], 1)
                    dve.wait_ge(A1["cs"], 5 * (2 * p + hd) + 1)
                    dve.tensor_tensor(prob_c[:, hd], sc, c_stat[:, 0, :].unsqueeze(2).to_broadcast([P, QB, NCP]),
                                      ALU.subtract).then_inc(A1["peak"], 1)

                def cmp_normalise(hd):
                    e = e0 + 9 * hd
                    n = 5 * (2 * p + hd)
                    dve.wait_ge(A1["exps"], e + 1 + CREDIT)
                    dve.tensor_reduce(c_stat[:, 1, :], prob_c[:, hd], AX.X, ALU.add).then_inc(A1["cs"], 1)
                    dve.wait_ge(A1["cs"], n + 2)
                    dve.reciprocal(c_stat[:, 2, :], c_stat[:, 1, :]).then_inc(A1["cs"], 1)
                    dve.wait_ge(A1["cs"], n + 3)
                    dve.tensor_tensor(c_stat[:, 2, :], c_stat[:, 2, :], gates[:, :, 4 * hd + p], ALU.mult).then_inc(A1["cs"], 1)
                    dve.wait_ge(A1["cs"], n + 4)
                    dve.tensor_tensor(c_stat[:, 3, :], c_stat[:, 2, :], valid[:, :, 0], ALU.mult).then_inc(A1["cs"], 1)
                    dve.wait_ge(A1["cs"], n + 5)
                    dve.tensor_tensor(prob_c[:, hd], prob_c[:, hd], c_stat[:, 3, :].unsqueeze(2).to_broadcast([P, QB, NCP]),
                                      ALU.mult).then_inc(A1["c"], 1)

                def cmp_split(hd):
                    e = e0 + 9 * hd
                    dve.wait_ge(A1["hi"], e + 1)
                    low(pt_lo[0:NCP, e % 2, :], ps[0:NCP, 4 + e % 2, :], pt_hi[0:NCP, e % 2, :], A1["lo"])

                def where(f):
                    return e0 + 9 * (f // 2) + 1 + 4 * (f % 2), 4 * p + f, 8 * (1 + f % 2) + 4 * (f // 2) + p

                def mx(f, qi):
                    e, n, _ = where(f)
                    peak(A1, e + qi, n % 2, stat, qi, 2 + (e + qi) % 2)

                def nrm(f, qi):
                    e, n, col = where(f)
                    normalise(A1, e + qi, n, n % 2, stat, prob[:, n % 2, :], qi, gates[:, qi, col:col + 1])

                def lo(f, kb):
                    e = where(f)[0] + kb
                    split_turned(A1, e, e % 2, (pt_hi, pt_lo), kb)

                def out_low(hd):
                    rows = slice(hd * HD, (hd + 1) * HD)
                    dve.wait_ge(A1["ohi"], 2 * p + hd + 1)
                    low(o_lo[rows, p, :], ps[rows, 6 + hd, :], o_hi[rows, p, :], A1["olo"])

                def conv(k):
                    n = 95 + 8 * p + k
                    taps(n, min(n + 1, CT * CONV_TAPS))

                def two_steps(new, old, n, k):
                    mx(new, 0); mx(new, 1); lo(old, 0); nrm(new, 0); mx(new, 2); lo(old, 1); nrm(new, 1)
                    lo(old, 2); mx(new, 3); nrm(new, 2); lo(old, 3); nrm(new, 3)
                    if n < 4:
                        merge_gate(p, n)
                    else:
                        cmp_normalise(1)
                        if p < 3:
                            nsa_q(p + 1)
                    conv(k); conv(k + 1)

                cmp_peak(0); mx(0, 0); cmp_normalise(0); cmp_split(0); mx(0, 1); nrm(0, 0); nrm(0, 1); conv(0)
                mx(0, 2); mx(0, 3); nrm(0, 2); nrm(0, 3); merge_gate(p, 0); conv(1)
                two_steps(1, 0, 1, 2)
                cmp_peak(1)
                two_steps(2, 1, 4, 4)
                out_low(0); cmp_split(1)
                two_steps(3, 2, 2, 6)
                lo(3, 0); lo(3, 1); lo(3, 2); lo(3, 3)
                if p < 3:
                    merge_gate(p, 3)
                else:
                    dve.wait_ge(s_mrg["conv"], CT * CONV_TAPS)
                    dve.wait_ge(A1["qlo"], 4)
                    dve.tensor_tensor(T[:, 0, :], conv_acc[:, 0, :], conv_acc[:, 1, :], ALU.add).then_inc(s_ln["sum"], 1)
                    for ct in (2, 3):
                        dve.wait_ge(s_ln["sum"], ct - 1)
                        dve.tensor_tensor(T[:, 0, :], T[:, 0, :], conv_acc[:, ct, :], ALU.add).then_inc(s_ln["sum"], 1)
                out_low(1)

            acc4 = [conv_acc[:, ct, :] for ct in range(CT)]
            dve.wait_ge(s_ln["mean"], 1)
            for ct in range(CT):
                dve.tensor_tensor(acc4[ct], acc4[ct], ps[:, 4, :], ALU.subtract).then_inc(s_ln["cent"], 1)
            for ct in range(CT):
                dve.wait_ge(s_ln["sq"], ct + 1)
                if ct == 0:
                    dve.tensor_copy(T[:, 1, :], sq[:, 0, :]).then_inc(s_ln["acc"], 1)
                else:
                    dve.wait_ge(s_ln["acc"], ct)
                    dve.tensor_tensor(T[:, 1, :], T[:, 1, :], sq[:, ct % 2, :], ALU.add).then_inc(s_ln["acc"], 1)
            merge_gate(3, 3)
            dve.wait_ge(s_ln["sd"], 1)
            dve.reciprocal(rms_c[:, 1, :], rms_c[:, 0, :]).then_inc(s_ln["inv"], 1)
            dve.wait_ge(s_ln["inv"], 1)
            dve.tensor_tensor(r_diag[:], ident[:].unsqueeze(1).to_broadcast([P, QB, P]),
                              rms_c[:, 1, :].unsqueeze(2).to_broadcast([P, QB, P]), ALU.mult).then_inc(s_ln["diag"], 1)
            dve.wait_ge(s_ln["r"], 1)
            dve.wait_ge(s_ln["cent"], 4)
            for ct in range(CT):
                if ct >= 2:
                    dve.wait_ge(s_ln["act"], ct - 1)
                dve.tensor_tensor(T2[:, ct % 2, :], acc4[ct], R[:, 0, :], ALU.mult).then_inc(s_ln["n"], 1)
                if ct >= 1:
                    dve.wait_ge(s_ln["hi"], ct)
                    low(xg_lo[:, ct - 1, :], acc4[ct - 1], xg_hi[:, ct - 1, :], s_ln["lo"])
            dve.wait_ge(s_ln["hi"], CT)
            low(xg_lo[:, CT - 1, :], acc4[CT - 1], xg_hi[:, CT - 1, :], s_ln["lo"])

            def mix(m, j, u, slot, sigmoids=2):
                dve.wait_ge(unit_done, u + 1)
                dve.wait_ge(s_mrg["sig"], CREDIT + sigmoids)
                dve.tensor_tensor(T[:, j:j + 1, :], ps[:, slot:slot + 1, :], merge[:, ds(m, 1), :], ALU.mult).then_inc(s_mix["a"], 1)
                dve.scalar_tensor_tensor(T2[:, j:j + 1, :], ps[:, slot + 2:slot + 3, :], vcol("b_conv_out", m), merge[:, ds(m + DC, 1), :],
                                         ALU.add, ALU.mult).then_inc(bank_free, 1)
                dve.wait_ge(s_mix["a"], m + 1)
                dve.wait_ge(bank_free, u + (1 + CREDIT))
                dve.tensor_tensor(T[:, j:j + 1, :], T[:, j:j + 1, :], T2[:, j:j + 1, :], ALU.add).then_inc(s_mix["y"], 1)
                dve.wait_ge(s_mix["hi"], m + 1)
                low(y_lo[:, ds(m, 1), :], T[:, j:j + 1, :], y_hi[:, ds(m, 1), :], s_mix["lo"])
                dve.wait_ge(s_mix["lo"], m + 1)

            units(U["mix"], 4, mix)
            units(U["mix"] + 4, 4, lambda m, j, u, slot: mix(m + 4, j, u, slot, 4))

            def add_to(dst, m, u, slot):
                dve.wait_ge(unit_done, u + 1)
                dve.wait_ge(bank_free, u + CREDIT)
                dve.tensor_tensor(dst[:, ds(m, 1), :], dst[:, ds(m, 1), :], ps[:, slot:slot + 1, :], ALU.add).then_inc(bank_free, 1)

            def into_norm(dst, n, prep=None, gain=None):
                def body(m, j, u, slot):
                    add_to(dst, m, u, slot)
                    add_square(n, m, j)
                    if prep is not None:
                        prep_low(prep, m, vcol(gain, m))
                return body

            def skip_embedding(n):
                dve.memset(token[:, 10 + n:11 + n], 0.0).then_inc(bank_free, 2)

            def p_low(n):
                dve.wait_ge(s_ple["phi"], n + 1)
                low(p_lo[:], p_raw[:], p_hi[:], s_ple["plo"])

            norm_start(2)
            units(U["w_out"], DC, into_norm(X, 2, 1, "g_ffn"))
            norm_inverse(2)
            dve.wait_ge(r_done, 2)

            for kind, p in ffn_order(len(FF1_PARTS)):
                u0 = U[f"ffn_{kind}{p}"]
                base = sum(FF1_PARTS[:p])
                if kind == "up":
                    with dve.Fori(0, FF1_PARTS[p]) as m:
                        for j in range(2):
                            uu = m * 2 + (u0 + j)
                            scaled(uu, (u0 + j) % 2, T[:, j:j + 1, :])
                            tile = m + (base + 22 * j)
                            done = m * 2 + (2 * base + j)
                            y, t = u4[:, j:j + 1, :], T[:, j:j + 1, :]
                            dve.wait_ge(s_ffn["t2"], done + 1)
                            dve.wait_ge(bank_free, uu + (1 + CREDIT))
                            dve.scalar_tensor_tensor(y[:, :, 1:S], t[:, :, 0:S - 1], vcol("ffn_w", tile + 44), y[:, :, 1:S],
                                                     ALU.mult, ALU.add).then_inc(s_ffn["tap"], 1)
                            dve.wait_ge(s_ffn["tap"], done + 1)
                            dve.scalar_tensor_tensor(y[:, :, 2:S], t[:, :, 0:S - 2], vcol("ffn_w", tile), y[:, :, 2:S],
                                                     ALU.mult, ALU.add).then_inc(s_ffn["conv"], 1)
                        dve.wait_ge(s_ffn["gelu"], m + (base + 1))
                        dve.wait_ge(s_ffn["conv"], m * 2 + (2 * base + 2))
                        dve.tensor_tensor(u4[:, 3:4, :], u4[:, 2:3, :], u4[:, 1:2, :], ALU.mult).then_inc(s_ffn["h"], 1)
                        dve.wait_ge(s_ffn["hhi"], m + (base + 1))
                        low(h_lo[:, p % 2, ds(m, 1), :], u4[:, 3:4, :], h_hi[:, p % 2, ds(m, 1), :], s_ffn["hlo"])
                        dve.wait_ge(s_ffn["hlo"], m + (base + 1))
                elif p < len(FF1_PARTS) - 1:
                    units(u0, DC, lambda m, j, u, slot: add_to(X, m, u, slot))
                else:
                    p_low(0)
                    norm_start(3)
                    units(u0, DC, into_norm(X, 3, 2, "g_ple"))

            def ple_gate(n, norm_n, dst):
                dve.wait_ge(s_ple["e"], DC * (n + 1))
                norm_inverse(norm_n)
                norm_start(norm_n + 1)
                dve.wait_ge(r_done, norm_n)

                def body(m, j, u, slot):
                    scaled(u, slot, T[:, j:j + 1, :])
                    dve.wait_ge(s_ple["sig"], m + (DC * n + 1))
                    if dst is X:
                        dve.tensor_tensor(T[:, j:j + 1, :], E[:, ds(m, 1), :], T2[:, j:j + 1, :], ALU.mult).then_inc(s_ple["g"], 1)
                        dve.wait_ge(s_ple["g"], m + 1)
                        dve.tensor_tensor(X[:, ds(m, 1), :], X[:, ds(m, 1), :], T[:, j:j + 1, :], ALU.add).then_inc(s_ple["x"], 1)
                    else:
                        dve.tensor_tensor(M[:, ds(m, 1), :], E[:, ds(m, 1), :], T2[:, j:j + 1, :], ALU.mult).then_inc(s_ple["x"], 1)
                    add_square(norm_n + 1, m, j)

                units(U[f"ple{n}"] + 2, DC, body)

            skip_embedding(0)
            ple_gate(0, 3, X)
            norm_inverse(4)
            norm_start(5)
            dve.wait_ge(r_done, 4)

            def final(m, j):
                dve.scalar_tensor_tensor(X[:, ds(m, 1), :], X[:, ds(m, 1), :], vcol("g_final", m), R[:],
                                         ALU.mult, ALU.mult).then_inc(final_x, 1)

            final(0, 0)
            spread_steps(lambda m, j: None, final, 3, lambda m: norm2_col(0, 0, m))
            norm_inverse(5)
            dve.wait_ge(r_done, 5)

            uu = U["forget"]
            dve.wait_ge(unit_done, uu + 1)
            f0, f1, f2, f3 = (logf[:, n, :] for n in range(4))
            dve.tensor_tensor(f0, ps[:, uu % 2, :], R[:, 0, :], ALU.mult).then_inc(bank_free, 1)
            dve.memset(f3, 1.0).then_inc(s_fg["dve"], 1)
            dve.wait_ge(bank_free, uu + 1 + CREDIT)
            dve.tensor_scalar(f1, f0, vec[:, VEC["b_forget"]:VEC["b_forget"] + 1], 0.0, ALU.add, ALU.min).then_inc(s_fg["dve"], 1)
            dve.wait_ge(s_fg["act"], 3)
            dve.wait_ge(s_fg["dve"], 2)
            dve.tensor_tensor(f0, f2, f1, ALU.subtract).then_inc(s_fg["dve"], 1)
            dve.wait_ge(s_fg["dve"], 3)
            dve.tensor_tensor_scan(c_rows[:], f3, f0, 0.0, ALU.mult, ALU.add).then_inc(s_fg["dve"], 1)
            dve.wait_ge(s_fg["act"], 4)
            dve.wait_ge(s_fg["dve"], 4)
            low(c_rows[32:64, :], c_rows[32:64, :], c_hi[32:64, :], s_fg["dve"])
            dve.wait_ge(s_fg["dve"], 5)

            u0 = U["fox"]

            def fox_qk(which, p, par, u):
                slot = (u0 + 3 * par + which) % 2
                scaled(u, slot, T[:, which:which + 1, :])
                dve.wait_ge(A2["qkhi"], p * 2 + (which + 1))
                if which == 0:
                    low_q(A2, fq_lo[:, par, :], T[:, 0, :], fq_hi[:, par, :], A2["qklo"])
                else:
                    low(fk_lo[:, par, :], T[:, 1, :], fk_hi[:, par, :], A2["qklo"])

            def fox_v(p, par, u):
                slot = (u0 + 3 * par + 2) % 2
                dve.wait_ge(unit_done, u + 1)
                dve.tensor_tensor(fv[:], ps[:, slot:slot + 1, :], R[:], ALU.mult).then_inc(A2["vs"], 1)

            def fox_v_low(p, par):
                slot = (u0 + 3 * par + 2) % 2
                dve.wait_ge(A2["vhi"], p + 1)
                low(fv_lo[:, par], ps[:, slot, :].rearrange("p (a b) -> p a b", b=P), fv_hi[:, par], bank_free)

            def head_rows(h, hd):
                dve.tensor_scalar(c_head[:, hd:hd + 1, :], c_rows[:].unsqueeze(1), head_sel[:, ds(h, 1)], None,
                                  ALU.mult).then_inc(A2["crow"], 1)

            head_rows(0, 0); head_rows(1, 1)
            fox_qk(0, 0, 0, u0)
            fox_qk(1, 0, 0, u0 + 1)
            fox_v(0, 0, u0 + 2)
            fox_v_low(0, 0)

            def fox_pair(p, par, more):
                nxt, npar = p + 1, 1 - par
                e0, n0 = p * 8, p * 2

                def mx(hd, qi):
                    peak(A2, e0 + (4 * hd + qi), hd, fstat, qi, 2 + qi % 2)

                def nrm(hd, qi):
                    normalise(A2, e0 + (4 * hd + qi), n0 + hd, hd, fstat, fprob[:, hd, :], qi)

                def lo(hd, kb):
                    split_turned(A2, e0 + (4 * hd + kb), kb % 2, (fpt_hi, fpt_lo), kb)

                def out_low(hd):
                    rows = slice(hd * HD, (hd + 1) * HD)
                    dve.wait_ge(A2["ohi"], n0 + (hd + 1))
                    low(fo_lo[rows, ds(p, 1), :], ps[rows, 6 + hd:7 + hd, :], fo_hi[rows, ds(p, 1), :], A2["olo"])

                mx(0, 0); mx(0, 1); nrm(0, 0); nrm(0, 1)
                if more:
                    fox_qk(0, nxt, npar, p * 3 + (u0 + 3))
                mx(0, 2); mx(0, 3); nrm(0, 2); nrm(0, 3); mx(1, 0); mx(1, 1)
                if more:
                    head_rows(n0 + 2, 0)
                    fox_qk(1, nxt, npar, p * 3 + (u0 + 4))
                lo(0, 0); nrm(1, 0); lo(0, 1); nrm(1, 1); mx(1, 2); lo(0, 2); nrm(1, 2); mx(1, 3); lo(0, 3); nrm(1, 3)
                out_low(0)
                if more:
                    head_rows(n0 + 3, 1)
                lo(1, 0); lo(1, 1)
                if more:
                    fox_v(nxt, npar, p * 3 + (u0 + 5))
                lo(1, 2); lo(1, 3); out_low(1)
                if more:
                    fox_v_low(nxt, npar)

            with dve.Fori(0, 3) as i:
                for par in range(2):
                    fox_pair(i * 2 + par, par, True)
            fox_pair(6, 0, True)
            fox_pair(7, 1, False)

            def branch_out(u0, n):
                norm_start(n)

                def body(m, j, u, slot):
                    dve.wait_ge(unit_done, u + 1)
                    dve.tensor_copy(M[:, ds(m, 1), :], ps[:, slot:slot + 1, :]).then_inc(bank_free, 1)
                    add_square(n, m, j)
                units(u0, DC, body)

            def post(k, n, layer, which, prep=None, embed=False):
                norm_inverse(n)
                if prep is not None:
                    norm_start(n + 1)
                dve.wait_ge(r_done, n)

                def branch(m, j):
                    dve.scalar_tensor_tensor(T[:, j:j + 1, :], M[:, ds(m, 1), :], norm2_col(layer, which, m), R[:],
                                             ALU.mult, ALU.mult).then_inc(post_t, 1)

                def add(m, j):
                    dve.wait_ge(post_t, m + (DC * k + 1))
                    dve.tensor_tensor(X[:, ds(m, 1), :], X[:, ds(m, 1), :], T[:, j:j + 1, :], ALU.add).then_inc(post_x, 1)

                branch(0, 0)
                if prep is None:
                    branch(1, 1)
                    with dve.Fori(0, DC // 2 - 1) as i:
                        for j in range(2):
                            add(i * 2 + j, j)
                            dve.wait_ge(post_x, i * 2 + (DC * k + j + 1))
                            branch(i * 2 + (j + 2), j)
                    add(DC - 2, 0)
                    add(DC - 1, 1)
                else:
                    spread_steps(add, branch, prep[0], lambda m: norm2_col(prep[1], prep[2], m))
                if prep is not None and not embed:
                    norm_inverse(n + 1)
                    dve.wait_ge(r_done, n + 1)

            def mlp(k):
                for kind, p in ffn_order(len(FF2_PARTS)):
                    u0 = U[f"mlp{k + 1}_{kind}{p}"]
                    if kind == "up":
                        def body(m, j, u, slot, base=32 * k + 8 * p, p=p):
                            t, s = T[:, j:j + 1, :], T2[:, j:j + 1, :]
                            scaled(u, slot, t)
                            dve.wait_ge(bank_free, u + (1 + CREDIT))
                            dve.scalar_tensor_tensor(s, t, 0.0, t, ALU.max, ALU.mult).then_inc(s_mlp["s"], 1)
                            dve.wait_ge(s_mlp["hi"], m + (base + 1))
                            low(h_lo[:, p % 2, ds(m, 1), :], s, h_hi[:, p % 2, ds(m, 1), :], s_mlp["lo"])
                            dve.wait_ge(s_mlp["lo"], m + (base + 1))
                        units(u0, DC, body)
                    elif p == 0:
                        def body(m, j, u, slot):
                            dve.wait_ge(unit_done, u + 1)
                            dve.tensor_copy(M[:, ds(m, 1), :], ps[:, slot:slot + 1, :]).then_inc(bank_free, 1)
                        units(u0, DC, body)
                    elif p < len(FF2_PARTS) - 1:
                        units(u0, DC, lambda m, j, u, slot: add_to(M, m, u, slot))
                    else:
                        norm_start(8 + 6 * k)
                        units(u0, DC, into_norm(M, 8 + 6 * k))

            branch_out(U["fox_out"], 6)
            post(0, 6, 0, 1, (4, 0, 2))
            mlp(0)
            p_low(1)
            skip_embedding(1)
            post(1, 8, 0, 3, (5, 0, 4), embed=True)
            ple_gate(1, 9, M)
            post(2, 10, 0, 5, (6, 1, 0))
            u0 = U["conv3"]
            with dve.Fori(0, DC // 2) as i:
                for jm in range(2):
                    m = i * 2 + jm
                    for j in range(3):
                        n = 3 * jm + j
                        scaled(i * 6 + (u0 + n), (u0 + n) % 2, c3t[:, j:j + 1, :])
                    dve.wait_ge(bank_free, i * 6 + (u0 + 3 * jm + 3 + CREDIT))
                    z, y = c3t[:, 3:4, :], c3t[:, 4:5, :]
                    dve.tensor_tensor(z, c3t[:, 1:2, :], c3t[:, 2:3, :], ALU.mult).then_inc(s_c3["zz"], 1)
                    dve.wait_ge(s_c3["z2"], m + 1)
                    dve.scalar_tensor_tensor(y[:, :, 1:S], z[:, :, 0:S - 1], vcol("conv3_w", m + DC), y[:, :, 1:S],
                                             ALU.mult, ALU.add).then_inc(s_c3["tap"], 1)
                    dve.wait_ge(s_c3["tap"], m * 2 + 1)
                    dve.scalar_tensor_tensor(y[:, :, 2:S], z[:, :, 0:S - 2], vcol("conv3_w", m), y[:, :, 2:S],
                                             ALU.mult, ALU.add).then_inc(s_c3["tap"], 1)
                    dve.wait_ge(s_c3["tap"], m * 2 + 2)
                    dve.tensor_tensor(c3t[:, 1:2, :], c3t[:, 0:1, :], y, ALU.mult).then_inc(s_c3["y"], 1)
                    dve.wait_ge(s_c3["hi"], m + 1)
                    low(cy_lo[:, ds(m, 1), :], c3t[:, 1:2, :], cy_hi[:, ds(m, 1), :], s_c3["lo"])
                    dve.wait_ge(s_c3["lo"], m + 1)
            branch_out(U["conv3_out"], 12)
            post(3, 12, 1, 1, (7, 1, 2))
            mlp(1)
            p_low(2)
            skip_embedding(2)
            post(4, 14, 1, 3, (8, 1, 4), embed=True)
            ple_gate(2, 15, M)
            post(5, 16, 1, 5)

        @block.scalar
        def _(act):
            def copy_hi(out, x, done, scale=1.0):
                act.activation(out, x, ACT.Copy, scale=scale).then_inc(done, 1)

            def high(u, slot, loads):
                act.wait_ge(w_loaded[slot], loads)
                act.activation(w_hi[:, slot, :], w_raw[:, slot, :], ACT.Copy).then_inc(w_hi_ready, 1)

            def split(u, slot):
                act.wait_ge(unit_done, u + 1)
                high(u + 2, slot, u * 8 + (16 + 8 * (2 - slot)))

            def splits(u0, n):
                for u in range(u0, u0 + n):
                    split(u, u % 2)

            def units(u0, n, body=None, begun=False, last=False):
                def two(i, more):
                    for j in range(2):
                        if more:
                            split(i * 2 + (u0 + j), (u0 + j) % 2)
                        if body is not None:
                            body(i * 2 + j, j, i * 2 + (u0 + j), (u0 + j) % 2)
                if begun:
                    two(0, False)
                with act.Fori(int(begun), n // 2 - int(last)) as i:
                    two(i, True)
                if last:
                    two(n // 2 - 1, False)

            def taken(u):
                act.wait_ge(bank_free, u + (1 + CREDIT))

            def square(n, src, m, j):
                act.wait_ge(summed, m + (10 * (n - 1) + 1))
                act.activation(sq[:, j:j + 1, :], src[:, ds(m, 1), :], ACT.Square).then_inc(squared, 1)

            def prep_high(m, g):
                act.activation(xg_hi[:, ds(m, 1), :], X[:, ds(m, 1), :], ACT.Copy, scale=g).then_inc(prep_hi, 1)

            def norm_root(n):
                act.wait_ge(ssq_done, n)
                act.activation(rms_c[:, 0, :], ps[:, 7, 0:QB], ACT.Sqrt, bias=eps_col[:]).then_inc(rms_done, 1)

            def norm_copy(n):
                act.wait_ge(bcast_done, n)
                act.activation(R[:, 0, :], ps[:, 7, :], ACT.Copy).then_inc(r_done, 1)

            def norm(n, u0=None):
                if u0 is not None:
                    split(u0, u0 % 2)
                norm_root(n)
                norm_copy(n)
                if u0 is not None:
                    split(u0 + 1, (u0 + 1) % 2)

            act.wait_ge(vec_loaded, 16)
            act.wait_ge(c_dve, 4)
            for m in range(DC):
                act.wait_ge(x_loaded[m // 2], 16)
                prep_high(m, vcol("g_mix", m))
                square(1, X, m, m % 2)
                if m in (1, 7):
                    high(m // 4, m // 4, 16)
            act.wait_ge(c_pool, 11)
            act.activation(ident_r[:], ident[:], ACT.Copy).then_inc(c_act, 1)
            act.activation(causal_r[:], causal[:], ACT.Copy).then_inc(c_act, 1)
            act.activation(cmp_mask_r[:], cmask[:], ACT.Copy).then_inc(c_act, 1)
            act.activation(ones_r[:], ones[:], ACT.Copy).then_inc(c_act, 1)
            norm(1, U["glu"])

            def glu_gate(m, j, u, slot):
                if j == 1:
                    taken(u)
                    act.activation(T2[:, 0:1, :], T[:, 1:2, :], ACT.Sigmoid).then_inc(s_glu["sig"], 1)

            units(U["glu"], 8, glu_gate, begun=True)
            splits(U["cmp_in"], 4)
            for kv in range(2):
                act.wait_ge(s_cmp["blk"], 4 * (kv + 1))
                copy_hi(blk_hi[:, kv], blk[:, kv], s_cmp["hi"])
            def hidden_gelu(kv):
                act.activation(hid[:, kv, :], ps[0:2 * NC1, 2 + kv, 0:2 * P], ACT.Gelu_apprx_tanh).then_inc(s_cmp["gelu"], 1)

            def hidden_high(kv):
                act.wait_ge(s_cmp["turned"], kv + 1)
                copy_hi(hid_hi[:, kv], ps[:, 6 + kv, 0:P].rearrange("p (a b) -> p a b", b=64)[:, :, 0:2 * NC1], s_cmp["ghi"])

            def keys(j):
                splits(U["keys"] + j, 1)
                taken(U["keys"] + j)
                copy_hi(kk_hi[:, j, :], T[:, j, :], s_kv["hi"])

            splits(U["cmp_hidden"], 4)
            hidden_gelu(0)
            splits(U["cmp_hidden"] + 4, 2)
            hidden_high(0)
            splits(U["cmp_hidden"] + 6, 2)
            hidden_gelu(1)
            keys(0)
            hidden_high(1)
            keys(1)
            splits(U["cmp_out"], 1)
            act.wait_ge(s_cmp["out"], 4)
            copy_hi(kc_hi[:], kc_f[:], s_cmp["khi"])
            copy_hi(vc_hi[:], vc_f[:], s_cmp["khi"])
            splits(U["values"], 2)
            splits(U["gates"], 1)
            taken(U["gates"])
            act.activation(sq[:, 0, :], T[:, 0, :], ACT.Sigmoid).then_inc(s_gate["sig"], 1)
            def nsa_q(p):
                u = pair_units(p - 1)[4] if p else U["q0"]
                split(u, u % 2)
                taken(u)
                copy_hi(q_hi[:, p % 2, :], T[:, p % 2, :], A1["qhi"], HD ** -0.5)

            nsa_q(0)
            for j in range(2):
                act.wait_ge(s_kv["turned"], j + 1)
                copy_hi(vv_hi[:, j], ps[:, 6 + j, :].rearrange("p (a b) -> p a b", b=P), s_kv["hi"])

            def exps(A, e, par, st, pr, qi, b):
                act.wait_ge(A["peak"], e + 1)
                act.activation(pr[:, P_OFF[qi]:P_OFF[qi] + (qi + 1) * P], ps[:, b, 0:(qi + 1) * P], ACT.Exp,
                               bias=st[:, 0, par, qi:qi + 1], accum_out=st[:, 1, par, qi:qi + 1]).then_inc(A["exps"], 1)

            def turned_hi(A, e, b, pt, kb):
                act.wait_ge(A["turned"], e + 1)
                copy_hi(pt[:, b, kb * P:S], ps[:, 4 + b, kb * P:S], A["hi"])

            for p in range(4):
                e0 = 18 * p

                def cmp_exps(hd):
                    e = e0 + 9 * hd
                    act.wait_ge(A1["peak"], e + 1)
                    act.activation(prob_c[:, hd], prob_c[:, hd], ACT.Exp).then_inc(A1["exps"], 1)

                def cmp_hi(hd):
                    e = e0 + 9 * hd
                    act.wait_ge(A1["turned"], e + 1)
                    copy_hi(pt_hi[0:NCP, e % 2, :], ps[0:NCP, 4 + e % 2, :], A1["hi"])

                def where(f):
                    return e0 + 9 * (f // 2) + 1 + 4 * (f % 2), 4 * p + f

                def ex(f, qi):
                    e, n = where(f)
                    exps(A1, e + qi, n % 2, stat, prob[:, n % 2, :], qi, 2 + (e + qi) % 2)

                def hi(f, kb):
                    e = where(f)[0] + kb
                    turned_hi(A1, e, e % 2, pt_hi, kb)

                def out_hi(hd):
                    rows = slice(hd * HD, (hd + 1) * HD)
                    act.wait_ge(A1["pv"], e0 + 9 * (hd + 1))
                    copy_hi(o_hi[rows, p, :], ps[rows, 6 + hd, :], A1["ohi"])

                def gate_done(i):
                    u = pair_units(p)[i]
                    split(u, u % 2)

                def two_steps(new, old, n):
                    ex(new, 0); ex(new, 1); hi(old, 0); hi(old, 1); ex(new, 2); hi(old, 2); ex(new, 3); hi(old, 3)
                    if n < 4:
                        gate_done(n)
                    elif p < 3:
                        nsa_q(p + 1)

                cmp_exps(0); ex(0, 0); cmp_hi(0); ex(0, 1); ex(0, 2); ex(0, 3); gate_done(0)
                two_steps(1, 0, 1)
                cmp_exps(1)
                two_steps(2, 1, 4)
                out_hi(0); cmp_hi(1)
                two_steps(3, 2, 2)
                for kb in range(QB):
                    hi(3, kb)
                if p < 3:
                    gate_done(3)
                out_hi(1)

            def merge_sigmoid(m):
                tiles = merge[:, m:m + 4, :]
                act.activation(tiles, tiles, ACT.Sigmoid).then_inc(s_mrg["sig"], 1)

            for ct in range(CT):
                act.wait_ge(s_ln["cent"], ct + 1)
                if ct >= 2:
                    act.wait_ge(s_ln["acc"], ct - 1)
                act.activation(sq[:, ct % 2, :], conv_acc[:, ct, :], ACT.Square).then_inc(s_ln["sq"], 1)
            taken(pair_units(3)[2])
            merge_sigmoid(0)
            gate_done(3)
            act.wait_ge(s_ln["var"], 1)
            act.activation(rms_c[:, 0, :], ps[:, 5, 0:QB], ACT.Sqrt, bias=eps_col[:]).then_inc(s_ln["sd"], 1)
            act.wait_ge(s_ln["bc"], 1)
            act.activation(R[:, 0, :], ps[:, 5, :], ACT.Copy).then_inc(s_ln["r"], 1)
            for ct in range(CT):
                act.wait_ge(s_ln["n"], ct + 1)
                act.activation(conv_acc[:, ct, :], T2[:, ct % 2, :], ACT.Silu, bias=vcol("ln_b", ct), scale=vcol("ln_g", ct)).then_inc(s_ln["act"], 1)
                act.wait_ge(s_ln["act"], ct + 1)
                copy_hi(xg_hi[:, ct, :], conv_acc[:, ct, :], s_ln["hi"])

            merge_sigmoid(DC)
            taken(pair_units(3)[3])

            def mix(m, j, u, slot):
                act.wait_ge(s_mix["y"], m + 1)
                copy_hi(y_hi[:, ds(m, 1), :], T[:, j:j + 1, :], s_mix["hi"])

            units(U["mix"], 4, mix)
            merge_sigmoid(4)
            merge_sigmoid(DC + 4)
            units(U["mix"] + 4, 4, lambda m, j, u, slot: mix(m + 4, j, u, slot))

            def into_norm(src, n, gain=None):
                def body(m, j, u, slot):
                    taken(u)
                    square(n, src, m, j)
                    if gain is not None:
                        prep_high(m, vcol(gain, m))
                return body

            units(U["w_out"], DC, into_norm(X, 2, "g_ffn"))
            def p_high(n):
                act.wait_ge(p_loaded, 16 * (n + 1))
                copy_hi(p_hi[:], p_raw[:], s_ple["phi"])

            norm(2, U["ffn_up0"])
            act.dma_start(p_raw[:], p_in[0]).then_inc(p_loaded, 16)

            for kind, p in ffn_order(len(FF1_PARTS)):
                u0 = U[f"ffn_{kind}{p}"]
                base = sum(FF1_PARTS[:p])
                if kind == "up":
                    def hidden(m, more, u0=u0, base=base, p=p):
                        for j in range(2):
                            if more:
                                split(m * 2 + (u0 + j), (u0 + j) % 2)
                            taken(m * 2 + (u0 + j))
                            tile = m + (base + 22 * j)
                            act.activation(u4[:, j:j + 1, :], T[:, j:j + 1, :], ACT.Identity, bias=vcol("ffn_b", tile),
                                           scale=vcol("ffn_w", tile + 88)).then_inc(s_ffn["t2"], 1)
                        act.wait_ge(s_ffn["conv"], m * 2 + (2 * base + 1))
                        act.activation(u4[:, 2:3, :], u4[:, 0:1, :], ACT.Gelu_apprx_tanh).then_inc(s_ffn["gelu"], 1)
                        act.wait_ge(s_ffn["h"], m + (base + 1))
                        copy_hi(h_hi[:, p % 2, ds(m, 1), :], u4[:, 3:4, :], s_ffn["hhi"])

                    if p == 0:
                        hidden(0, False)
                    with act.Fori(int(p == 0), FF1_PARTS[p]) as m:
                        hidden(m, True)
                else:
                    if p == len(FF1_PARTS) - 1:
                        p_high(0)
                    units(u0, DC, into_norm(X, 3, "g_ple") if p == len(FF1_PARTS) - 1 else None)

            def p_next(n):
                act.wait_ge(s_ple["plo"], n)
                act.dma_start(p_raw[:], p_in[n]).then_inc(p_loaded, 16)

            def embed_tile(n, t):
                if t % 4 < 3:
                    act.wait_ge(s_ple["epe"], 6 * n + 3 * (t // 4) + t % 4 + 1)
                else:
                    act.wait_ge(unit_done, U[f"ple{n}"] + t // 4 + 1)
                act.activation(E[:, t, :], ps[:, 2 + t % 4, :], ACT.Copy).then_inc(s_ple["e"], 1)
                if t % 4 == 3:
                    splits(U[f"ple{n}"] + t // 4, 1)

            def ple_gate(n, norm_n, src):
                norm(norm_n, U[f"ple{n}"] + 2)

                def body(m, j, u, slot):
                    taken(u)
                    act.activation(T2[:, j:j + 1, :], T[:, j:j + 1, :], ACT.Sigmoid).then_inc(s_ple["sig"], 1)
                    act.wait_ge(s_ple["x"], m + (DC * n + 1))
                    square(norm_n + 1, src, m, j)

                units(U[f"ple{n}"] + 2, DC, body, begun=True, last=n == 2)

            for t in range(DC):
                embed_tile(0, t)
            ple_gate(0, 3, X)
            norm(4)
            with act.Fori(0, DC // 2) as i:
                for j in range(2):
                    m = i * 2 + j
                    act.wait_ge(final_x, m + 1)
                    square(5, X, m, j)
                    prep_high(m, norm2_col(0, 0, m))
            norm(5)
            splits(U["forget"], 1)

            taken(U["forget"])
            f0, f1, f2, f3 = (logf[:, n, :] for n in range(4))
            act.activation(f2, f0, ACT.Abs, bias=vec[:, VEC["b_forget"]:VEC["b_forget"] + 1]).then_inc(s_fg["act"], 1)
            act.wait_ge(s_fg["act"], 1)
            act.activation(f2, f2, ACT.Exp, scale=-1.0).then_inc(s_fg["act"], 1)
            act.wait_ge(s_fg["act"], 2)
            act.activation(f2, f2, ACT.Ln, bias=ones[:, 0:1]).then_inc(s_fg["act"], 1)
            act.wait_ge(s_fg["dve"], 4)
            act.activation(c_hi[:], c_rows[:], ACT.Copy).then_inc(s_fg["act"], 1)

            u0 = U["fox"]

            def fox_qk(which, p, par, u):
                split(u, (u0 + 3 * par + which) % 2)
                taken(u)
                if which == 0:
                    copy_hi(fq_hi[:, par, :], T[:, 0, :], A2["qkhi"], HD ** -0.5)
                else:
                    copy_hi(fk_hi[:, par, :], T[:, 1, :], A2["qkhi"])

            def fox_v_high(p, par):
                slot = (u0 + 3 * par + 2) % 2
                act.wait_ge(A2["vturned"], p + 1)
                copy_hi(fv_hi[:, par], ps[:, slot, :].rearrange("p (a b) -> p a b", b=P), A2["vhi"])

            fox_qk(0, 0, 0, u0)
            fox_qk(1, 0, 0, u0 + 1)
            splits(u0 + 2, 1)
            fox_v_high(0, 0)

            def fox_pair(p, par, more):
                nxt, npar = p + 1, 1 - par
                e0 = p * 8

                def ex(hd, qi):
                    exps(A2, e0 + (4 * hd + qi), hd, fstat, fprob[:, hd, :], qi, 2 + qi % 2)

                def hi(hd, kb):
                    turned_hi(A2, e0 + (4 * hd + kb), kb % 2, fpt_hi, kb)

                def out_hi(hd):
                    rows = slice(hd * HD, (hd + 1) * HD)
                    act.wait_ge(A2["pv"], e0 + 4 * (hd + 1))
                    copy_hi(fo_hi[rows, ds(p, 1), :], ps[rows, 6 + hd:7 + hd, :], A2["ohi"])

                ex(0, 0); ex(0, 1)
                if more:
                    fox_qk(0, nxt, npar, p * 3 + (u0 + 3))
                ex(0, 2); ex(0, 3); ex(1, 0); ex(1, 1)
                if more:
                    fox_qk(1, nxt, npar, p * 3 + (u0 + 4))
                hi(0, 0); hi(0, 1); ex(1, 2); hi(0, 2); ex(1, 3); hi(0, 3); out_hi(0)
                hi(1, 0); hi(1, 1); hi(1, 2); hi(1, 3); out_hi(1)
                if more:
                    split(p * 3 + (u0 + 5), (u0 + 3 * npar + 2) % 2)
                    fox_v_high(nxt, npar)

            with act.Fori(0, 3) as i:
                for par in range(2):
                    fox_pair(i * 2 + par, par, True)
            fox_pair(6, 0, True)
            fox_pair(7, 1, False)

            def post(k, n, prep=None, embed=None, u0=None):
                norm(n)
                if embed is not None:
                    for m in range(DC):
                        act.wait_ge(post_x, DC * k + m + 1)
                        prep_high(m, norm2_col(prep[1], prep[2], m))
                        square(n + 1, X, m, m % 2)
                        embed_tile(embed, m)
                elif prep is not None:
                    with act.Fori(0, DC // 2) as i:
                        for j in range(2):
                            m = i * 2 + j
                            act.wait_ge(post_x, m + (DC * k + 1))
                            square(n + 1, X, m, j)
                            prep_high(m, norm2_col(prep[1], prep[2], m))
                    norm(n + 1, u0)

            def mlp(k):
                for kind, p in ffn_order(len(FF2_PARTS)):
                    u0 = U[f"mlp{k + 1}_{kind}{p}"]
                    if kind == "up":
                        def body(m, j, u, slot, base=32 * k + 8 * p, p=p):
                            act.wait_ge(s_mlp["s"], m + (base + 1))
                            copy_hi(h_hi[:, p % 2, ds(m, 1), :], T2[:, j:j + 1, :], s_mlp["hi"])
                        units(u0, DC, body, begun=p == 0)
                    else:
                        units(u0, DC, into_norm(M, 8 + 6 * k) if p == len(FF2_PARTS) - 1 else None)

            units(U["fox_out"], DC, into_norm(M, 6))
            p_next(1)
            post(0, 6, (4, 0, 2), u0=U["mlp1_up0"])
            mlp(0)
            p_high(1)
            post(1, 8, (5, 0, 4), embed=1)
            p_next(2)
            ple_gate(1, 9, M)
            post(2, 10, (6, 1, 0), u0=U["conv3"])

            def conv3_pair(i, begun=0):
                u0 = U["conv3"]
                for jm in range(2):
                    m = i * 2 + jm
                    for n in range(3 * jm, 3 * jm + 3):
                        if n >= begun:
                            split(i * 6 + (u0 + n), (u0 + n) % 2)
                    act.wait_ge(s_c3["zz"], m + 1)
                    act.activation(c3t[:, 4:5, :], c3t[:, 3:4, :], ACT.Copy, scale=vcol("conv3_w", m + 2 * DC)).then_inc(s_c3["z2"], 1)
                    act.wait_ge(s_c3["y"], m + 1)
                    copy_hi(cy_hi[:, ds(m, 1), :], c3t[:, 1:2, :], s_c3["hi"])

            conv3_pair(0, begun=2)
            with act.Fori(1, DC // 2) as i:
                conv3_pair(i)
            units(U["conv3_out"], DC, into_norm(M, 12))
            post(3, 12, (7, 1, 2), u0=U["mlp2_up0"])
            mlp(1)
            p_high(2)
            post(4, 14, (8, 1, 4), embed=2)
            ple_gate(2, 15, M)
            post(5, 16)


def _pack(w, rows=None, cols=None):
    w = w if cols is None else w[:, cols]
    k, n = w.shape
    return w.reshape(k // P, P, n // P, P).transpose(2, 1, 0, 3).reshape(n // P, P, k)


def _full(t):
    return np.concatenate([t, np.zeros((*t.shape[:-1], UW - t.shape[-1]), t.dtype)], -1) if t.shape[-1] < UW else t


def _weights(a):
    U = layout_units()
    f = np.float32
    w_in = a["w_in"][0]
    kv0 = 4 * P
    gates0, conv0 = kv0 + 768, kv0 + 768 + 24
    merge0 = conv0 + 1024
    out = []

    def add(stage, t):
        assert len(out) == U[stage], stage
        out.extend(_full(t))

    def inter(*ts):
        return np.stack(ts, 1).reshape(-1, *ts[0].shape[1:])

    add("glu", inter(_pack(w_in[:, conv0:conv0 + 512]), _pack(w_in[:, conv0 + 512:conv0 + 1024])))
    dup = [w_in[:, kv0 + i * P + g * HD:kv0 + i * P + (g + 1) * HD] for i in range(2) for g in range(2)]
    add("cmp_in", np.concatenate([_pack(np.concatenate([d, d], 1)) for d in dup]))
    hidden = [a[n][0].reshape(4, 4, P, 256).transpose(0, 2, 1, 3).reshape(4, P, UW) for n in ("w_cmp_k1", "w_cmp_v1")]
    add("cmp_hidden", np.concatenate(hidden))
    kv = lambda i: w_in[:, kv0 + i * P:kv0 + (i + 1) * P]
    add("keys", np.concatenate([_pack(kv(2)), _pack(kv(4))]))
    k2, v2 = a["w_cmp_k2"][0], a["w_cmp_v2"][0]
    add("cmp_out", np.concatenate([_pack(np.concatenate([k2, k2], 1)), v2.reshape(2, P, HD).transpose(1, 0, 2).reshape(1, P, P)], -1))
    add("values", np.concatenate([_pack(kv(3)), _pack(kv(5))]))
    gate = np.zeros((D, P), f)
    gate[:, :24] = w_in[:, gates0:gates0 + 24]
    add("gates", _pack(gate))
    heads = np.concatenate([np.arange(g * 256 + p * HD, g * 256 + (p + 1) * HD) for p in range(4) for g in range(2)])
    q, merge = _pack(w_in[:, heads]), _pack(w_in[:, merge0:])
    add("q0", q[:1])
    add("pairs", np.concatenate([np.stack([merge[4 * p], merge[4 * p + 1], *q[p + 1:p + 2], merge[4 * p + 2], merge[4 * p + 3]])
                                 for p in range(4)]))
    add("mix", np.concatenate([_pack(a["w_o_nsa"][0][heads]), _pack(a["w_conv_out"][0])], -1))
    add("w_out", _pack(a["w_out"][0]))
    up, down = a["w_up"][0], a["w_down"][0]
    for kind, p in ffn_order(len(FF1_PARTS)):
        r = slice(P * sum(FF1_PARTS[:p]), P * sum(FF1_PARTS[:p + 1]))
        add(f"ffn_{kind}{p}", inter(_pack(up[:, :22 * P][:, r]), _pack(up[:, 22 * P:][:, r])) if kind == "up" else _pack(down[r]))

    def embed(w):
        return _pack(w).reshape(2, 4, P, 256).transpose(0, 2, 1, 3).reshape(2, P, UW)

    add("ple0", np.concatenate([embed(a["w_ple"][0]), _pack(a["w_ple_gate"][0])]))
    w = a["w_attn_in_2"][0]
    gate = np.zeros((D, P), f)
    gate[:, 0:16] = gate[:, 32:48] = w[:, 3 * D:]
    add("forget", _pack(gate))
    add("fox", inter(_pack(w[:, :D]), _pack(w[:, D:2 * D]), _pack(w[:, 2 * D:3 * D])))
    add("fox_out", _pack(a["w_attn_out_2"][0]))
    for n in (1, 2):
        if n == 2:
            w = a["w_conv_in_2"][0]
            add("conv3", inter(_pack(w[:, :D]), _pack(w[:, D:2 * D]), _pack(w[:, 2 * D:])))
            add("conv3_out", _pack(a["w_conv_out_2"][0]))
        for kind, p in ffn_order(len(FF2_PARTS)):
            r = slice(p * D, (p + 1) * D)
            add(f"mlp{n}_{kind}{p}", _pack(a["w_mlp_up_2"][n - 1][:, r]) if kind == "up" else _pack(a["w_mlp_down_2"][n - 1][r]))
        add(f"ple{n}", np.concatenate([embed(a["w_ple_proj_2"][n - 1]), _pack(a["w_ple_gate_2"][n - 1])]))
    assert len(out) == U["end"]
    return np.ascontiguousarray(np.stack(out))


def _vectors(a):
    v = np.zeros((P, NVEC), np.float32)

    def put(name, cols):
        v[:cols.shape[0], VEC[name]:VEC[name] + cols.shape[1]] = cols

    def tiles(x):
        return x.reshape(-1, P).T

    for name, key in (("g_mix", "g_mix"), ("g_ffn", "g_ffn"), ("g_ple", "g_ple"), ("g_final", "g_final"), ("norm2", "norm_g_2"),
                      ("conv_b", "conv_b"), ("ln_g", "conv_ln_g"), ("ln_b", "conv_ln_b"), ("b_conv_out", "b_conv_out"),
                      ("ffn_w", "ffn_conv_w"), ("ffn_b", "ffn_conv_b"), ("conv3_w", "conv_w_2")):
        put(name, tiles(a[key]))
    put("conv_w", a["conv_w"][0].reshape(CONV_TAPS, CT, P).transpose(2, 1, 0).reshape(P, -1))
    b = np.zeros((P, 1), np.float32)
    b[0:16, 0] = b[32:48, 0] = a["b_forget_2"][0]
    put("b_forget", b)
    put("pos_k", a["cmp_pos_k"][0].reshape(16, P).T)
    put("pos_v", a["cmp_pos_v"][0].reshape(16, P).T)
    return v


def kernel(**inputs):
    import concourse.bacc as bacc
    from concourse.bass_utils import run_bass_kernel_spmd

    a = {k: np.asarray(v) for k, v in inputs.items()}

    def feature_tiles(x):
        return np.ascontiguousarray(x.T.reshape(-1, P, S).transpose(1, 0, 2))

    arrays = {
        "in_x": feature_tiles(a["x"][0]),
        "in_p": np.stack([feature_tiles(t) for t in (a["p"][0, 0], a["p_2"][0, 0], a["p_2"][1, 0])]),
        "in_weights": _weights(a),
        "in_vectors": _vectors(a),
    }
    nc = bacc.Bacc("TRN2", target_bir_lowering=False, num_devices=1)
    args = [nc.dram_tensor(n, v.shape, F32, kind="ExternalInput").ap() for n, v in arrays.items()]
    out = nc.dram_tensor("out_x", (P, DC, S), F32, kind="ExternalOutput").ap()
    build(nc, *args, out)
    r = run_bass_kernel_spmd(nc, [arrays], core_ids=[0])
    got = r.results[0]["out_x"]
    return np.ascontiguousarray(got.transpose(2, 1, 0).reshape(1, S, D))
```
